# Optimizing a Trainium2 kernel written in Bass

```python
import math
import jax, jax.numpy as jnp
from jax import lax
import numpy as np

D_MODEL = 1024
BATCH = 1
SEQ = 256
DEPTH = 2

MIX_WIDTH = D_MODEL
A_WIDTH = MIX_WIDTH // 2
B_WIDTH = MIX_WIDTH - A_WIDTH
C_WIDTH = MIX_WIDTH // 2
D_WIDTH = MIX_WIDTH - C_WIDTH
EVEN_IN_WIDTH = A_WIDTH + 3 * B_WIDTH
ODD_IN_WIDTH = 2 * C_WIDTH + 3 * D_WIDTH
S5_GROUP = 16
S5_GROUPS = A_WIDTH // S5_GROUP
S5_STATE = 64
DT_MIN = 1e-3
DT_MAX = 1e-1
CONV_WIDTH = 3
GMLP_CHUNK = 128
GMLP_HEADS = 8
GMLP_HEAD_DIM = C_WIDTH // GMLP_HEADS
SB_HEADS = 8
SB_HEAD_DIM = D_WIDTH // SB_HEADS
SB_BLOCK = 128
PEER_HEADS = 8
PEER_N_KEYS = 128
PEER_N_EXPERTS = PEER_N_KEYS ** 2
PEER_TOPK = 16
PEER_QUERY_DIM = 256
PEER_HALF = PEER_QUERY_DIM // 2
PEER_TOKEN_BLOCK = 128
RMS_EPS = 1e-6

kernel_name = "hybrid_s5_shortconv_gmlp_stickbreak_peer"

def rmsnorm(x, g):
    xf = x.astype(jnp.float32)
    y = xf * lax.rsqrt(jnp.mean(xf * xf, axis=-1, keepdims=True) + RMS_EPS)
    return (y * g.astype(jnp.float32)).astype(x.dtype)

def _complex_affine_combine(e1, e2):
    a1r, a1i, b1r, b1i = e1
    a2r, a2i, b2r, b2i = e2
    ar = a2r * a1r - a2i * a1i
    ai = a2r * a1i + a2i * a1r
    br = a2r * b1r - a2i * b1i + b2r
    bi = a2r * b1i + a2i * b1r + b2i
    return (ar, ai, br, bi)

def s5_mixer(u, lam_re, lam_im, log_dt, b_re, b_im, c_re, c_im, d_skip, glu_w, glu_b):
    bsz, seqlen, _ = u.shape
    dt = jnp.exp(log_dt.astype(jnp.float32))[:, None]
    lr = lam_re.astype(jnp.float32)
    li = lam_im.astype(jnp.float32)
    mag = jnp.exp(lr * dt)
    ar = mag * jnp.cos(li * dt)
    ai = mag * jnp.sin(li * dt)
    den = lr * lr + li * li
    nr = ar - 1.0
    fr = (nr * lr + ai * li) / den
    fi = (ai * lr - nr * li) / den
    bre = b_re.astype(jnp.float32)
    bim = b_im.astype(jnp.float32)
    bbar_re = fr[..., None] * bre - fi[..., None] * bim
    bbar_im = fr[..., None] * bim + fi[..., None] * bre
    uf = u.astype(jnp.float32).reshape(bsz, seqlen, S5_GROUPS, S5_GROUP)
    bu_re = jnp.einsum('gpc,blgc->blgp', bbar_re, uf)
    bu_im = jnp.einsum('gpc,blgc->blgp', bbar_im, uf)
    a_re = jnp.broadcast_to(ar, bu_re.shape)
    a_im = jnp.broadcast_to(ai, bu_im.shape)
    _, _, h_re, h_im = lax.associative_scan(_complex_affine_combine, (a_re, a_im, bu_re, bu_im), axis=1)
    y = (jnp.einsum('gcp,blgp->blgc', c_re.astype(jnp.float32), h_re)
         - jnp.einsum('gcp,blgp->blgc', c_im.astype(jnp.float32), h_im)
         + d_skip.astype(jnp.float32) * uf)
    y = jax.nn.gelu(y.reshape(bsz, seqlen, A_WIDTH))
    out = y * jax.nn.sigmoid(y @ glu_w.astype(jnp.float32) + glu_b.astype(jnp.float32))
    return out.astype(u.dtype)

def short_conv_mixer(b_gate, c_gate, x_in, conv_w):
    z = c_gate * x_in
    w = conv_w.astype(z.dtype)[:, None, :]
    conv = lax.conv_general_dilated(z, w, window_strides=(1,), padding=[(CONV_WIDTH - 1, 0)],
                                    dimension_numbers=('NWC', 'WIO', 'NWC'),
                                    feature_group_count=B_WIDTH)
    return b_gate * conv

def gmlp_mixer(u, v, vnorm_g, ws, bs):
    bsz, seqlen, _ = v.shape
    u = jax.nn.gelu(u)
    v = rmsnorm(jax.nn.gelu(v), vnorm_g)
    vc = v.reshape(bsz, seqlen // GMLP_CHUNK, GMLP_CHUNK, GMLP_HEADS, GMLP_HEAD_DIM)
    tril = jnp.tril(jnp.ones((GMLP_CHUNK, GMLP_CHUNK), dtype=bool))
    wm = jnp.where(tril, ws, jnp.zeros_like(ws))
    y = jnp.einsum('hts,bnshd->bnthd', wm, vc) + bs.T[None, None, :, :, None]
    return u * y.reshape(bsz, seqlen, C_WIDTH)

def stick_breaking_attention(q, k, v):
    bsz, seqlen, _ = q.shape
    nblk = seqlen // SB_BLOCK
    qf = q.astype(jnp.float32).reshape(bsz, seqlen, SB_HEADS, SB_HEAD_DIM) * (SB_HEAD_DIM ** -0.5)
    qb = qf.reshape(bsz, nblk, SB_BLOCK, SB_HEADS, SB_HEAD_DIM).transpose(1, 0, 3, 2, 4)
    kf = k.astype(jnp.float32).reshape(bsz, seqlen, SB_HEADS, SB_HEAD_DIM)
    vf = v.astype(jnp.float32).reshape(bsz, seqlen, SB_HEADS, SB_HEAD_DIM)
    key_pos = jnp.arange(seqlen)

    def block(args):
        q_blk, bidx = args
        q_pos = bidx * SB_BLOCK + jnp.arange(SB_BLOCK)
        z = jnp.einsum('bhqd,bkhd->bhqk', q_blk, kf)
        mask = key_pos[None, :] < q_pos[:, None]
        log_1mb = jnp.where(mask, jax.nn.log_sigmoid(-z), 0.0)
        rest = lax.cumsum(log_1mb, axis=3, reverse=True) - log_1mb
        w = jnp.where(mask, jnp.exp(jax.nn.log_sigmoid(z) + rest), 0.0)
        return jnp.einsum('bhqk,bkhd->bqhd', w, vf)

    o = lax.map(block, (qb, jnp.arange(nblk)))
    o = o.transpose(1, 0, 2, 3, 4).reshape(bsz, seqlen, D_WIDTH)
    return o.astype(q.dtype)

def peer_ffn(h, wq, k1, k2, u_tab, v_tab):
    bsz, seqlen, dm = h.shape
    hb = h.reshape(-1, PEER_TOKEN_BLOCK, dm)
    k1f = k1.astype(jnp.float32)
    k2f = k2.astype(jnp.float32)

    def block(hx):
        q = (hx @ wq).astype(jnp.float32).reshape(PEER_TOKEN_BLOCK, PEER_HEADS, 2, PEER_HALF)
        s1 = jnp.einsum('thd,hnd->thn', q[:, :, 0], k1f)
        s2 = jnp.einsum('thd,hnd->thn', q[:, :, 1], k2f)
        v1, i1 = lax.top_k(s1, PEER_TOPK)
        v2, i2 = lax.top_k(s2, PEER_TOPK)
        cand_s = (v1[..., :, None] + v2[..., None, :]).reshape(PEER_TOKEN_BLOCK, PEER_HEADS, PEER_TOPK * PEER_TOPK)
        cand_i = (i1[..., :, None] * PEER_N_KEYS + i2[..., None, :]).reshape(PEER_TOKEN_BLOCK, PEER_HEADS, PEER_TOPK * PEER_TOPK)
        top_s, pos = lax.top_k(cand_s, PEER_TOPK)
        idx = jnp.take_along_axis(cand_i, pos, axis=-1)
        g = jax.nn.softmax(top_s, axis=-1)
        u_sel = u_tab[idx]
        act = jax.nn.gelu(jnp.einsum('thkd,td->thk', u_sel, hx).astype(jnp.float32))
        v_sel = v_tab[idx]
        return jnp.einsum('thk,thkd->td', (g * act).astype(v_sel.dtype), v_sel).astype(hx.dtype)

    return lax.map(block, hb).reshape(bsz, seqlen, dm)

def even_mixer(h, w_in, lam_re, lam_im, log_dt, b_re, b_im, c_re, c_im, d_skip, glu_w, glu_b, conv_w, w_out):
    p = h @ w_in
    a_u = p[..., :A_WIDTH]
    b_b = p[..., A_WIDTH:A_WIDTH + B_WIDTH]
    b_c = p[..., A_WIDTH + B_WIDTH:A_WIDTH + 2 * B_WIDTH]
    b_x = p[..., A_WIDTH + 2 * B_WIDTH:]
    ya = s5_mixer(a_u, lam_re, lam_im, log_dt, b_re, b_im, c_re, c_im, d_skip, glu_w, glu_b)
    yb = short_conv_mixer(b_b, b_c, b_x, conv_w)
    return jnp.concatenate([ya, yb], axis=-1) @ w_out

def odd_mixer(h, w_in, vnorm_g, ws, bs, w_out):
    p = h @ w_in
    c_u = p[..., :C_WIDTH]
    c_v = p[..., C_WIDTH:2 * C_WIDTH]
    o = 2 * C_WIDTH
    d_q = p[..., o:o + D_WIDTH]
    d_k = p[..., o + D_WIDTH:o + 2 * D_WIDTH]
    d_v = p[..., o + 2 * D_WIDTH:]
    yc = gmlp_mixer(c_u, c_v, vnorm_g, ws, bs)
    yd = stick_breaking_attention(d_q, d_k, d_v)
    return jnp.concatenate([yc, yd], axis=-1) @ w_out

def setup_inputs(seed: int = 0) -> dict:
    key = jax.random.key(seed)
    ks = iter(jax.random.split(key, 48))

    def nrm(shape, scale):
        return jax.random.normal(next(ks), shape, jnp.float32) * scale

    def gain(n):
        return 1.0 + nrm((n,), 0.02)

    def peer_params():
        return (nrm((D_MODEL, PEER_HEADS * PEER_QUERY_DIM), D_MODEL ** -0.5),
                nrm((PEER_HEADS, PEER_N_KEYS, PEER_HALF), PEER_HALF ** -0.5),
                nrm((PEER_HEADS, PEER_N_KEYS, PEER_HALF), PEER_HALF ** -0.5),
                nrm((PEER_N_EXPERTS, D_MODEL), D_MODEL ** -0.5),
                nrm((PEER_N_EXPERTS, D_MODEL), PEER_HEADS ** -0.5))

    x = nrm((BATCH, SEQ, D_MODEL), 1.0)
    l0_norm_mix_g = gain(D_MODEL)
    l0_w_in = nrm((D_MODEL, EVEN_IN_WIDTH), D_MODEL ** -0.5)
    a_lam_re = -0.5 + nrm((S5_GROUPS, S5_STATE), 0.01)
    a_lam_im = math.pi * jnp.arange(S5_STATE, dtype=jnp.float32)[None, :] + nrm((S5_GROUPS, S5_STATE), 0.01)
    a_log_dt = jax.random.uniform(next(ks), (S5_GROUPS,), jnp.float32, math.log(DT_MIN), math.log(DT_MAX))
    a_b_re = nrm((S5_GROUPS, S5_STATE, S5_GROUP), (2 * S5_GROUP) ** -0.5)
    a_b_im = nrm((S5_GROUPS, S5_STATE, S5_GROUP), (2 * S5_GROUP) ** -0.5)
    a_c_re = nrm((S5_GROUPS, S5_GROUP, S5_STATE), S5_STATE ** -0.5)
    a_c_im = nrm((S5_GROUPS, S5_GROUP, S5_STATE), S5_STATE ** -0.5)
    a_d = nrm((S5_GROUPS, S5_GROUP), 1.0)
    a_glu_w = nrm((A_WIDTH, A_WIDTH), A_WIDTH ** -0.5)
    a_glu_b = nrm((A_WIDTH,), 0.02)
    b_conv_w = nrm((CONV_WIDTH, B_WIDTH), CONV_WIDTH ** -0.5)
    l0_w_out = nrm((MIX_WIDTH, D_MODEL), MIX_WIDTH ** -0.5)
    l0_norm_ffn_g = gain(D_MODEL)
    l0_peer_wq, l0_peer_k1, l0_peer_k2, l0_peer_u, l0_peer_v = peer_params()
    l1_norm_mix_g = gain(D_MODEL)
    l1_w_in = nrm((D_MODEL, ODD_IN_WIDTH), D_MODEL ** -0.5)
    c_vnorm_g = gain(C_WIDTH)
    c_ws = nrm((GMLP_HEADS, GMLP_CHUNK, GMLP_CHUNK), 0.5 * GMLP_CHUNK ** -0.5)
    c_bs = 1.0 + nrm((GMLP_HEADS, GMLP_CHUNK), 0.1)
    l1_w_out = nrm((MIX_WIDTH, D_MODEL), MIX_WIDTH ** -0.5)
    l1_norm_ffn_g = gain(D_MODEL)
    l1_peer_wq, l1_peer_k1, l1_peer_k2, l1_peer_u, l1_peer_v = peer_params()
    final_norm_g = gain(D_MODEL)
    return {
        "x": x,
        "l0_norm_mix_g": l0_norm_mix_g, "l0_w_in": l0_w_in,
        "a_lam_re": a_lam_re, "a_lam_im": a_lam_im, "a_log_dt": a_log_dt,
        "a_b_re": a_b_re, "a_b_im": a_b_im, "a_c_re": a_c_re, "a_c_im": a_c_im, "a_d": a_d,
        "a_glu_w": a_glu_w, "a_glu_b": a_glu_b, "b_conv_w": b_conv_w, "l0_w_out": l0_w_out,
        "l0_norm_ffn_g": l0_norm_ffn_g, "l0_peer_wq": l0_peer_wq, "l0_peer_k1": l0_peer_k1,
        "l0_peer_k2": l0_peer_k2, "l0_peer_u": l0_peer_u, "l0_peer_v": l0_peer_v,
        "l1_norm_mix_g": l1_norm_mix_g, "l1_w_in": l1_w_in, "c_vnorm_g": c_vnorm_g,
        "c_ws": c_ws, "c_bs": c_bs, "l1_w_out": l1_w_out,
        "l1_norm_ffn_g": l1_norm_ffn_g, "l1_peer_wq": l1_peer_wq, "l1_peer_k1": l1_peer_k1,
        "l1_peer_k2": l1_peer_k2, "l1_peer_u": l1_peer_u, "l1_peer_v": l1_peer_v,
        "final_norm_g": final_norm_g,
    }

def reference(x, l0_norm_mix_g, l0_w_in, a_lam_re, a_lam_im, a_log_dt, a_b_re, a_b_im, a_c_re, a_c_im, a_d,
              a_glu_w, a_glu_b, b_conv_w, l0_w_out, l0_norm_ffn_g, l0_peer_wq, l0_peer_k1, l0_peer_k2,
              l0_peer_u, l0_peer_v, l1_norm_mix_g, l1_w_in, c_vnorm_g, c_ws, c_bs, l1_w_out, l1_norm_ffn_g,
              l1_peer_wq, l1_peer_k1, l1_peer_k2, l1_peer_u, l1_peer_v, final_norm_g):
    layers = (
        (l0_norm_mix_g, (l0_w_in, a_lam_re, a_lam_im, a_log_dt, a_b_re, a_b_im, a_c_re, a_c_im, a_d,
                         a_glu_w, a_glu_b, b_conv_w, l0_w_out),
         l0_norm_ffn_g, (l0_peer_wq, l0_peer_k1, l0_peer_k2, l0_peer_u, l0_peer_v)),
        (l1_norm_mix_g, (l1_w_in, c_vnorm_g, c_ws, c_bs, l1_w_out),
         l1_norm_ffn_g, (l1_peer_wq, l1_peer_k1, l1_peer_k2, l1_peer_u, l1_peer_v)),
    )
    h = x
    for layer in range(DEPTH):
        norm_mix_g, mix_params, norm_ffn_g, peer_params = layers[layer]
        hn = rmsnorm(h, norm_mix_g)
        if layer % 2 == 0:
            h = h + even_mixer(hn, *mix_params)
        else:
            h = h + odd_mixer(hn, *mix_params)
        h = h + peer_ffn(rmsnorm(h, norm_ffn_g), *peer_params)
    return rmsnorm(h, final_norm_g)


_drawn_inputs = setup_inputs


def setup_inputs(seed=0):
    import zlib

    import numpy as np

    out = dict(_drawn_inputs(seed))
    spreads = {}
    factors = {'a_lam_re': 64.0,
     'a_glu_b': 4.657,
     'l1_norm_mix_g': 3.049,
     'c_vnorm_g': 24.163,
     'l1_norm_ffn_g': 13.565,
     'final_norm_g': 8.016}
    for name, (base, spread) in spreads.items():
        noise = np.random.default_rng([zlib.crc32(name.encode()), seed]).standard_normal(out[name].shape)
        drawn = base * np.exp(spread * noise) if base else spread * noise
        out[name] = __import__('jax').numpy.asarray(drawn.astype(out[name].dtype))
    for name, factor in factors.items():
        out[name] = (out[name] * factor).astype(out[name].dtype)
    return out
```

```python
import concourse.bass as bass
from concourse import mybir
from contextlib import ExitStack

F32 = mybir.dt.float32
F32R = mybir.dt.float32r
U32 = mybir.dt.uint32
ALU = mybir.AluOpType
ACT = mybir.ActivationFunctionType
AXX = mybir.AxisListType.X

P = 128
SEQ = 256
TB = SEQ // P
D = 1024
KC = D // P
GROUP = 512
EVEN_IN = 2048
ODD_IN = 2560
WIDTH = 512
WC = WIDTH // P
S5_TILES = 2048 // P
HEADS = 8
ROWS = 2 * HEADS
KEYS = 128
TOPK = 16
CAND = TOPK * TOPK
PICKS = HEADS * TOPK
SLICES = 128
UNROLL = 4
GATE_TOKENS = 8
EPS = 1e-6
LOWEST = -3.0e38
TWO_PI = 6.283185307179586
TP1 = 6.28125
TP2 = 0.0019340515136718750
TP3 = TWO_PI - TP1 - TP2
ROUND = 12582912.0
PI_IN = 3.1415925


def trunk(nc, a, out):
    ctx = ExitStack()
    with ctx:
        def sb(name, shape, dt=F32):
            return ctx.enter_context(nc.sbuf_tensor(name, shape, dt))

        arena = sb("arena", [P, 32768])
        ring = sb("ring", [P, 8192])
        x = sb("x_res", [P, TB * D])
        h_parts = sb("h_parts", [P, KC * 2 * SEQ], F32R)
        u_parts = sb("u_parts", [P, 2 * D], F32R)
        v_parts = sb("v_parts", [P, 2 * D], F32R)
        w_parts = sb("w_parts", [P, 2 * 2 * SEQ], F32R)
        act_buf = sb("act_buf", [P, 2 * SEQ])
        low_buf = sb("low_buf", [P, SEQ])
        ident = sb("ident", [P, P])
        stat = sb("stat", [P, 64])
        psum = [ctx.enter_context(nc.psum_tensor(f"bank{i}", [P, 512], F32)) for i in range(8)]

        mem = dict(arena=arena, ring=ring, x=x, h_parts=h_parts, u_parts=u_parts, v_parts=v_parts,
                   w_parts=w_parts, act_buf=act_buf, low_buf=low_buf, ident=ident, stat=stat, psum=psum)
        made = {}

        def sem(name):
            if name not in made:
                made[name] = nc.alloc_semaphore(name)
            return made[name]

        def phase_over():
            nc.clear_and_free_semaphores(list(made.values()))
            nc.all_engine_barrier()
            made.clear()

        even_mixer(nc, a, mem, sem)
        phase_over()
        peer(nc, a, mem, sem, "l0")
        phase_over()
        odd_mixer(nc, a, mem, sem)
        phase_over()
        peer(nc, a, mem, sem, "l1")
        phase_over()
        final_norm(nc, a, mem, sem, out)


def ordered(eng, sem):
    count = [0]

    def link(ins):
        count[0] += 1
        ins.then_inc(sem, 1)
        eng.wait_ge(sem, count[0])
    return link



def norm_act(nc, act, mem, s, n, xn):
    for tb in range(TB):
        nc.scalar.activation(xn[:, tb * D:(tb + 1) * D], mem["x"][:, tb * D:(tb + 1) * D], ACT.Square,
                             accum_out=mem["stat"][:, tb:tb + 1]).then_inc(s(n + "_squares"), 1)
    act.wait_ge(s(n + "_meansq"), 1)
    nc.scalar.activation(mem["stat"][:, 4:6], mem["stat"][:, 2:4], ACT.Sqrt).then_inc(s(n + "_rms"), 1)


def norm_scale(nc, dve, mem, s, n, xn):
    stat = mem["stat"]
    dve.wait_ge(s(n + "_squares"), TB)
    nc.vector.tensor_scalar(stat[:, 2:4], stat[:, 0:2], 1.0 / D, EPS, ALU.mult, ALU.add)\
        .then_inc(s(n + "_meansq"), 1)
    dve.wait_ge(s(n + "_rms"), 1)
    nc.vector.reciprocal(stat[:, 6:8], stat[:, 4:6]).then_inc(s(n + "_rstd"), 1)
    dve.wait_ge(s(n + "_rstd"), 1)
    for tb in range(TB):
        nc.vector.tensor_scalar(xn[:, tb * D:(tb + 1) * D], mem["x"][:, tb * D:(tb + 1) * D],
                                stat[:, 6 + tb:7 + tb], None, ALU.mult).then_inc(s(n + "_xn"), 1)


def norm_pe(nc, pe, mem, s, n, xn):
    for tb in range(TB):
        pe.wait_ge(s(n + "_xn"), tb + 1)
        for c in range(KC):
            o = (c % 2) * SEQ + tb * P
            last = nc.tensor.transpose(mem["psum"][c // 2][:, o:o + P],
                                       xn[:, tb * D + c * P:tb * D + (c + 1) * P], mem["ident"][:, :])
    last.then_inc(s(n + "_turned"), 1)


def norm_gain(nc, dve, mem, s, n, hT, gain):
    dve.wait_ge(s(n + "_turned"), 1)
    for b in range(4):
        nc.vector.tensor_tensor(
            hT[:, 2 * b * SEQ:2 * (b + 1) * SEQ].rearrange("p (c t) -> p c t", c=2),
            mem["psum"][b][:, :].rearrange("p (c t) -> p c t", c=2),
            gain[:, 2 * b:2 * b + 2].unsqueeze(2).broadcast_to([P, 2, SEQ]), ALU.mult)\
            .then_inc(s(n + "_hT"), 1)



def even_mixer(nc, a, mem, s):
    arena, ring, x, psum, ident = mem["arena"], mem["ring"], mem["x"], mem["psum"], mem["ident"]
    w_in = arena[:, 0:16384].rearrange("p (g k m) -> p g k m", g=4, k=KC)
    pT = arena[:, 16384:20480].rearrange("p (m t) -> p m t", t=SEQ)
    e_cos = arena[:, 20480:24576].rearrange("p (i t) -> p i t", t=SEQ)
    e_sin = arena[:, 24576:28672].rearrange("p (i t) -> p i t", t=SEQ)
    hT = arena[:, 28672:30720]
    xn = arena[:, 30720:32768]
    w_out = arena[:, 0:8192].rearrange("p (k m) -> p k m", k=KC)
    scratch = arena[:, 8192:16384]
    catT = hT.rearrange("p (m t) -> p m t", t=SEQ)
    b_re = ring[:, 0:512].rearrange("p (c n) -> p c n", c=WC)
    b_im = ring[:, 512:1024].rearrange("p (c n) -> p c n", c=WC)
    c_re = ring[:, 1024:1536].rearrange("p (i n) -> p i n", i=S5_TILES)
    c_im = ring[:, 1536:2048].rearrange("p (i n) -> p i n", i=S5_TILES)
    glu_w = ring[:, 2048:4096].rearrange("p (k m) -> p k m", k=WC)
    t1 = ring[:, 4096:6144]
    t2 = ring[:, 6144:8192]
    small = mem["act_buf"]

    def col(i, n=S5_TILES):
        return small[:, 16 * i:16 * i + n]
    (lam_re, lam_im, dt, lrdt, mag, th, rev, turn, rem, sin, half, cos, a_im, den, nr, f_re, f_im,
     tmp1, tmp2, pw_cos, pw_sin, pw_cos2, pw_sin2) = (col(i) for i in range(23))
    gain = col(23, KC)
    conv_w = small[:, 384:396].rearrange("p (k c) -> p k c", k=3)
    d_skip = small[:, 400:404]
    glu_b = small[:, 404:408]

    with nc.Block() as block:
        @block.sync
        def _(sp):
            sp.dma_start(x[:, :].rearrange("p (b d) -> p b d", b=TB),
                         a["x"].rearrange("(b p) d -> p b d", p=P)).then_inc(s("x_in"), 16)
            sp.dma_start(small[:, 0:48], a["s5_params"]).then_inc(s("s5_params_in"), 16)
            sp.dma_start(gain, a["l0_norm_mix_g"]).then_inc(s("gain0_in"), 16)
            src = a["l0_w_in"].rearrange("(k p) (g m) -> g p k m", p=P, g=4)
            for g in range(4):
                sp.dma_start(w_in[:, g], src[g]).then_inc(s(f"w_in0_{g}"), 16)
            sp.dma_start(ring[:, 0:1024], a["s5_b"]).then_inc(s("s5_b_in"), 16)
            sp.dma_start(ring[:, 1024:2048], a["s5_c"]).then_inc(s("s5_c_in"), 16)
            sp.dma_start(small[:, 384:396], a["conv_w"]).then_inc(s("conv_w_in"), 16)
            sp.dma_start(small[:, 400:408], a["d_and_glu_b"]).then_inc(s("d_in"), 16)
            sp.dma_start(glu_w, a["a_glu_w"].rearrange("(k p) m -> p k m", p=P)).then_inc(s("glu_w_in"), 16)
            sp.wait_ge(s("proj0"), 8)
            sp.dma_start(w_out, a["l0_w_out"].rearrange("(k p) m -> p k m", p=P)).then_inc(s("w_out0_in"), 16)

        @block.gpsimd
        def _(pool):
            nc.gpsimd.memset(ident[:, :], 0.0).then_inc(s("ident_zero"), 1)
            pool.wait_ge(s("ident_zero"), 1)
            nc.gpsimd.affine_select(out=ident[:, :], in_=ident[:, :], compare_op=ALU.not_equal, fill=1.0,
                                    base=0, pattern=[[-1, P]], channel_multiplier=1)\
                .then_inc(s("ident_made"), 1)
            pool.wait_ge(s("e_tables"), 1)
            for i in range(S5_TILES):
                g, o1, o2, h = (scratch[:, (i % 2) * 4096 + 512 * n:(i % 2) * 4096 + 512 * (n + 1)]
                                for n in (3, 4, 5, 6))
                pool.wait_ge(s("s5_scanned"), 2 * i + 2)
                nc.gpsimd.tensor_tensor(o1.rearrange("p (r t) -> p r t", r=2),
                                        g.rearrange("p (r t) -> p r t", r=2),
                                        e_cos[:, i].unsqueeze(1).broadcast_to([P, 2, SEQ]), ALU.mult)\
                    .then_inc(s("s5_turned"), 1)
                nc.gpsimd.tensor_tensor(o2.rearrange("p (r t) -> p r t", r=2),
                                        g.rearrange("p (r t) -> p r t", r=2),
                                        e_sin[:, i].unsqueeze(1).broadcast_to([P, 2, SEQ]), ALU.mult)\
                    .then_inc(s("s5_turned"), 1)
                pool.wait_ge(s("s5_turned"), 2 * i + 2)
                if i >= 2:
                    pool.wait_ge(s("s5_y"), i - 1)
                nc.gpsimd.tensor_tensor(h[:, 0:SEQ], o1[:, 0:SEQ], o2[:, SEQ:2 * SEQ], ALU.subtract)\
                    .then_inc(s("s5_h"), 1)
                nc.gpsimd.tensor_tensor(h[:, SEQ:2 * SEQ], o1[:, SEQ:2 * SEQ], o2[:, 0:SEQ], ALU.add)\
                    .then_inc(s("s5_h"), 1)

        @block.scalar
        def _(act):
            act.wait_ge(s("x_in"), 16)
            norm_act(nc, act, mem, s, "n0", xn)
            act.wait_ge(s("s5_params_in"), 16)
            nc.scalar.activation(dt, dt, ACT.Exp).then_inc(s("s5_dt"), 1)
            act.wait_ge(s("s5_angles"), 1)
            nc.scalar.activation(mag, lrdt, ACT.Exp).then_inc(s("s5_mag"), 1)
            nc.scalar.activation(sin, rem, ACT.Sin).then_inc(s("s5_sin"), 1)
            nc.scalar.activation(half, rem, ACT.Sin, scale=0.5).then_inc(s("s5_sin"), 1)
            for b in range(8):
                act.wait_ge(s("proj0"), b + 1)
                nc.scalar.activation(pT[:, 2 * b:2 * b + 2], psum[b][:, :].rearrange("p (m t) -> p m t", m=2),
                                     ACT.Copy).then_inc(s("pT"), 1)
            for c in range(WC):
                act.wait_ge(s("s5_skip"), c + 1)
                nc.scalar.activation(pT[:, c], pT[:, c], ACT.Gelu_apprx_tanh).then_inc(s("s5_gelu"), 1)
            for c in range(WC):
                act.wait_ge(s("glu"), c + 1)
                nc.scalar.activation(scratch[:, c * SEQ:(c + 1) * SEQ], psum[c][:, 0:SEQ], ACT.Sigmoid,
                                     bias=glu_b[:, c:c + 1]).then_inc(s("glu_sig"), 1)

        @block.vector
        def _(dve):
            link = ordered(dve, s("even_dve_order"))
            tt, ts = nc.vector.tensor_tensor, nc.vector.tensor_scalar
            dve.wait_ge(s("x_in"), 16)
            norm_scale(nc, dve, mem, s, "n0", xn)
            dve.wait_ge(s("s5_dt"), 1)
            link(tt(lrdt, lam_re, dt, ALU.mult))
            link(tt(th, lam_im, dt, ALU.mult))
            link(ts(rev, th, 1.0 / TWO_PI, ROUND, ALU.mult, ALU.add))
            link(ts(turn, rev, -ROUND, None, ALU.add))
            link(nc.vector.scalar_tensor_tensor(rem, turn, -TP1, th, ALU.mult, ALU.add))
            link(nc.vector.scalar_tensor_tensor(rem, turn, -TP2, rem, ALU.mult, ALU.add))
            link(nc.vector.scalar_tensor_tensor(rem, turn, -TP3, rem, ALU.mult, ALU.add))
            ts(rem, rem, PI_IN, -PI_IN, ALU.min, ALU.max).then_inc(s("s5_angles"), 1)
            norm_needs_gain = s("gain0_in")
            dve.wait_ge(norm_needs_gain, 16)
            norm_gain(nc, dve, mem, s, "n0", hT, gain)
            dve.wait_ge(s("s5_mag"), 1)
            dve.wait_ge(s("s5_sin"), 2)
            link(tt(cos, half, half, ALU.mult))
            link(ts(cos, cos, -2.0, 1.0, ALU.mult, ALU.add))
            link(tt(nr, mag, cos, ALU.mult))
            link(ts(nr, nr, -1.0, None, ALU.add))
            link(tt(a_im, mag, sin, ALU.mult))
            link(tt(tmp1, lam_re, lam_re, ALU.mult))
            link(tt(tmp2, lam_im, lam_im, ALU.mult))
            link(tt(den, tmp1, tmp2, ALU.add))
            link(nc.vector.reciprocal(den, den))
            link(tt(tmp1, nr, lam_re, ALU.mult))
            link(tt(tmp2, a_im, lam_im, ALU.mult))
            link(tt(tmp1, tmp1, tmp2, ALU.add))
            link(tt(f_re, tmp1, den, ALU.mult))
            link(tt(tmp1, a_im, lam_re, ALU.mult))
            link(tt(tmp2, nr, lam_im, ALU.mult))
            link(tt(tmp1, tmp1, tmp2, ALU.subtract))
            link(tt(f_im, tmp1, den, ALU.mult))
            nc.vector.memset(e_cos[:, :, 0:1], 1.0)
            link(nc.vector.memset(e_sin[:, :, 0:1], 0.0))
            link(nc.vector.tensor_copy(pw_cos, cos))
            link(nc.vector.tensor_copy(pw_sin, sin))
            n = 1
            while n < SEQ:
                pc = pw_cos.unsqueeze(2).broadcast_to([P, S5_TILES, n])
                ps = pw_sin.unsqueeze(2).broadcast_to([P, S5_TILES, n])
                u1 = t1[:, 0:S5_TILES * n].rearrange("p (i t) -> p i t", i=S5_TILES)
                u2 = t2[:, 0:S5_TILES * n].rearrange("p (i t) -> p i t", i=S5_TILES)
                tt(u1, e_cos[:, :, 0:n], pc, ALU.mult)
                link(tt(u2, e_sin[:, :, 0:n], ps, ALU.mult))
                link(tt(e_cos[:, :, n:2 * n], u1, u2, ALU.subtract))
                tt(u1, e_cos[:, :, 0:n], ps, ALU.mult)
                link(tt(u2, e_sin[:, :, 0:n], pc, ALU.mult))
                link(tt(e_sin[:, :, n:2 * n], u1, u2, ALU.add))
                n *= 2
                if n < SEQ:
                    tt(pw_cos2, pw_cos, pw_cos, ALU.mult)
                    tt(tmp1, pw_sin, pw_sin, ALU.mult)
                    link(tt(pw_sin2, pw_cos, pw_sin, ALU.mult))
                    tt(pw_cos, pw_cos2, tmp1, ALU.subtract)
                    link(ts(pw_sin, pw_sin2, 2.0, None, ALU.mult))
            dve.wait_ge(s("s5_c_in"), 16)
            fr = f_re.unsqueeze(2).broadcast_to([P, S5_TILES, 32])
            fi = f_im.unsqueeze(2).broadcast_to([P, S5_TILES, 32])
            q1, q2, q3, q4 = (t1[:, 512 * n:512 * (n + 1)].rearrange("p (i n) -> p i n", i=S5_TILES)
                              for n in range(4))
            tt(q1, c_re, fr, ALU.mult)
            tt(q2, c_im, fi, ALU.mult)
            tt(q3, c_re, fi, ALU.mult)
            link(tt(q4, c_im, fr, ALU.mult))
            link(tt(c_re, q1, q2, ALU.subtract))
            link(tt(q3, q3, q4, ALU.add))
            ts(c_im, q3, -1.0, None, ALU.mult).then_inc(s("s5_c_scaled"), 1)
            link(nc.vector.tensor_copy(tmp1, tmp2))
            nc.vector.tensor_copy(tmp1, tmp2).then_inc(s("e_tables"), 1)
            dve.wait_ge(s("proj0"), 8)
            for i in range(S5_TILES):
                m1, m2, pq, g = (scratch[:, (i % 2) * 4096 + 512 * n:(i % 2) * 4096 + 512 * (n + 1)]
                                 for n in range(4))
                dve.wait_ge(s("s5_bu"), i + 1)
                bu = psum[i % 2][:, :].rearrange("p (r t) -> p r t", r=2)
                tt(m1.rearrange("p (r t) -> p r t", r=2), bu,
                   e_cos[:, i].unsqueeze(1).broadcast_to([P, 2, SEQ]), ALU.mult).then_inc(s("s5_bu_used"), 1)
                tt(m2.rearrange("p (r t) -> p r t", r=2), bu,
                   e_sin[:, i].unsqueeze(1).broadcast_to([P, 2, SEQ]), ALU.mult).then_inc(s("s5_bu_used"), 1)
                dve.wait_ge(s("s5_bu_used"), 2 * i + 2)
                tt(pq[:, 0:SEQ], m1[:, 0:SEQ], m2[:, SEQ:], ALU.add)
                link(tt(pq[:, SEQ:], m1[:, SEQ:], m2[:, 0:SEQ], ALU.subtract))
                if i >= 2:
                    dve.wait_ge(s("s5_turned"), 2 * (i - 1))
                decay = mag[:, i:i + 1].broadcast_to([P, SEQ])
                for r in range(2):
                    nc.vector.tensor_tensor_scan(g[:, r * SEQ:(r + 1) * SEQ], decay,
                                                 pq[:, r * SEQ:(r + 1) * SEQ], 0.0, ALU.mult, ALU.add)\
                        .then_inc(s("s5_scanned"), 1)
                if i % 4 == 3:
                    c = i // 4
                    if c == 0:
                        dve.wait_ge(s("pT"), 8)
                        dve.wait_ge(s("conv_w_in"), 16)
                    z, acc = t1[:, 0:SEQ], t1[:, SEQ:2 * SEQ]
                    link(tt(z, pT[:, 8 + c], pT[:, 12 + c], ALU.mult))
                    link(ts(acc, z, conv_w[:, 2, c:c + 1], None, ALU.mult))
                    link(nc.vector.scalar_tensor_tensor(acc[:, 1:], z[:, 0:SEQ - 1], conv_w[:, 1, c:c + 1],
                                                        acc[:, 1:], ALU.mult, ALU.add))
                    link(nc.vector.scalar_tensor_tensor(acc[:, 2:], z[:, 0:SEQ - 2], conv_w[:, 0, c:c + 1],
                                                        acc[:, 2:], ALU.mult, ALU.add))
                    link(tt(catT[:, WC + c], acc, pT[:, 4 + c], ALU.mult))
            dve.wait_ge(s("d_in"), 16)
            for c in range(WC):
                dve.wait_ge(s("s5_y"), 4 * c + 4)
                nc.vector.scalar_tensor_tensor(pT[:, c], pT[:, c], d_skip[:, c:c + 1], psum[4 + c][:, 0:SEQ],
                                               ALU.mult, ALU.add).then_inc(s("s5_skip"), 1)
            for c in range(WC):
                dve.wait_ge(s("glu_sig"), c + 1)
                dve.wait_ge(s("s5_gelu"), WC)
                tt(catT[:, c], pT[:, c], scratch[:, c * SEQ:(c + 1) * SEQ], ALU.mult)\
                    .then_inc(s("catT0"), 1)
            for n in range(4):
                dve.wait_ge(s("mixed0"), n + 1)
                xs = x[:, n * 512:(n + 1) * 512]
                tt(xs, xs, psum[4 + n][:, :], ALU.add).then_inc(s("x_after_mix0"), 1)
            dve.wait_ge(s("x_after_mix0"), 4)

        @block.tensor
        def _(pe):
            pe.wait_ge(s("ident_made"), 1)
            norm_pe(nc, pe, mem, s, "n0", xn)
            pe.wait_ge(s("n0_hT"), 4)
            for m in range(16):
                if m % 4 == 0:
                    pe.wait_ge(s(f"w_in0_{m // 4}"), 16)
                for k in range(KC):
                    last = nc.tensor.matmul(psum[m // 2][:, (m % 2) * SEQ:(m % 2 + 1) * SEQ],
                                            w_in[:, m // 4, k, (m % 4) * P:(m % 4 + 1) * P],
                                            hT[:, k * SEQ:(k + 1) * SEQ], start=(k == 0), stop=(k == KC - 1))
                if m % 2:
                    last.then_inc(s("proj0"), 1)
            pe.wait_ge(s("s5_b_in"), 16)
            pe.wait_ge(s("pT"), 8)
            pe.wait_ge(s("s5_c_scaled"), 1)

            def product_in(i):
                c, j = i // 4, i % 4
                if i >= 2:
                    pe.wait_ge(s("s5_bu_used"), 2 * (i - 1))
                for r, b in enumerate((b_re, b_im)):
                    last = nc.tensor.matmul(psum[i % 2][:, r * SEQ:(r + 1) * SEQ], b[32 * j:32 * j + 32, c, :],
                                            pT[32 * j:32 * j + 32, c, :], start=True, stop=True)
                last.then_inc(s("s5_bu"), 1)

            def product_out(i):
                c, j = i // 4, i % 4
                pe.wait_ge(s("s5_h"), 2 * i + 2)
                h = scratch[:, (i % 2) * 4096 + 3072:(i % 2) * 4096 + 3584]
                for r, cm in enumerate((c_re, c_im)):
                    last = nc.tensor.matmul(psum[4 + c][32 * j:32 * j + 32, 0:SEQ], cm[:, i, :],
                                            h[:, r * SEQ:(r + 1) * SEQ], start=(r == 0), stop=(r == 1))
                last.then_inc(s("s5_y"), 1)

            for i in range(S5_TILES + 2):
                if i < S5_TILES:
                    product_in(i)
                if i >= 2:
                    product_out(i - 2)
            pe.wait_ge(s("glu_w_in"), 16)
            pe.wait_ge(s("s5_gelu"), WC)
            for m in range(WC):
                for k in range(WC):
                    last = nc.tensor.matmul(psum[m][:, 0:SEQ], glu_w[:, k, m * P:(m + 1) * P], pT[:, k, :],
                                            start=(k == 0), stop=(k == WC - 1))
                last.then_inc(s("glu"), 1)
            pe.wait_ge(s("w_out0_in"), 16)
            pe.wait_ge(s("catT0"), WC)
            for n in range(4):
                tb, half = n // 2, n % 2
                for k in range(KC):
                    last = nc.tensor.matmul(psum[4 + n][:, :], catT[:, k, tb * P:(tb + 1) * P],
                                            w_out[:, k, half * 512:(half + 1) * 512],
                                            start=(k == 0), stop=(k == KC - 1))
                last.then_inc(s("mixed0"), 1)



def odd_mixer(nc, a, mem, s):
    arena, ring, x, psum, ident = mem["arena"], mem["ring"], mem["x"], mem["psum"], mem["ident"]
    w_in = arena[:, 0:20480].rearrange("p (g k m) -> p g k m", g=5, k=KC)
    u = arena[:, 20480:21504]
    v = arena[:, 21504:22528]
    vals = arena[:, 22528:23552]
    qT = arena[:, 23552:24576].rearrange("p (c t) -> p c t", t=SEQ)
    kT = arena[:, 24576:25600].rearrange("p (c t) -> p c t", t=SEQ)
    ws = arena[:, 25600:26624].rearrange("p (h t) -> p h t", h=HEADS)
    catT = arena[:, 26624:28672].rearrange("p (m t) -> p m t", t=SEQ)
    hT = arena[:, 28672:30720]
    xn = arena[:, 30720:32768]
    w_out = arena[:, 0:8192].rearrange("p (k m) -> p k m", k=KC)
    scratch = arena[:, 8192:16384]
    vgain = ring[:, 0:512]
    mask = ring[:, 512:1024].rearrange("p (b t) -> p b t", b=2)
    tri = ring[:, 1024:1152]
    ones = ring[:, 1152:1280]
    sq = ring[:, 2048:3072]
    small = mem["act_buf"]
    gain = small[:, 0:KC]
    bias = small[:, 16:16 + HEADS]
    stat = mem["stat"]


    with nc.Block() as block:
        @block.sync
        def _(sp):
            sp.dma_start(gain, a["l1_norm_mix_g"]).then_inc(s("gain2_in"), 16)
            src = a["l1_w_in"].rearrange("(k p) (g m) -> g p k m", p=P, g=5)
            for g in range(5):
                sp.dma_start(w_in[:, g], src[g]).then_inc(s(f"w_in1_{g}"), 16)
            sp.dma_start(vgain, a["c_vnorm_g"].partition_broadcast(P)).then_inc(s("vgain_in"), 16)
            sp.dma_start(ws, a["c_ws"]).then_inc(s("ws_in"), 16)
            sp.dma_start(bias, a["c_bs"]).then_inc(s("bias_in"), 16)
            sp.wait_ge(s("proj_v"), TB)
            sp.dma_start(w_out, a["l1_w_out"].rearrange("(k p) m -> p k m", p=P)).then_inc(s("w_out1_in"), 16)

        @block.gpsimd
        def _(pool):
            nc.gpsimd.memset(ring[:, 512:1280], 1.0).then_inc(s("masks_one"), 1)
            pool.wait_ge(s("masks_one"), 1)
            for b in range(2):
                nc.gpsimd.affine_select(out=mask[:, b], in_=mask[:, b], compare_op=ALU.is_ge, fill=0.0,
                                        base=-1 - P * b, pattern=[[1, SEQ]], channel_multiplier=-1)\
                    .then_inc(s("masks_made"), 1)
            nc.gpsimd.affine_select(out=tri, in_=tri, compare_op=ALU.is_ge, fill=0.0,
                                    base=0, pattern=[[-1, P]], channel_multiplier=1)\
                .then_inc(s("masks_made"), 1)
            pool.wait_ge(s("ws_in"), 16)
            nc.gpsimd.affine_select(out=ws, in_=ws, compare_op=ALU.is_ge, fill=0.0,
                                    base=0, pattern=[[0, HEADS], [1, P]], channel_multiplier=-1)\
                .then_inc(s("ws_masked"), 1)

        @block.scalar
        def _(act):
            norm_act(nc, act, mem, s, "n2", xn)
            for tb in range(TB):
                act.wait_ge(s("proj_u"), tb + 1)
                nc.scalar.activation(u[:, tb * 512:(tb + 1) * 512], psum[4 + tb][:, :],
                                     ACT.Gelu_apprx_tanh).then_inc(s("u_gelu"), 1)
            for tb in range(TB):
                act.wait_ge(s("proj_v"), tb + 1)
                nc.scalar.activation(v[:, tb * 512:(tb + 1) * 512], psum[6 + tb][:, :],
                                     ACT.Gelu_apprx_tanh).then_inc(s("v_gelu"), 1)
            act.wait_ge(s("v_gelu"), TB)
            for tb in range(TB):
                nc.scalar.activation(sq[:, tb * 512:(tb + 1) * 512], v[:, tb * 512:(tb + 1) * 512], ACT.Square,
                                     accum_out=stat[:, 16 + tb:17 + tb]).then_inc(s("v_squares"), 1)
            for b in range(2):
                act.wait_ge(s("proj_q"), b + 1)
                nc.scalar.activation(qT[:, 2 * b:2 * b + 2], psum[b][:, :].rearrange("p (c t) -> p c t", c=2),
                                     ACT.Copy, scale=0.125).then_inc(s("qT"), 1)
            for b in range(2):
                act.wait_ge(s("proj_k"), b + 1)
                nc.scalar.activation(kT[:, 2 * b:2 * b + 2], psum[2 + b][:, :].rearrange("p (c t) -> p c t", c=2),
                                     ACT.Copy).then_inc(s("kT"), 1)
            for tb in range(TB):
                act.wait_ge(s("proj_vals"), tb + 1)
                nc.scalar.activation(vals[:, tb * 512:(tb + 1) * 512], psum[4 + tb][:, :],
                                     ACT.Copy).then_inc(s("vals"), 1)
            act.wait_ge(s("v_meansq"), 1)
            nc.scalar.activation(stat[:, 20:22], stat[:, 18:20], ACT.Sqrt).then_inc(s("v_rms"), 1)
            for h in range(HEADS):
                z, e, w = (scratch[:, (h % 2) * 2048 + 512 * n:(h % 2) * 2048 + 512 * (n + 1)]
                           for n in (0, 1, 3))
                act.wait_ge(s("sb_z"), h + 1)
                if h >= 2:
                    act.wait_ge(s("sb_arg"), 2 * (h - 1))
                nc.scalar.activation(z, psum[h % 2][:, :], ACT.Copy).then_inc(s("sb_z_copied"), 1)
                nc.scalar.activation(e, psum[h % 2][:, :], ACT.Abs).then_inc(s("sb_act_order"), 1)
                act.wait_ge(s("sb_act_order"), 3 * h + 1)
                nc.scalar.activation(e, e, ACT.Exp, scale=-1.0).then_inc(s("sb_act_order"), 1)
                act.wait_ge(s("sb_act_order"), 3 * h + 2)
                nc.scalar.activation(e, e, ACT.Ln, bias=1.0).then_inc(s("sb_act_order"), 1)
                act.wait_ge(s("sb_arg"), 2 * h + 2)
                nc.scalar.activation(w, w, ACT.Exp).then_inc(s("sb_exp"), 1)
                if h % 2 and h >= 3:
                    c = h // 2 - 1
                    act.wait_ge(s("sb_o"), 2 * c + 2)
                    nc.scalar.activation(catT[:, WC + c], psum[4 + c % 2][:, 0:SEQ], ACT.Copy)\
                        .then_inc(s("sb_out"), 1)
            act.wait_ge(s("sb_o"), HEADS)
            nc.scalar.activation(catT[:, WC + 3], psum[5][:, 0:SEQ], ACT.Copy).then_inc(s("sb_out"), 1)

        @block.vector
        def _(dve):
            link = ordered(dve, s("odd_dve_order"))
            tt, ts, stt = nc.vector.tensor_tensor, nc.vector.tensor_scalar, nc.vector.scalar_tensor_tensor
            norm_scale(nc, dve, mem, s, "n2", xn)
            dve.wait_ge(s("gain2_in"), 16)
            norm_gain(nc, dve, mem, s, "n2", hT, gain)
            dve.wait_ge(s("v_squares"), TB)
            ts(stat[:, 18:20], stat[:, 16:18], 1.0 / WIDTH, EPS, ALU.mult, ALU.add).then_inc(s("v_meansq"), 1)
            dve.wait_ge(s("v_rms"), 1)
            link(nc.vector.reciprocal(stat[:, 22:24], stat[:, 20:22]))
            dve.wait_ge(s("vgain_in"), 16)
            for tb in range(TB):
                vs = v[:, tb * 512:(tb + 1) * 512]
                stt(vs, vs, stat[:, 22 + tb:23 + tb], vgain, ALU.mult, ALU.mult).then_inc(s("v_normed"), 1)
            dve.wait_ge(s("bias_in"), 16)
            dve.wait_ge(s("u_gelu"), TB)
            for tb in range(TB):
                dve.wait_ge(s("spatial"), tb + 1)
                us = u[:, tb * 512:(tb + 1) * 512]
                y = sq[:, tb * 512:(tb + 1) * 512]
                link(tt(y.rearrange("p (h d) -> p h d", h=HEADS),
                        psum[6 + tb][:, :].rearrange("p (h d) -> p h d", h=HEADS),
                        bias.unsqueeze(2).broadcast_to([P, HEADS, 64]), ALU.add))
                tt(us, us, y, ALU.mult).then_inc(s("gmlp"), 1)
            dve.wait_ge(s("gmlp_turned"), 1)
            for b in range(2):
                nc.vector.tensor_copy(catT[:, 2 * b:2 * b + 2],
                                      psum[2 + b][:, :].rearrange("p (c t) -> p c t", c=2))\
                    .then_inc(s("catT1"), 1)
            dve.wait_ge(s("masks_made"), 3)
            for h in range(HEADS):
                z, e, sp_, w = (scratch[:, (h % 2) * 2048 + 512 * n:(h % 2) * 2048 + 512 * (n + 1)]
                                for n in range(4))
                m = mask.rearrange("p b t -> p (b t)")
                dve.wait_ge(s("sb_act_order"), 3 * h + 3)
                dve.wait_ge(s("sb_z_copied"), h + 1)
                if h >= 2:
                    dve.wait_ge(s("sb_sum"), h - 1)
                link(stt(sp_, z, 0.0, e, ALU.max, ALU.add))
                tt(sp_, sp_, m, ALU.mult).then_inc(s("sb_softplus"), 1)
                dve.wait_ge(s("sb_sum"), h + 1)
                if h >= 2:
                    dve.wait_ge(s("sb_o"), h - 1)
                tt(w, z, psum[2 + h % 2][:, :], ALU.subtract).then_inc(s("sb_arg"), 1)
                dve.wait_ge(s("sb_arg"), 2 * h + 1)
                ts(w, w, 0.0, None, ALU.min).then_inc(s("sb_arg"), 1)
                dve.wait_ge(s("sb_exp"), h + 1)
                tt(w, w, m, ALU.mult).then_inc(s("sb_w"), 1)
            for n in range(4):
                dve.wait_ge(s("mixed1"), n + 1)
                xs = x[:, n * 512:(n + 1) * 512]
                tt(xs, xs, psum[n if n < 2 else 4 + n][:, :], ALU.add).then_inc(s("x_after_mix1"), 1)
            dve.wait_ge(s("x_after_mix1"), 4)

        @block.tensor
        def _(pe):
            norm_pe(nc, pe, mem, s, "n2", xn)
            pe.wait_ge(s("n2_hT"), 4)

            def token_major(g, bank, name):
                pe.wait_ge(s(f"w_in1_{g}"), 16)
                for tb in range(TB):
                    for k in range(KC):
                        last = nc.tensor.matmul(psum[bank + tb][:, :], hT[:, k * SEQ + tb * P:k * SEQ + (tb + 1) * P],
                                                w_in[:, g, k, :], start=(k == 0), stop=(k == KC - 1))
                    last.then_inc(s(name), 1)

            def feature_major(g, bank, name):
                pe.wait_ge(s(f"w_in1_{g}"), 16)
                for m in range(WC):
                    for k in range(KC):
                        last = nc.tensor.matmul(psum[bank + m // 2][:, (m % 2) * SEQ:(m % 2 + 1) * SEQ],
                                                w_in[:, g, k, m * P:(m + 1) * P], hT[:, k * SEQ:(k + 1) * SEQ],
                                                start=(k == 0), stop=(k == KC - 1))
                    if m % 2:
                        last.then_inc(s(name), 1)

            token_major(0, 4, "proj_u")
            token_major(1, 6, "proj_v")
            feature_major(2, 0, "proj_q")
            feature_major(3, 2, "proj_k")
            pe.wait_ge(s("u_gelu"), TB)
            token_major(4, 4, "proj_vals")
            pe.wait_ge(s("proj_vals"), TB)
            pe.wait_ge(s("qT"), 2)
            pe.wait_ge(s("ws_masked"), 1)
            for tb in range(TB):
                pe.wait_ge(s("v_normed"), tb + 1)
                for h in range(HEADS):
                    last = nc.tensor.matmul(psum[6 + tb][:, h * 64:(h + 1) * 64], ws[:, h, :],
                                            v[:, tb * 512 + h * 64:tb * 512 + (h + 1) * 64],
                                            start=True, stop=True)
                last.then_inc(s("spatial"), 1)
            pe.wait_ge(s("kT"), 2)
            for tb in range(TB):
                pe.wait_ge(s("gmlp"), tb + 1)
                for c in range(WC):
                    o = (c % 2) * SEQ + tb * P
                    last = nc.tensor.transpose(psum[2 + c // 2][:, o:o + P],
                                               u[:, tb * 512 + c * P:tb * 512 + (c + 1) * P], ident[:, :])
            last.then_inc(s("gmlp_turned"), 1)
            pe.wait_ge(s("vals"), TB)
            pe.wait_ge(s("masks_made"), 3)

            def scores(h):
                if h >= 2:
                    pe.wait_ge(s("sb_z_copied"), h - 1)
                    pe.wait_ge(s("sb_act_order"), 3 * (h - 2) + 1)
                r = 64 * (h % 2)
                for b in range(2):
                    last = nc.tensor.matmul(psum[h % 2][:, b * SEQ:(b + 1) * SEQ],
                                            kT[r:r + 64, h // 2, b * P:(b + 1) * P], qT[r:r + 64, h // 2, :],
                                            start=True, stop=True)
                last.then_inc(s("sb_z"), 1)

            def sums(h):
                sp_ = scratch[:, (h % 2) * 2048 + 1024:(h % 2) * 2048 + 1536]
                pe.wait_ge(s("sb_softplus"), h + 1)
                if h < 2:
                    pe.wait_ge(s("catT1"), 2)
                else:
                    pe.wait_ge(s("sb_arg"), 2 * (h - 2) + 1)
                bank = psum[2 + h % 2]
                nc.tensor.matmul(bank[:, SEQ:], tri, sp_[:, SEQ:], start=True, stop=True)
                nc.tensor.matmul(bank[:, 0:SEQ], tri, sp_[:, 0:SEQ], start=True, stop=False)
                nc.tensor.matmul(bank[:, 0:SEQ], ones, sp_[:, SEQ:], start=False, stop=True)\
                    .then_inc(s("sb_sum"), 1)

            def outputs(h):
                w = scratch[:, (h % 2) * 2048 + 1536:(h % 2) * 2048 + 2048]
                c, r = h // 2, 64 * (h % 2)
                pe.wait_ge(s("sb_w"), h + 1)
                if c >= 2:
                    pe.wait_ge(s("sb_out"), c - 1)
                for b in range(2):
                    last = nc.tensor.matmul(psum[4 + c % 2][r:r + 64, 0:SEQ],
                                            vals[:, b * 512 + h * 64:b * 512 + (h + 1) * 64],
                                            w[:, b * SEQ:(b + 1) * SEQ], start=(b == 0), stop=(b == 1))
                last.then_inc(s("sb_o"), 1)

            scores(0)
            scores(1)
            for h in range(HEADS):
                sums(h)
                if h >= 1:
                    outputs(h - 1)
                if 2 <= h + 1 < HEADS:
                    scores(h + 1)
            outputs(HEADS - 1)
            pe.wait_ge(s("w_out1_in"), 16)
            pe.wait_ge(s("sb_out"), WC)
            pe.wait_ge(s("sb_act_order"), 3 * HEADS)
            for n in range(4):
                tb, half = n // 2, n % 2
                for k in range(KC):
                    last = nc.tensor.matmul(psum[n if n < 2 else 4 + n][:, :], catT[:, k, tb * P:(tb + 1) * P],
                                            w_out[:, k, half * 512:(half + 1) * 512],
                                            start=(k == 0), stop=(k == KC - 1))
                last.then_inc(s("mixed1"), 1)



def peer(nc, a, mem, shared_sem, layer):
    def s(name):
        return shared_sem(f"{layer}_{name}")

    arena, ring, x, psum, ident = (mem[k] for k in ("arena", "ring", "x", "psum", "ident"))
    h_parts = mem["h_parts"][:, :].rearrange("p (c r t) -> p c r t", c=KC, r=2)
    u_parts = mem["u_parts"][:, :].rearrange("p (r c e) -> p r c e", r=2, c=KC)
    v_parts = mem["v_parts"][:, :].rearrange("p (r d) -> p r d", r=2)
    w_parts = mem["w_parts"][:, :].rearrange("p (b r t) -> p b r t", b=2, r=2)
    act_buf, low_buf = mem["act_buf"], mem["low_buf"]
    iota = low_buf[:, 0:P]
    wq = arena[:, 0:16384].rearrange("p (g k m) -> p g k m", g=4, k=KC)
    keysT = arena[:, 16384:18432].rearrange("p (r n) -> p r n", r=ROWS)
    qT = arena[:, 18432:22528].rearrange("p (r t) -> p r t", t=SEQ)
    scores = [arena[:, 22528 + 2048 * tb:24576 + 2048 * tb].rearrange("p (r n) -> p r n", r=ROWS)
              for tb in range(TB)]
    rest = arena[:, 26624:28672].rearrange("p (r n) -> p r n", r=ROWS)
    hT = arena[:, 28672:30720]
    xn = arena[:, 30720:32768]
    cand = ring[:, 0:2048].rearrange("p (h c) -> p h c", h=HEADS)
    cand_rest = ring[:, 2048:4096].rearrange("p (h c) -> p h c", h=HEADS)
    eq = ring[:, 4096:6144]
    SM = 6144

    def small(i, n=128):
        return ring[:, SM + 128 * i:SM + 128 * i + n]
    best = small(0, 256).rearrange("p (r k) -> p r k", r=ROWS)
    best_at = small(2, 256).bitcast(U32).rearrange("p (r k) -> p r k", r=ROWS)
    key_of = small(4, 256).rearrange("p (r k) -> p r k", r=ROWS)
    top = small(6).rearrange("p (h k) -> p h k", h=HEADS)
    top_at = small(7).bitcast(U32).rearrange("p (h k) -> p h k", h=HEADS)
    part_at = small(8).bitcast(U32)
    part = small(9)
    total = small(10, HEADS)
    choice = [[arena[:, 30720 + 384 * tb + 128 * n:30720 + 384 * tb + 128 * (n + 1)] for n in range(3)]
              for tb in range(TB)]
    picks = [ring[:, 3072 + 256 * n:3072 + 256 * (n + 1)] for n in range(3)]
    one_hot = [[ring[:, 4096 + 2048 * b + 1024 * n:4096 + 2048 * b + 1024 * (n + 1)]
                .rearrange("p (t e) -> p t e", t=GATE_TOKENS) for n in range(2)] for b in range(2)]
    gates = arena[:, :].rearrange("p (e t) -> p e t", t=SEQ)
    table_u = [ring[:, 1024 * n:1024 * (n + 1)] for n in range(UNROLL)]
    table_v = [ring[:, 4096 + 1024 * n:4096 + 1024 * (n + 1)] for n in range(UNROLL)]
    u_src = a[layer + "_peer_u"]
    v_src = a[layer + "_peer_v"].rearrange("(p e) d -> e p d", p=P)
    gain = act_buf[:, 0:KC]

    def chain(i):
        return i % UNROLL, i // UNROLL

    with nc.Block() as block:
        @block.sync
        def _(sp):
            sp.dma_start(gain, a[layer + "_norm_ffn_g"]).then_inc(s("gain_in"), 16)
            src = a[layer + "_peer_wq"].rearrange("(k p) (g m) -> g p k m", p=P, g=4)
            for g in range(4):
                sp.dma_start(wq[:, g], src[g]).then_inc(s(f"wq_{g}"), 16)
            sp.dma_start(arena[:, 16384:18432], a[layer + "_keys"]).then_inc(s("keys_in"), 16)

        @block.gpsimd
        def _(pool):
            nc.gpsimd.iota(iota, [[1, P]], base=0, channel_multiplier=0,
                           allow_small_or_imprecise_dtypes=True).then_inc(s("iota_made"), 1)

        @block.scalar
        def _(act):
            norm_act(nc, act, mem, s, "n", xn)
            for b in range(4):
                act.wait_ge(s("n_hT"), 4)
                act.activation(h_parts[:, 2 * b:2 * b + 2, 0], hT[:, 512 * b:512 * (b + 1)]
                               .rearrange("p (c t) -> p c t", c=2), ACT.Copy).then_inc(s("h_high"), 1)
            for b in range(8):
                act.wait_ge(s("query"), b + 1)
                nc.scalar.activation(qT[:, 2 * b:2 * b + 2], psum[b % 4][:, :].rearrange("p (r t) -> p r t", r=2),
                                     ACT.Copy).then_inc(s("qT"), 1)
            for tb in range(TB):
                for b in range(4):
                    act.wait_ge(s("scored"), 4 * tb + b + 1)
                    nc.scalar.activation(scores[tb][:, 4 * b:4 * b + 4],
                                         psum[4 * (1 - tb) + b][:, :].rearrange("p (r n) -> p r n", r=4),
                                         ACT.Copy).then_inc(s("scores"), 1)
            for tb in range(TB):
                act.wait_ge(s("top_shifted"), tb + 1)
                nc.scalar.activation(top, top, ACT.Exp).then_inc(s("top_exp"), 1)

        @block.vector
        def _(dve):
            tt, ts = nc.vector.tensor_tensor, nc.vector.tensor_scalar
            link = ordered(dve, s("dve_order"))
            norm_scale(nc, dve, mem, s, "n", xn)
            dve.wait_ge(s("gain_in"), 16)
            norm_gain(nc, dve, mem, s, "n", hT, gain)
            dve.wait_ge(s("n_hT"), 4)
            dve.wait_ge(s("h_high"), 4)
            dve.wait_ge(s("iota_made"), 1)
            for b in range(4):
                h_in = hT[:, 512 * b:512 * (b + 1)].rearrange("p (c t) -> p c t", c=2)
                tt(h_parts[:, 2 * b:2 * b + 2, 1], h_in, h_parts[:, 2 * b:2 * b + 2, 0].bitcast(F32),
                   ALU.subtract).then_inc(s("h_low"), 1)
            for tb in range(TB):
                def best16(n, src, left, val, at):
                    for r in range(n):
                        last = nc.vector.max(val[:, r, 0:8], src[:, r])
                    link(last)
                    for r in range(n):
                        nc.vector.max_index(at[:, r, 0:8], val[:, r, 0:8], src[:, r])
                        last = nc.vector.match_replace(left[:, r], val[:, r, 0:8], src[:, r], LOWEST)
                    link(last)
                    for r in range(n):
                        last = nc.vector.max(val[:, r, 8:16], left[:, r])
                    link(last)
                    for r in range(n):
                        last = nc.vector.max_index(at[:, r, 8:16], val[:, r, 8:16], left[:, r])
                    link(last)
                dve.wait_ge(s("scores"), 4 * tb + 4)
                best16(ROWS, scores[tb], rest, best, best_at)
                link(nc.vector.tensor_copy(key_of, best_at))
                halves = best.rearrange("p (h z) k -> p h z k", z=2)
                link(tt(cand.rearrange("p h (i j) -> p h i j", i=TOPK),
                        halves[:, :, 0].unsqueeze(3).broadcast_to([P, HEADS, TOPK, TOPK]),
                        halves[:, :, 1].unsqueeze(2).broadcast_to([P, HEADS, TOPK, TOPK]), ALU.add))
                best16(HEADS, cand, cand_rest, top, top_at)
                keys = key_of.rearrange("p (h z) k -> p h z k", z=2)
                for z in range(2):
                    if z == 0:
                        link(ts(part_at, small(7).bitcast(U32), 4, None, ALU.logical_shift_right))
                    else:
                        link(ts(part_at, small(7).bitcast(U32), 15, None, ALU.bitwise_and))
                    link(nc.vector.tensor_copy(part, part_at))
                    eq4 = eq.rearrange("p (h k j) -> p h k j", h=HEADS, k=TOPK)
                    link(tt(eq4, part.rearrange("p (h k) -> p h k", h=HEADS).unsqueeze(3)
                            .broadcast_to([P, HEADS, TOPK, TOPK]),
                            iota[:, 0:TOPK].unsqueeze(1).unsqueeze(1).broadcast_to([P, HEADS, TOPK, TOPK]),
                            ALU.is_equal))
                    link(tt(eq4, eq4, keys[:, :, z].unsqueeze(2).broadcast_to([P, HEADS, TOPK, TOPK]), ALU.mult))
                    link(nc.vector.tensor_reduce(choice[tb][z], eq.rearrange("p (n j) -> p n j", j=TOPK),
                                                 AXX, ALU.add))
                link(nc.vector.tensor_copy(total, top[:, :, 0]))
                tt(top, top, total.unsqueeze(2).broadcast_to([P, HEADS, TOPK]), ALU.subtract)\
                    .then_inc(s("top_shifted"), 1)
                dve.wait_ge(s("top_exp"), tb + 1)
                link(nc.vector.tensor_reduce(total, top, AXX, ALU.add))
                link(nc.vector.reciprocal(total, total))
                tt(choice[tb][2].rearrange("p (h k) -> p h k", h=HEADS), top,
                   total.unsqueeze(2).broadcast_to([P, HEADS, TOPK]), ALU.mult).then_inc(s("chosen"), 1)
            dve.wait_ge(s("chosen"), TB)
            dve.wait_ge(s("choice_turned"), 1)
            for n in range(3):
                nc.vector.tensor_copy(picks[n], psum[n // 2][:, (n % 2) * SEQ:(n % 2 + 1) * SEQ])\
                    .then_inc(s("picks"), 1)

        @block.tensor
        def _(pe):
            norm_pe(nc, pe, mem, s, "n", xn)
            pe.wait_ge(s("n_hT"), 4)
            for r in range(ROWS):
                if r % 4 == 0:
                    pe.wait_ge(s(f"wq_{r // 4}"), 16)
                if r % 2 == 0 and r >= 8:
                    pe.wait_ge(s("qT"), r // 2 - 3)
                for k in range(KC):
                    last = nc.tensor.matmul(psum[(r // 2) % 4][:, (r % 2) * SEQ:(r % 2 + 1) * SEQ],
                                            wq[:, r // 4, k, (r % 4) * P:(r % 4 + 1) * P],
                                            hT[:, k * SEQ:(k + 1) * SEQ], start=(k == 0), stop=(k == KC - 1))
                if r % 2:
                    last.then_inc(s("query"), 1)
            pe.wait_ge(s("keys_in"), 16)
            pe.wait_ge(s("qT"), 8)
            for tb in range(TB):
                for r in range(ROWS):
                    last = nc.tensor.matmul(psum[4 * (1 - tb) + r // 4][:, (r % 4) * P:(r % 4 + 1) * P],
                                            qT[:, r, tb * P:(tb + 1) * P], keysT[:, r, :], start=True, stop=True)
                    if r % 4 == 3:
                        last.then_inc(s("scored"), 1)
            pe.wait_ge(s("scores"), 8)
            for tb in range(TB):
                pe.wait_ge(s("chosen"), tb + 1)
                for n in range(3):
                    o = (n % 2) * SEQ + tb * P
                    last = nc.tensor.transpose(psum[n // 2][:, o:o + P], choice[tb][n], ident[:, :])
            last.then_inc(s("choice_turned"), 1)

    TURNS = SEQ // (2 * GATE_TOKENS)
    with nc.Block() as block:
        @block.vector
        def _(dve):
            dve.wait_ge(s("picks"), 3)
            wide = [P, GATE_TOKENS, KEYS]
            with dve.Fori(0, TURNS) as turn:
                for b in range(2):
                    dve.wait_ge(s("gate_banks"), turn * 4 + 2 * b + 2)
                    at = turn * (2 * GATE_TOKENS) + b * GATE_TOKENS
                    idx = [p[:, bass.ds(at, GATE_TOKENS)].unsqueeze(2).broadcast_to(wide) for p in picks]
                    every = iota[:, :].unsqueeze(1).broadcast_to(wide)
                    nc.vector.tensor_tensor(one_hot[b][0], idx[0], every, ALU.is_equal)\
                        .then_inc(s("hot_rows"), 1)
                    nc.vector.tensor_tensor(one_hot[b][1], idx[1], every, ALU.is_equal)\
                        .then_inc(s("hot_ready"), 1)
                    dve.wait_ge(s("hot_rows"), turn * 2 + b + 1)
                    nc.vector.tensor_tensor(one_hot[b][0], one_hot[b][0], idx[2], ALU.mult)\
                        .then_inc(s("hot_ready"), 1)

        @block.tensor
        def _(pe):
            for n in range(4):
                nc.tensor.nop().then_inc(s("gate_banks"), 1)
            with pe.Fori(0, TURNS) as turn:
                for b in range(2):
                    pe.wait_ge(s("hot_ready"), turn * 4 + 2 * b + 2)
                    for t in range(GATE_TOKENS):
                        bank = 2 * b + t // 4
                        if t % 4 == 0:
                            pe.wait_ge(s("gate_copied"), turn * 4 + 2 * b + t // 4 + 1)
                        last = nc.tensor.matmul(psum[bank][:, (t % 4) * P:(t % 4 + 1) * P],
                                                one_hot[b][0][:, t], one_hot[b][1][:, t], start=True, stop=True)
                        if t % 4 == 3:
                            last.then_inc(s("gate_banks"), 1)

        @block.scalar
        def _(act):
            for n in range(4):
                nc.scalar.nop().then_inc(s("gate_copied"), 1)
            with act.Fori(0, TURNS) as turn:
                for n in range(4):
                    act.wait_ge(s("gate_banks"), turn * 4 + n + 5)
                    nc.scalar.activation(gates[:, :, bass.ds(turn * (2 * GATE_TOKENS) + 4 * n, 4)],
                                         psum[n][:, :].rearrange("p (t e) -> p e t", t=4), ACT.Copy)\
                        .then_inc(s("gate_copied"), 1)

    with nc.Block() as block:
        @block.sync
        def _(sp):
            def fetch(slot, row, used):
                if used is not None:
                    sp.wait_ge(s("u_split"), used * 2 + 2)
                sp.dma_start(table_u[slot], u_src[row]).then_inc(s(f"u_in_{slot}"), 16)
                if used is not None:
                    sp.wait_ge(s("v_split"), used * 2 + 2)
                sp.dma_start(table_v[slot], v_src[row]).then_inc(s(f"v_in_{slot}"), 16)
            for n in range(UNROLL):
                fetch(n, n, None)
            with sp.Fori(1, SLICES // UNROLL) as turn:
                for n in range(UNROLL):
                    fetch(n, turn * UNROLL + n, (turn - 1) * UNROLL + n)

        def run(eng, step):
            for n in range(UNROLL):
                step(n, 0, n)
            with eng.Fori(1, SLICES // UNROLL - 1) as turn:
                for n in range(UNROLL):
                    step(turn * UNROLL + n, turn, n)
            last = SLICES // UNROLL - 1
            for n in range(UNROLL):
                step(last * UNROLL + n, last, n)

        @block.scalar
        def _(act):
            def v_high(i, turn, n, first):
                act.wait_ge(s(f"v_in_{n}"), turn * 16 + 16)
                for hf in range(2):
                    if not first:
                        act.wait_ge(s("v_used"), i * 2 - 1 + hf)
                    nc.scalar.activation(v_parts[:, 0, 512 * hf:512 * (hf + 1)],
                                         table_v[n][:, 512 * hf:512 * (hf + 1)], ACT.Copy)\
                        .then_inc(s("v_high"), 1)

            def u_high(i, turn, n, first):
                act.wait_ge(s(f"u_in_{n}"), turn * 16 + 16)
                for hf in range(2):
                    if not first:
                        act.wait_ge(s("u_used"), i * 2 - 1 + hf)
                    nc.scalar.activation(u_parts[:, 0, 4 * hf:4 * (hf + 1)],
                                         table_u[n][:, 512 * hf:512 * (hf + 1)]
                                         .rearrange("p (c e) -> p c e", c=4), ACT.Copy)\
                        .then_inc(s("u_high"), 1)

            def pre_low(i, n):
                if not (isinstance(i, int) and i == 0):
                    act.wait_ge(s("pre_sum"), i)
                act.wait_ge(s("u_used"), i * 2 + 2)
                nc.scalar.activation(low_buf[:, :], psum[4 + n % 2][:, SEQ:],
                                     ACT.Copy).then_inc(s("pre_low"), 1)

            def gelu(i, n):
                act.wait_ge(s("pre_sum"), i + 1)
                nc.scalar.activation(act_buf[:, (n % 2) * SEQ:(n % 2 + 1) * SEQ],
                                     act_buf[:, (n % 2) * SEQ:(n % 2 + 1) * SEQ],
                                     ACT.Gelu_apprx_tanh).then_inc(s("gelu"), 1)

            def step(i, turn, n):
                is_last = isinstance(i, int) and i == SLICES - 1
                if not is_last:
                    u_high(i + 1, turn if n < UNROLL - 1 else turn + 1, (n + 1) % UNROLL, False)
                pre_low(i, n)
                gelu(i, n)
                v_high(i, turn, n, isinstance(i, int) and i == 0)
            u_high(0, 0, 0, True)
            run(act, step)

        @block.vector
        def _(dve):
            tt = nc.vector.tensor_tensor

            def v_low(i, n):
                for hf in range(2):
                    dve.wait_ge(s("v_high"), i * 2 + hf + 1)
                    cut = slice(512 * hf, 512 * (hf + 1))
                    tt(v_parts[:, 1, cut], table_v[n][:, cut], v_parts[:, 0, cut].bitcast(F32),
                       ALU.subtract).then_inc(s("v_split"), 1)

            def u_low(i, hf, n):
                dve.wait_ge(s("u_high"), i * 2 + hf + 1)
                cut = slice(4 * hf, 4 * (hf + 1))
                tt(u_parts[:, 1, cut], table_u[n][:, 512 * hf:512 * (hf + 1)]
                   .rearrange("p (c e) -> p c e", c=4), u_parts[:, 0, cut].bitcast(F32),
                   ALU.subtract).then_inc(s("u_split"), 1)

            def weigh(i, n):
                buf = act_buf[:, (n % 2) * SEQ:(n % 2 + 1) * SEQ]
                dve.wait_ge(s("gelu"), i + 1)
                tt(buf, buf, arena[:, bass.ds(i * SEQ, SEQ)], ALU.mult).then_inc(s("weighed"), 1)
                dve.wait_ge(s("weighed"), i + 1)
                nc.vector.tensor_copy(w_parts[:, n % 2, 0], buf).then_inc(s("weight_high"), 1)
                dve.wait_ge(s("weight_high"), i + 1)
                tt(w_parts[:, n % 2, 1], buf, w_parts[:, n % 2, 0].bitcast(F32), ALU.subtract)\
                    .then_inc(s("weight"), 1)

            def pre_sum(i, n):
                dve.wait_ge(s("pre_low"), i + 1)
                buf = act_buf[:, (n % 2) * SEQ:(n % 2 + 1) * SEQ]
                tt(buf, psum[4 + n % 2][:, 0:SEQ], low_buf[:, :], ALU.add)\
                    .then_inc(s("pre_sum"), 1)

            def step(i, turn, n):
                if isinstance(i, int) and i == SLICES - 1:
                    pre_sum(i, n)
                else:
                    u_low(i + 1, 0, (n + 1) % UNROLL)
                    pre_sum(i, n)
                    u_low(i + 1, 1, (n + 1) % UNROLL)
                weigh(i, n)
                v_low(i, n)
            u_low(0, 0, 0)
            u_low(0, 1, 0)
            run(dve, step)
            dve.wait_ge(s("weight"), SLICES)
            for n in range(4):
                dve.wait_ge(s("v_used"), 2 * SLICES)
                xs = x[:, n * 512:(n + 1) * 512]
                tt(xs, xs, psum[n][:, :], ALU.add).then_inc(s("x_after"), 1)
            dve.wait_ge(s("x_after"), 4)

        @block.tensor
        def _(pe):
            def pre(i, n, first):
                if not first:
                    pe.wait_ge(s("pre_sum"), i - 1)
                bank = psum[4 + n % 2]
                for hf in range(2):
                    pe.wait_ge(s("u_split"), i * 2 + hf + 1)
                    for c in range(4 * hf, 4 * hf + 4):
                        nc.tensor.matmul(bank[:, :], u_parts[:, 0, c], h_parts[:, c].rearrange("p r t -> p (r t)"),
                                         start=(c == 0), stop=False)
                        last = nc.tensor.matmul(bank[:, 0:SEQ], u_parts[:, 1, c], h_parts[:, c, 0],
                                                start=False, stop=(c == KC - 1))
                    last.then_inc(s("u_used"), 1)

            def combine(i, n, first, final):
                pe.wait_ge(s("weight"), i + 1)
                for hf in range(2):
                    pe.wait_ge(s("v_split"), i * 2 + hf + 1)
                    for tb in range(TB):
                        w = [w_parts[:, n % 2, r, tb * P:(tb + 1) * P] for r in range(2)]
                        v = [v_parts[:, r, 512 * hf:512 * (hf + 1)] for r in range(2)]
                        o = psum[2 * tb + hf][:, :]
                        nc.tensor.matmul(o, w[0], v[0], start=first, stop=False)
                        nc.tensor.matmul(o, w[0], v[1], start=False, stop=False)
                        last = nc.tensor.matmul(o, w[1], v[0], start=False, stop=final)
                    last.then_inc(s("v_used"), 1)

            def step(i, turn, n):
                at_start = isinstance(i, int) and i < UNROLL
                pre(i, n, at_start and i < 2)
                if not (at_start and i == 0):
                    combine(i - 1, (n - 1) % UNROLL, at_start and i == 1, False)
            run(pe, step)
            combine(SLICES - 1, UNROLL - 1, False, True)


def final_norm(nc, a, mem, s, out):
    arena, x, stat = mem["arena"], mem["x"], mem["stat"]
    xn = arena[:, 0:2048]
    gain = arena[:, 2048:3072]
    with nc.Block() as block:
        @block.scalar
        def _(act):
            norm_act(nc, act, mem, s, "nf", xn)

        @block.vector
        def _(dve):
            norm_scale(nc, dve, mem, s, "nf", xn)
            dve.wait_ge(s("gainf_in"), 16)
            for tb in range(TB):
                xs = xn[:, tb * D:(tb + 1) * D]
                dve.wait_ge(s("nf_xn"), tb + 1)
                nc.vector.tensor_tensor(xs, xs, gain, ALU.mult).then_inc(s("y"), 1)

        @block.sync
        def _(sp):
            sp.dma_start(gain, a["final_norm_g"].partition_broadcast(P)).then_inc(s("gainf_in"), 16)
            dst = out.rearrange("(b p) d -> b p d", p=P)
            for tb in range(TB):
                sp.wait_ge(s("y"), tb + 1)
                sp.dma_start(dst[tb], xn[:, tb * D:(tb + 1) * D]).then_inc(s("y_out"), 16)
            sp.wait_ge(s("y_out"), 16 * TB)



def _layout(np, i):
    f = {k: np.asarray(v) for k, v in i.items()}
    d = {"x": f["x"].reshape(SEQ, D)}
    for k in ("l0_w_in", "l0_w_out", "l1_w_in", "l1_w_out", "l0_peer_wq", "l1_peer_wq", "l0_peer_v",
              "l1_peer_v", "a_glu_w", "final_norm_g", "c_vnorm_g"):
        d[k] = f[k]
    for k in ("l0_norm_mix_g", "l0_norm_ffn_g", "l1_norm_mix_g", "l1_norm_ffn_g"):
        d[k] = f[k].reshape(KC, P).T

    def states(m):
        return m.reshape(S5_TILES, P).T
    d["s5_params"] = np.concatenate([states(f["a_lam_re"]), states(f["a_lam_im"]),
                                     states(np.repeat(f["a_log_dt"], 64).reshape(32, 64))], 1)
    b = np.zeros((2, 8, 16, WC, 2, 64), np.float32)
    c = np.zeros((2, 2, 64, S5_TILES, 2, 16), np.float32)
    for r, (bb, cc) in enumerate(((f["a_b_re"], f["a_c_re"]), (f["a_b_im"], f["a_c_im"]))):
        for g in range(32):
            b[r, g % 8, :, g // 8, g % 2, :] = bb[g].T
            c[r, g % 2, :, g // 2, g % 2, :] = cc[g].T
    d["s5_b"] = b.reshape(2, P, 512).transpose(1, 0, 2).reshape(P, 1024)
    d["s5_c"] = c.reshape(2, P, 512).transpose(1, 0, 2).reshape(P, 1024)
    d["conv_w"] = f["b_conv_w"].reshape(3, WC, P).transpose(2, 0, 1).reshape(P, 12)
    d["d_and_glu_b"] = np.concatenate([f["a_d"].reshape(WC, P).T, f["a_glu_b"].reshape(WC, P).T], 1)
    d["c_ws"] = f["c_ws"].transpose(2, 0, 1)
    d["c_bs"] = f["c_bs"].T
    for n in ("l0", "l1"):
        keys = np.stack([f[n + "_peer_k1"], f[n + "_peer_k2"]], 1).reshape(ROWS, KEYS, P)
        d[n + "_keys"] = keys.transpose(2, 0, 1).reshape(P, ROWS * KEYS)
        u = f[n + "_peer_u"].reshape(KEYS, SLICES, KC, P)
        d[n + "_peer_u"] = u.transpose(1, 3, 2, 0).reshape(SLICES, P, KC * KEYS)
    return {k: np.ascontiguousarray(v) for k, v in d.items()}


def kernel(**inputs):
    import numpy as _np
    import concourse.bacc as _bacc
    from concourse import mybir as _mybir
    from concourse.bass_utils import run_bass_kernel_spmd as _run

    nc = _bacc.Bacc("TRN2", target_bir_lowering=False, num_devices=1)
    arrays, aps = {}, {}
    for name, v in _layout(_np, inputs).items():
        arrays[f"in_{name}"] = v
        aps[name] = nc.dram_tensor(f"in_{name}", v.shape, _mybir.dt.from_np(v.dtype), kind="ExternalInput").ap()
    out = nc.dram_tensor("out_0", (SEQ, D), F32, kind="ExternalOutput").ap()
    trunk(nc, aps, out)
    r = _run(nc, [arrays], core_ids=[0])
    return r.results[0]["out_0"].reshape(1, SEQ, D)
```

```python
import concourse.bass as bass
from concourse import mybir
from contextlib import ExitStack

F32 = mybir.dt.float32
F32R = mybir.dt.float32r
U32 = mybir.dt.uint32
ALU = mybir.AluOpType
ACT = mybir.ActivationFunctionType
AXX = mybir.AxisListType.X

P = 128
SEQ = 256
TB = SEQ // P
D = 1024
KC = D // P
GROUP = 512
EVEN_IN = 2048
ODD_IN = 2560
WIDTH = 512
WC = WIDTH // P
S5_TILES = 2048 // P
HEADS = 8
ROWS = 2 * HEADS
KEYS = 128
TOPK = 16
CAND = TOPK * TOPK
PICKS = HEADS * TOPK
SLICES = 128
UNROLL = 4
GATE_TOKENS = 4
EARLY = 40
EPS = 1e-6
LOWEST = -3.0e38
TWO_PI = 6.283185307179586
TP1 = 6.28125
TP2 = 0.0019340515136718750
TP3 = TWO_PI - TP1 - TP2
ROUND = 12582912.0
PI_IN = 3.1415925


def trunk(nc, a, out):
    ctx = ExitStack()
    with ctx:
        def sb(name, shape, dt=F32):
            return ctx.enter_context(nc.sbuf_tensor(name, shape, dt))

        arena = sb("arena", [P, 32768])
        ring = sb("ring", [P, 8192])
        x = sb("x_res", [P, TB * D])
        h_parts = sb("h_parts", [P, KC * 2 * SEQ], F32R)
        u_parts = sb("u_parts", [P, 2 * D], F32R)
        v_parts = sb("v_parts", [P, 2 * D], F32R)
        w_parts = sb("w_parts", [P, 2 * 2 * SEQ], F32R)
        act_buf = sb("act_buf", [P, 2 * SEQ])
        low_buf = sb("low_buf", [P, SEQ])
        ident = sb("ident", [P, P])
        stat = sb("stat", [P, 64])
        psum = [ctx.enter_context(nc.psum_tensor(f"bank{i}", [P, 512], F32)) for i in range(8)]

        mem = dict(arena=arena, ring=ring, x=x, h_parts=h_parts, u_parts=u_parts, v_parts=v_parts,
                   w_parts=w_parts, act_buf=act_buf, low_buf=low_buf, ident=ident, stat=stat, psum=psum)
        made = {}

        def sem(name):
            if name not in made:
                made[name] = nc.alloc_semaphore(name)
            return made[name]

        def phase_over():
            nc.clear_and_free_semaphores(list(made.values()))
            nc.all_engine_barrier()
            made.clear()

        even_mixer(nc, a, mem, sem)
        phase_over()
        peer(nc, a, mem, sem, "l0")
        phase_over()
        odd_mixer(nc, a, mem, sem)
        phase_over()
        peer(nc, a, mem, sem, "l1")
        phase_over()
        final_norm(nc, a, mem, sem, out)


def ordered(eng, sem):
    count = [0]

    def link(ins):
        count[0] += 1
        ins.then_inc(sem, 1)
        eng.wait_ge(sem, count[0])
    return link



def norm_act(nc, act, mem, s, n, xn):
    for tb in range(TB):
        nc.scalar.activation(xn[:, tb * D:(tb + 1) * D], mem["x"][:, tb * D:(tb + 1) * D], ACT.Square,
                             accum_out=mem["stat"][:, tb:tb + 1]).then_inc(s(n + "_squares"), 1)
    act.wait_ge(s(n + "_meansq"), 1)
    nc.scalar.activation(mem["stat"][:, 4:6], mem["stat"][:, 2:4], ACT.Sqrt).then_inc(s(n + "_rms"), 1)


def norm_scale(nc, dve, mem, s, n, xn):
    stat = mem["stat"]
    dve.wait_ge(s(n + "_squares"), TB)
    nc.vector.tensor_scalar(stat[:, 2:4], stat[:, 0:2], 1.0 / D, EPS, ALU.mult, ALU.add)\
        .then_inc(s(n + "_meansq"), 1)
    dve.wait_ge(s(n + "_rms"), 1)
    nc.vector.reciprocal(stat[:, 6:8], stat[:, 4:6]).then_inc(s(n + "_rstd"), 1)
    dve.wait_ge(s(n + "_rstd"), 1)
    for tb in range(TB):
        nc.vector.tensor_scalar(xn[:, tb * D:(tb + 1) * D], mem["x"][:, tb * D:(tb + 1) * D],
                                stat[:, 6 + tb:7 + tb], None, ALU.mult).then_inc(s(n + "_xn"), 1)


def norm_pe(nc, pe, mem, s, n, xn):
    for tb in range(TB):
        pe.wait_ge(s(n + "_xn"), tb + 1)
        for c in range(KC):
            o = (c % 2) * SEQ + tb * P
            last = nc.tensor.transpose(mem["psum"][c // 2][:, o:o + P],
                                       xn[:, tb * D + c * P:tb * D + (c + 1) * P], mem["ident"][:, :])
    last.then_inc(s(n + "_turned"), 1)


def norm_gain(nc, dve, mem, s, n, hT, gain):
    dve.wait_ge(s(n + "_turned"), 1)
    for b in range(4):
        nc.vector.tensor_tensor(
            hT[:, 2 * b * SEQ:2 * (b + 1) * SEQ].rearrange("p (c t) -> p c t", c=2),
            mem["psum"][b][:, :].rearrange("p (c t) -> p c t", c=2),
            gain[:, 2 * b:2 * b + 2].unsqueeze(2).broadcast_to([P, 2, SEQ]), ALU.mult)\
            .then_inc(s(n + "_hT"), 1)



def even_mixer(nc, a, mem, s):
    arena, ring, x, psum, ident = mem["arena"], mem["ring"], mem["x"], mem["psum"], mem["ident"]
    w_in = arena[:, 0:16384].rearrange("p (g k m) -> p g k m", g=4, k=KC)
    pT = arena[:, 16384:20480].rearrange("p (m t) -> p m t", t=SEQ)
    e_cos = arena[:, 20480:24576].rearrange("p (i t) -> p i t", t=SEQ)
    e_sin = arena[:, 24576:28672].rearrange("p (i t) -> p i t", t=SEQ)
    hT = arena[:, 28672:30720]
    xn = arena[:, 30720:32768]
    w_out = arena[:, 0:8192].rearrange("p (k m) -> p k m", k=KC)
    scratch = arena[:, 8192:16384]
    catT = hT.rearrange("p (m t) -> p m t", t=SEQ)
    b_re = ring[:, 0:512].rearrange("p (c n) -> p c n", c=WC)
    b_im = ring[:, 512:1024].rearrange("p (c n) -> p c n", c=WC)
    c_re = ring[:, 1024:1536].rearrange("p (i n) -> p i n", i=S5_TILES)
    c_im = ring[:, 1536:2048].rearrange("p (i n) -> p i n", i=S5_TILES)
    glu_w = ring[:, 2048:4096].rearrange("p (k m) -> p k m", k=WC)
    t1 = ring[:, 4096:6144]
    t2 = ring[:, 6144:8192]
    small = mem["act_buf"]

    def col(i, n=S5_TILES):
        return small[:, 16 * i:16 * i + n]
    (lam_re, lam_im, dt, lrdt, mag, th, rev, turn, rem, sin, half, cos, a_im, den, nr, f_re, f_im,
     tmp1, tmp2, pw_cos, pw_sin, pw_cos2, pw_sin2) = (col(i) for i in range(23))
    gain = col(23, KC)
    conv_w = small[:, 384:396].rearrange("p (k c) -> p k c", k=3)
    d_skip = small[:, 400:404]
    glu_b = small[:, 404:408]

    with nc.Block() as block:
        @block.sync
        def _(sp):
            sp.dma_start(x[:, :].rearrange("p (b d) -> p b d", b=TB),
                         a["x"].rearrange("(b p) d -> p b d", p=P)).then_inc(s("x_in"), 16)
            sp.dma_start(small[:, 0:48], a["s5_params"]).then_inc(s("s5_params_in"), 16)
            sp.dma_start(gain, a["l0_norm_mix_g"]).then_inc(s("gain0_in"), 16)
            src = a["l0_w_in"].rearrange("(k p) (g m) -> g p k m", p=P, g=4)
            for g in range(4):
                sp.dma_start(w_in[:, g], src[g]).then_inc(s(f"w_in0_{g}"), 16)
            sp.dma_start(ring[:, 0:1024], a["s5_b"]).then_inc(s("s5_b_in"), 16)
            sp.dma_start(ring[:, 1024:2048], a["s5_c"]).then_inc(s("s5_c_in"), 16)
            sp.dma_start(small[:, 384:396], a["conv_w"]).then_inc(s("conv_w_in"), 16)
            sp.dma_start(small[:, 400:408], a["d_and_glu_b"]).then_inc(s("d_in"), 16)
            sp.dma_start(glu_w, a["a_glu_w"].rearrange("(k p) m -> p k m", p=P)).then_inc(s("glu_w_in"), 16)
            sp.wait_ge(s("proj0"), 8)
            sp.dma_start(w_out, a["l0_w_out"].rearrange("(k p) m -> p k m", p=P)).then_inc(s("w_out0_in"), 16)

        @block.gpsimd
        def _(pool):
            nc.gpsimd.memset(ident[:, :], 0.0).then_inc(s("ident_zero"), 1)
            pool.wait_ge(s("ident_zero"), 1)
            nc.gpsimd.affine_select(out=ident[:, :], in_=ident[:, :], compare_op=ALU.not_equal, fill=1.0,
                                    base=0, pattern=[[-1, P]], channel_multiplier=1)\
                .then_inc(s("ident_made"), 1)
            pool.wait_ge(s("e_tables"), 1)
            for i in range(S5_TILES):
                g, o1, o2, h = (scratch[:, (i % 2) * 4096 + 512 * n:(i % 2) * 4096 + 512 * (n + 1)]
                                for n in (3, 4, 5, 6))
                pool.wait_ge(s("s5_scanned"), 2 * i + 2)
                nc.gpsimd.tensor_tensor(o1.rearrange("p (r t) -> p r t", r=2),
                                        g.rearrange("p (r t) -> p r t", r=2),
                                        e_cos[:, i].unsqueeze(1).broadcast_to([P, 2, SEQ]), ALU.mult)\
                    .then_inc(s("s5_turned"), 1)
                nc.gpsimd.tensor_tensor(o2.rearrange("p (r t) -> p r t", r=2),
                                        g.rearrange("p (r t) -> p r t", r=2),
                                        e_sin[:, i].unsqueeze(1).broadcast_to([P, 2, SEQ]), ALU.mult)\
                    .then_inc(s("s5_turned"), 1)
                pool.wait_ge(s("s5_turned"), 2 * i + 2)
                if i >= 2:
                    pool.wait_ge(s("s5_y"), i - 1)
                nc.gpsimd.tensor_tensor(h[:, 0:SEQ], o1[:, 0:SEQ], o2[:, SEQ:2 * SEQ], ALU.subtract)\
                    .then_inc(s("s5_h"), 1)
                nc.gpsimd.tensor_tensor(h[:, SEQ:2 * SEQ], o1[:, SEQ:2 * SEQ], o2[:, 0:SEQ], ALU.add)\
                    .then_inc(s("s5_h"), 1)

        @block.scalar
        def _(act):
            act.wait_ge(s("x_in"), 16)
            norm_act(nc, act, mem, s, "n0", xn)
            act.wait_ge(s("s5_params_in"), 16)
            nc.scalar.activation(dt, dt, ACT.Exp).then_inc(s("s5_dt"), 1)
            act.wait_ge(s("s5_angles"), 1)
            nc.scalar.activation(mag, lrdt, ACT.Exp).then_inc(s("s5_mag"), 1)
            nc.scalar.activation(sin, rem, ACT.Sin).then_inc(s("s5_sin"), 1)
            nc.scalar.activation(half, rem, ACT.Sin, scale=0.5).then_inc(s("s5_sin"), 1)
            for b in range(8):
                act.wait_ge(s("proj0"), b + 1)
                nc.scalar.activation(pT[:, 2 * b:2 * b + 2], psum[b][:, :].rearrange("p (m t) -> p m t", m=2),
                                     ACT.Copy).then_inc(s("pT"), 1)
            for c in range(WC):
                act.wait_ge(s("s5_skip"), c + 1)
                nc.scalar.activation(pT[:, c], pT[:, c], ACT.Gelu_apprx_tanh).then_inc(s("s5_gelu"), 1)
            for c in range(WC):
                act.wait_ge(s("glu"), c + 1)
                nc.scalar.activation(scratch[:, c * SEQ:(c + 1) * SEQ], psum[c][:, 0:SEQ], ACT.Sigmoid,
                                     bias=glu_b[:, c:c + 1]).then_inc(s("glu_sig"), 1)

        @block.vector
        def _(dve):
            link = ordered(dve, s("even_dve_order"))
            tt, ts = nc.vector.tensor_tensor, nc.vector.tensor_scalar
            dve.wait_ge(s("x_in"), 16)
            norm_scale(nc, dve, mem, s, "n0", xn)
            dve.wait_ge(s("s5_dt"), 1)
            link(tt(lrdt, lam_re, dt, ALU.mult))
            link(tt(th, lam_im, dt, ALU.mult))
            link(ts(rev, th, 1.0 / TWO_PI, ROUND, ALU.mult, ALU.add))
            link(ts(turn, rev, -ROUND, None, ALU.add))
            link(nc.vector.scalar_tensor_tensor(rem, turn, -TP1, th, ALU.mult, ALU.add))
            link(nc.vector.scalar_tensor_tensor(rem, turn, -TP2, rem, ALU.mult, ALU.add))
            link(nc.vector.scalar_tensor_tensor(rem, turn, -TP3, rem, ALU.mult, ALU.add))
            ts(rem, rem, PI_IN, -PI_IN, ALU.min, ALU.max).then_inc(s("s5_angles"), 1)
            norm_needs_gain = s("gain0_in")
            dve.wait_ge(norm_needs_gain, 16)
            norm_gain(nc, dve, mem, s, "n0", hT, gain)
            dve.wait_ge(s("s5_mag"), 1)
            dve.wait_ge(s("s5_sin"), 2)
            link(tt(cos, half, half, ALU.mult))
            link(ts(cos, cos, -2.0, 1.0, ALU.mult, ALU.add))
            link(tt(nr, mag, cos, ALU.mult))
            link(ts(nr, nr, -1.0, None, ALU.add))
            link(tt(a_im, mag, sin, ALU.mult))
            link(tt(tmp1, lam_re, lam_re, ALU.mult))
            link(tt(tmp2, lam_im, lam_im, ALU.mult))
            link(tt(den, tmp1, tmp2, ALU.add))
            link(nc.vector.reciprocal(den, den))
            link(tt(tmp1, nr, lam_re, ALU.mult))
            link(tt(tmp2, a_im, lam_im, ALU.mult))
            link(tt(tmp1, tmp1, tmp2, ALU.add))
            link(tt(f_re, tmp1, den, ALU.mult))
            link(tt(tmp1, a_im, lam_re, ALU.mult))
            link(tt(tmp2, nr, lam_im, ALU.mult))
            link(tt(tmp1, tmp1, tmp2, ALU.subtract))
            link(tt(f_im, tmp1, den, ALU.mult))
            nc.vector.memset(e_cos[:, :, 0:1], 1.0)
            link(nc.vector.memset(e_sin[:, :, 0:1], 0.0))
            link(nc.vector.tensor_copy(pw_cos, cos))
            link(nc.vector.tensor_copy(pw_sin, sin))
            n = 1
            while n < SEQ:
                pc = pw_cos.unsqueeze(2).broadcast_to([P, S5_TILES, n])
                ps = pw_sin.unsqueeze(2).broadcast_to([P, S5_TILES, n])
                u1 = t1[:, 0:S5_TILES * n].rearrange("p (i t) -> p i t", i=S5_TILES)
                u2 = t2[:, 0:S5_TILES * n].rearrange("p (i t) -> p i t", i=S5_TILES)
                tt(u1, e_cos[:, :, 0:n], pc, ALU.mult)
                link(tt(u2, e_sin[:, :, 0:n], ps, ALU.mult))
                link(tt(e_cos[:, :, n:2 * n], u1, u2, ALU.subtract))
                tt(u1, e_cos[:, :, 0:n], ps, ALU.mult)
                link(tt(u2, e_sin[:, :, 0:n], pc, ALU.mult))
                link(tt(e_sin[:, :, n:2 * n], u1, u2, ALU.add))
                n *= 2
                if n < SEQ:
                    tt(pw_cos2, pw_cos, pw_cos, ALU.mult)
                    tt(tmp1, pw_sin, pw_sin, ALU.mult)
                    link(tt(pw_sin2, pw_cos, pw_sin, ALU.mult))
                    tt(pw_cos, pw_cos2, tmp1, ALU.subtract)
                    link(ts(pw_sin, pw_sin2, 2.0, None, ALU.mult))
            dve.wait_ge(s("s5_c_in"), 16)
            fr = f_re.unsqueeze(2).broadcast_to([P, S5_TILES, 32])
            fi = f_im.unsqueeze(2).broadcast_to([P, S5_TILES, 32])
            q1, q2, q3, q4 = (t1[:, 512 * n:512 * (n + 1)].rearrange("p (i n) -> p i n", i=S5_TILES)
                              for n in range(4))
            tt(q1, c_re, fr, ALU.mult)
            tt(q2, c_im, fi, ALU.mult)
            tt(q3, c_re, fi, ALU.mult)
            link(tt(q4, c_im, fr, ALU.mult))
            link(tt(c_re, q1, q2, ALU.subtract))
            link(tt(q3, q3, q4, ALU.add))
            ts(c_im, q3, -1.0, None, ALU.mult).then_inc(s("s5_c_scaled"), 1)
            link(nc.vector.tensor_copy(tmp1, tmp2))
            nc.vector.tensor_copy(tmp1, tmp2).then_inc(s("e_tables"), 1)
            dve.wait_ge(s("proj0"), 8)
            for i in range(S5_TILES):
                m1, m2, pq, g = (scratch[:, (i % 2) * 4096 + 512 * n:(i % 2) * 4096 + 512 * (n + 1)]
                                 for n in range(4))
                dve.wait_ge(s("s5_bu"), i + 1)
                bu = psum[i % 2][:, :].rearrange("p (r t) -> p r t", r=2)
                tt(m1.rearrange("p (r t) -> p r t", r=2), bu,
                   e_cos[:, i].unsqueeze(1).broadcast_to([P, 2, SEQ]), ALU.mult).then_inc(s("s5_bu_used"), 1)
                tt(m2.rearrange("p (r t) -> p r t", r=2), bu,
                   e_sin[:, i].unsqueeze(1).broadcast_to([P, 2, SEQ]), ALU.mult).then_inc(s("s5_bu_used"), 1)
                dve.wait_ge(s("s5_bu_used"), 2 * i + 2)
                tt(pq[:, 0:SEQ], m1[:, 0:SEQ], m2[:, SEQ:], ALU.add)
                link(tt(pq[:, SEQ:], m1[:, SEQ:], m2[:, 0:SEQ], ALU.subtract))
                if i >= 2:
                    dve.wait_ge(s("s5_turned"), 2 * (i - 1))
                decay = mag[:, i:i + 1].broadcast_to([P, SEQ])
                for r in range(2):
                    nc.vector.tensor_tensor_scan(g[:, r * SEQ:(r + 1) * SEQ], decay,
                                                 pq[:, r * SEQ:(r + 1) * SEQ], 0.0, ALU.mult, ALU.add)\
                        .then_inc(s("s5_scanned"), 1)
                if i % 4 == 3:
                    c = i // 4
                    if c == 0:
                        dve.wait_ge(s("pT"), 8)
                        dve.wait_ge(s("conv_w_in"), 16)
                    z, acc = t1[:, 0:SEQ], t1[:, SEQ:2 * SEQ]
                    link(tt(z, pT[:, 8 + c], pT[:, 12 + c], ALU.mult))
                    link(ts(acc, z, conv_w[:, 2, c:c + 1], None, ALU.mult))
                    link(nc.vector.scalar_tensor_tensor(acc[:, 1:], z[:, 0:SEQ - 1], conv_w[:, 1, c:c + 1],
                                                        acc[:, 1:], ALU.mult, ALU.add))
                    link(nc.vector.scalar_tensor_tensor(acc[:, 2:], z[:, 0:SEQ - 2], conv_w[:, 0, c:c + 1],
                                                        acc[:, 2:], ALU.mult, ALU.add))
                    link(tt(catT[:, WC + c], acc, pT[:, 4 + c], ALU.mult))
            dve.wait_ge(s("d_in"), 16)
            for c in range(WC):
                dve.wait_ge(s("s5_y"), 4 * c + 4)
                nc.vector.scalar_tensor_tensor(pT[:, c], pT[:, c], d_skip[:, c:c + 1], psum[4 + c][:, 0:SEQ],
                                               ALU.mult, ALU.add).then_inc(s("s5_skip"), 1)
            for c in range(WC):
                dve.wait_ge(s("glu_sig"), c + 1)
                dve.wait_ge(s("s5_gelu"), WC)
                tt(catT[:, c], pT[:, c], scratch[:, c * SEQ:(c + 1) * SEQ], ALU.mult)\
                    .then_inc(s("catT0"), 1)
            for n in range(4):
                dve.wait_ge(s("mixed0"), n + 1)
                xs = x[:, n * 512:(n + 1) * 512]
                tt(xs, xs, psum[4 + n][:, :], ALU.add).then_inc(s("x_after_mix0"), 1)
            dve.wait_ge(s("x_after_mix0"), 4)

        @block.tensor
        def _(pe):
            pe.wait_ge(s("ident_made"), 1)
            norm_pe(nc, pe, mem, s, "n0", xn)
            pe.wait_ge(s("n0_hT"), 4)
            for m in range(16):
                if m % 4 == 0:
                    pe.wait_ge(s(f"w_in0_{m // 4}"), 16)
                for k in range(KC):
                    last = nc.tensor.matmul(psum[m // 2][:, (m % 2) * SEQ:(m % 2 + 1) * SEQ],
                                            w_in[:, m // 4, k, (m % 4) * P:(m % 4 + 1) * P],
                                            hT[:, k * SEQ:(k + 1) * SEQ], start=(k == 0), stop=(k == KC - 1))
                if m % 2:
                    last.then_inc(s("proj0"), 1)
            pe.wait_ge(s("s5_b_in"), 16)
            pe.wait_ge(s("pT"), 8)
            pe.wait_ge(s("s5_c_scaled"), 1)

            def product_in(i):
                c, j = i // 4, i % 4
                if i >= 2:
                    pe.wait_ge(s("s5_bu_used"), 2 * (i - 1))
                for r, b in enumerate((b_re, b_im)):
                    last = nc.tensor.matmul(psum[i % 2][:, r * SEQ:(r + 1) * SEQ], b[32 * j:32 * j + 32, c, :],
                                            pT[32 * j:32 * j + 32, c, :], start=True, stop=True)
                last.then_inc(s("s5_bu"), 1)

            def product_out(i):
                c, j = i // 4, i % 4
                pe.wait_ge(s("s5_h"), 2 * i + 2)
                h = scratch[:, (i % 2) * 4096 + 3072:(i % 2) * 4096 + 3584]
                for r, cm in enumerate((c_re, c_im)):
                    last = nc.tensor.matmul(psum[4 + c][32 * j:32 * j + 32, 0:SEQ], cm[:, i, :],
                                            h[:, r * SEQ:(r + 1) * SEQ], start=(r == 0), stop=(r == 1))
                last.then_inc(s("s5_y"), 1)

            for i in range(S5_TILES + 2):
                if i < S5_TILES:
                    product_in(i)
                if i >= 2:
                    product_out(i - 2)
            pe.wait_ge(s("glu_w_in"), 16)
            pe.wait_ge(s("s5_gelu"), WC)
            for m in range(WC):
                for k in range(WC):
                    last = nc.tensor.matmul(psum[m][:, 0:SEQ], glu_w[:, k, m * P:(m + 1) * P], pT[:, k, :],
                                            start=(k == 0), stop=(k == WC - 1))
                last.then_inc(s("glu"), 1)
            pe.wait_ge(s("w_out0_in"), 16)
            pe.wait_ge(s("catT0"), WC)
            for n in range(4):
                tb, half = n // 2, n % 2
                for k in range(KC):
                    last = nc.tensor.matmul(psum[4 + n][:, :], catT[:, k, tb * P:(tb + 1) * P],
                                            w_out[:, k, half * 512:(half + 1) * 512],
                                            start=(k == 0), stop=(k == KC - 1))
                last.then_inc(s("mixed0"), 1)



def odd_mixer(nc, a, mem, s):
    arena, ring, x, psum, ident = mem["arena"], mem["ring"], mem["x"], mem["psum"], mem["ident"]
    w_in = arena[:, 0:20480].rearrange("p (g k m) -> p g k m", g=5, k=KC)
    u = arena[:, 20480:21504]
    v = arena[:, 21504:22528]
    vals = arena[:, 22528:23552]
    qT = arena[:, 23552:24576].rearrange("p (c t) -> p c t", t=SEQ)
    kT = arena[:, 24576:25600].rearrange("p (c t) -> p c t", t=SEQ)
    ws = arena[:, 25600:26624].rearrange("p (h t) -> p h t", h=HEADS)
    catT = arena[:, 26624:28672].rearrange("p (m t) -> p m t", t=SEQ)
    hT = arena[:, 28672:30720]
    xn = arena[:, 30720:32768]
    w_out = arena[:, 0:8192].rearrange("p (k m) -> p k m", k=KC)
    scratch = arena[:, 8192:16384]
    vgain = ring[:, 0:512]
    mask = ring[:, 512:1024].rearrange("p (b t) -> p b t", b=2)
    tri = ring[:, 1024:1152]
    ones = ring[:, 1152:1280]
    sq = ring[:, 2048:3072]
    small = mem["act_buf"]
    gain = small[:, 0:KC]
    bias = small[:, 16:16 + HEADS]
    stat = mem["stat"]


    with nc.Block() as block:
        @block.sync
        def _(sp):
            sp.dma_start(gain, a["l1_norm_mix_g"]).then_inc(s("gain2_in"), 16)
            src = a["l1_w_in"].rearrange("(k p) (g m) -> g p k m", p=P, g=5)
            for g in range(5):
                sp.dma_start(w_in[:, g], src[g]).then_inc(s(f"w_in1_{g}"), 16)
            sp.dma_start(vgain, a["c_vnorm_g"].partition_broadcast(P)).then_inc(s("vgain_in"), 16)
            sp.dma_start(ws, a["c_ws"]).then_inc(s("ws_in"), 16)
            sp.dma_start(bias, a["c_bs"]).then_inc(s("bias_in"), 16)
            sp.wait_ge(s("proj_v"), TB)
            sp.dma_start(w_out, a["l1_w_out"].rearrange("(k p) m -> p k m", p=P)).then_inc(s("w_out1_in"), 16)

        @block.gpsimd
        def _(pool):
            nc.gpsimd.memset(ring[:, 512:1280], 1.0).then_inc(s("masks_one"), 1)
            pool.wait_ge(s("masks_one"), 1)
            for b in range(2):
                nc.gpsimd.affine_select(out=mask[:, b], in_=mask[:, b], compare_op=ALU.is_ge, fill=0.0,
                                        base=-1 - P * b, pattern=[[1, SEQ]], channel_multiplier=-1)\
                    .then_inc(s("masks_made"), 1)
            nc.gpsimd.affine_select(out=tri, in_=tri, compare_op=ALU.is_ge, fill=0.0,
                                    base=0, pattern=[[-1, P]], channel_multiplier=1)\
                .then_inc(s("masks_made"), 1)
            pool.wait_ge(s("ws_in"), 16)
            nc.gpsimd.affine_select(out=ws, in_=ws, compare_op=ALU.is_ge, fill=0.0,
                                    base=0, pattern=[[0, HEADS], [1, P]], channel_multiplier=-1)\
                .then_inc(s("ws_masked"), 1)

        @block.scalar
        def _(act):
            norm_act(nc, act, mem, s, "n2", xn)
            for tb in range(TB):
                act.wait_ge(s("proj_u"), tb + 1)
                nc.scalar.activation(u[:, tb * 512:(tb + 1) * 512], psum[4 + tb][:, :],
                                     ACT.Gelu_apprx_tanh).then_inc(s("u_gelu"), 1)
            for tb in range(TB):
                act.wait_ge(s("proj_v"), tb + 1)
                nc.scalar.activation(v[:, tb * 512:(tb + 1) * 512], psum[6 + tb][:, :],
                                     ACT.Gelu_apprx_tanh).then_inc(s("v_gelu"), 1)
            act.wait_ge(s("v_gelu"), TB)
            for tb in range(TB):
                nc.scalar.activation(sq[:, tb * 512:(tb + 1) * 512], v[:, tb * 512:(tb + 1) * 512], ACT.Square,
                                     accum_out=stat[:, 16 + tb:17 + tb]).then_inc(s("v_squares"), 1)
            for b in range(2):
                act.wait_ge(s("proj_q"), b + 1)
                nc.scalar.activation(qT[:, 2 * b:2 * b + 2], psum[b][:, :].rearrange("p (c t) -> p c t", c=2),
                                     ACT.Copy, scale=0.125).then_inc(s("qT"), 1)
            for b in range(2):
                act.wait_ge(s("proj_k"), b + 1)
                nc.scalar.activation(kT[:, 2 * b:2 * b + 2], psum[2 + b][:, :].rearrange("p (c t) -> p c t", c=2),
                                     ACT.Copy).then_inc(s("kT"), 1)
            for tb in range(TB):
                act.wait_ge(s("proj_vals"), tb + 1)
                nc.scalar.activation(vals[:, tb * 512:(tb + 1) * 512], psum[4 + tb][:, :],
                                     ACT.Copy).then_inc(s("vals"), 1)
            act.wait_ge(s("v_meansq"), 1)
            nc.scalar.activation(stat[:, 20:22], stat[:, 18:20], ACT.Sqrt).then_inc(s("v_rms"), 1)
            for h in range(HEADS):
                z, e, w = (scratch[:, (h % 2) * 2048 + 512 * n:(h % 2) * 2048 + 512 * (n + 1)]
                           for n in (0, 1, 3))
                act.wait_ge(s("sb_z"), h + 1)
                if h >= 2:
                    act.wait_ge(s("sb_arg"), 2 * (h - 1))
                nc.scalar.activation(z, psum[h % 2][:, :], ACT.Copy).then_inc(s("sb_z_copied"), 1)
                nc.scalar.activation(e, psum[h % 2][:, :], ACT.Abs).then_inc(s("sb_act_order"), 1)
                act.wait_ge(s("sb_act_order"), 3 * h + 1)
                nc.scalar.activation(e, e, ACT.Exp, scale=-1.0).then_inc(s("sb_act_order"), 1)
                act.wait_ge(s("sb_act_order"), 3 * h + 2)
                nc.scalar.activation(e, e, ACT.Ln, bias=1.0).then_inc(s("sb_act_order"), 1)
                act.wait_ge(s("sb_arg"), 2 * h + 2)
                nc.scalar.activation(w, w, ACT.Exp).then_inc(s("sb_exp"), 1)
                if h % 2 and h >= 3:
                    c = h // 2 - 1
                    act.wait_ge(s("sb_o"), 2 * c + 2)
                    nc.scalar.activation(catT[:, WC + c], psum[4 + c % 2][:, 0:SEQ], ACT.Copy)\
                        .then_inc(s("sb_out"), 1)
            act.wait_ge(s("sb_o"), HEADS)
            nc.scalar.activation(catT[:, WC + 3], psum[5][:, 0:SEQ], ACT.Copy).then_inc(s("sb_out"), 1)

        @block.vector
        def _(dve):
            link = ordered(dve, s("odd_dve_order"))
            tt, ts, stt = nc.vector.tensor_tensor, nc.vector.tensor_scalar, nc.vector.scalar_tensor_tensor
            norm_scale(nc, dve, mem, s, "n2", xn)
            dve.wait_ge(s("gain2_in"), 16)
            norm_gain(nc, dve, mem, s, "n2", hT, gain)
            dve.wait_ge(s("v_squares"), TB)
            ts(stat[:, 18:20], stat[:, 16:18], 1.0 / WIDTH, EPS, ALU.mult, ALU.add).then_inc(s("v_meansq"), 1)
            dve.wait_ge(s("v_rms"), 1)
            link(nc.vector.reciprocal(stat[:, 22:24], stat[:, 20:22]))
            dve.wait_ge(s("vgain_in"), 16)
            for tb in range(TB):
                vs = v[:, tb * 512:(tb + 1) * 512]
                stt(vs, vs, stat[:, 22 + tb:23 + tb], vgain, ALU.mult, ALU.mult).then_inc(s("v_normed"), 1)
            dve.wait_ge(s("bias_in"), 16)
            dve.wait_ge(s("u_gelu"), TB)
            for tb in range(TB):
                dve.wait_ge(s("spatial"), tb + 1)
                us = u[:, tb * 512:(tb + 1) * 512]
                y = sq[:, tb * 512:(tb + 1) * 512]
                link(tt(y.rearrange("p (h d) -> p h d", h=HEADS),
                        psum[6 + tb][:, :].rearrange("p (h d) -> p h d", h=HEADS),
                        bias.unsqueeze(2).broadcast_to([P, HEADS, 64]), ALU.add))
                tt(us, us, y, ALU.mult).then_inc(s("gmlp"), 1)
            dve.wait_ge(s("gmlp_turned"), 1)
            for b in range(2):
                nc.vector.tensor_copy(catT[:, 2 * b:2 * b + 2],
                                      psum[2 + b][:, :].rearrange("p (c t) -> p c t", c=2))\
                    .then_inc(s("catT1"), 1)
            dve.wait_ge(s("masks_made"), 3)
            for h in range(HEADS):
                z, e, sp_, w = (scratch[:, (h % 2) * 2048 + 512 * n:(h % 2) * 2048 + 512 * (n + 1)]
                                for n in range(4))
                m = mask.rearrange("p b t -> p (b t)")
                dve.wait_ge(s("sb_act_order"), 3 * h + 3)
                dve.wait_ge(s("sb_z_copied"), h + 1)
                if h >= 2:
                    dve.wait_ge(s("sb_sum"), h - 1)
                link(stt(sp_, z, 0.0, e, ALU.max, ALU.add))
                tt(sp_, sp_, m, ALU.mult).then_inc(s("sb_softplus"), 1)
                dve.wait_ge(s("sb_sum"), h + 1)
                if h >= 2:
                    dve.wait_ge(s("sb_o"), h - 1)
                tt(w, z, psum[2 + h % 2][:, :], ALU.subtract).then_inc(s("sb_arg"), 1)
                dve.wait_ge(s("sb_arg"), 2 * h + 1)
                ts(w, w, 0.0, None, ALU.min).then_inc(s("sb_arg"), 1)
                dve.wait_ge(s("sb_exp"), h + 1)
                tt(w, w, m, ALU.mult).then_inc(s("sb_w"), 1)
            for n in range(4):
                dve.wait_ge(s("mixed1"), n + 1)
                xs = x[:, n * 512:(n + 1) * 512]
                tt(xs, xs, psum[n if n < 2 else 4 + n][:, :], ALU.add).then_inc(s("x_after_mix1"), 1)
            dve.wait_ge(s("x_after_mix1"), 4)

        @block.tensor
        def _(pe):
            norm_pe(nc, pe, mem, s, "n2", xn)
            pe.wait_ge(s("n2_hT"), 4)

            def token_major(g, bank, name):
                pe.wait_ge(s(f"w_in1_{g}"), 16)
                for tb in range(TB):
                    for k in range(KC):
                        last = nc.tensor.matmul(psum[bank + tb][:, :], hT[:, k * SEQ + tb * P:k * SEQ + (tb + 1) * P],
                                                w_in[:, g, k, :], start=(k == 0), stop=(k == KC - 1))
                    last.then_inc(s(name), 1)

            def feature_major(g, bank, name):
                pe.wait_ge(s(f"w_in1_{g}"), 16)
                for m in range(WC):
                    for k in range(KC):
                        last = nc.tensor.matmul(psum[bank + m // 2][:, (m % 2) * SEQ:(m % 2 + 1) * SEQ],
                                                w_in[:, g, k, m * P:(m + 1) * P], hT[:, k * SEQ:(k + 1) * SEQ],
                                                start=(k == 0), stop=(k == KC - 1))
                    if m % 2:
                        last.then_inc(s(name), 1)

            token_major(0, 4, "proj_u")
            token_major(1, 6, "proj_v")
            feature_major(2, 0, "proj_q")
            feature_major(3, 2, "proj_k")
            pe.wait_ge(s("u_gelu"), TB)
            token_major(4, 4, "proj_vals")
            pe.wait_ge(s("proj_vals"), TB)
            pe.wait_ge(s("qT"), 2)
            pe.wait_ge(s("ws_masked"), 1)
            for tb in range(TB):
                pe.wait_ge(s("v_normed"), tb + 1)
                for h in range(HEADS):
                    last = nc.tensor.matmul(psum[6 + tb][:, h * 64:(h + 1) * 64], ws[:, h, :],
                                            v[:, tb * 512 + h * 64:tb * 512 + (h + 1) * 64],
                                            start=True, stop=True)
                last.then_inc(s("spatial"), 1)
            pe.wait_ge(s("kT"), 2)
            for tb in range(TB):
                pe.wait_ge(s("gmlp"), tb + 1)
                for c in range(WC):
                    o = (c % 2) * SEQ + tb * P
                    last = nc.tensor.transpose(psum[2 + c // 2][:, o:o + P],
                                               u[:, tb * 512 + c * P:tb * 512 + (c + 1) * P], ident[:, :])
            last.then_inc(s("gmlp_turned"), 1)
            pe.wait_ge(s("vals"), TB)
            pe.wait_ge(s("masks_made"), 3)

            def scores(h):
                if h >= 2:
                    pe.wait_ge(s("sb_z_copied"), h - 1)
                    pe.wait_ge(s("sb_act_order"), 3 * (h - 2) + 1)
                r = 64 * (h % 2)
                for b in range(2):
                    last = nc.tensor.matmul(psum[h % 2][:, b * SEQ:(b + 1) * SEQ],
                                            kT[r:r + 64, h // 2, b * P:(b + 1) * P], qT[r:r + 64, h // 2, :],
                                            start=True, stop=True)
                last.then_inc(s("sb_z"), 1)

            def sums(h):
                sp_ = scratch[:, (h % 2) * 2048 + 1024:(h % 2) * 2048 + 1536]
                pe.wait_ge(s("sb_softplus"), h + 1)
                if h < 2:
                    pe.wait_ge(s("catT1"), 2)
                else:
                    pe.wait_ge(s("sb_arg"), 2 * (h - 2) + 1)
                bank = psum[2 + h % 2]
                nc.tensor.matmul(bank[:, SEQ:], tri, sp_[:, SEQ:], start=True, stop=True)
                nc.tensor.matmul(bank[:, 0:SEQ], tri, sp_[:, 0:SEQ], start=True, stop=False)
                nc.tensor.matmul(bank[:, 0:SEQ], ones, sp_[:, SEQ:], start=False, stop=True)\
                    .then_inc(s("sb_sum"), 1)

            def outputs(h):
                w = scratch[:, (h % 2) * 2048 + 1536:(h % 2) * 2048 + 2048]
                c, r = h // 2, 64 * (h % 2)
                pe.wait_ge(s("sb_w"), h + 1)
                if c >= 2:
                    pe.wait_ge(s("sb_out"), c - 1)
                for b in range(2):
                    last = nc.tensor.matmul(psum[4 + c % 2][r:r + 64, 0:SEQ],
                                            vals[:, b * 512 + h * 64:b * 512 + (h + 1) * 64],
                                            w[:, b * SEQ:(b + 1) * SEQ], start=(b == 0), stop=(b == 1))
                last.then_inc(s("sb_o"), 1)

            scores(0)
            scores(1)
            for h in range(HEADS):
                sums(h)
                if h >= 1:
                    outputs(h - 1)
                if 2 <= h + 1 < HEADS:
                    scores(h + 1)
            outputs(HEADS - 1)
            pe.wait_ge(s("w_out1_in"), 16)
            pe.wait_ge(s("sb_out"), WC)
            pe.wait_ge(s("sb_act_order"), 3 * HEADS)
            for n in range(4):
                tb, half = n // 2, n % 2
                for k in range(KC):
                    last = nc.tensor.matmul(psum[n if n < 2 else 4 + n][:, :], catT[:, k, tb * P:(tb + 1) * P],
                                            w_out[:, k, half * 512:(half + 1) * 512],
                                            start=(k == 0), stop=(k == KC - 1))
                last.then_inc(s("mixed1"), 1)



def peer(nc, a, mem, shared_sem, layer):
    def s(name):
        return shared_sem(f"{layer}_{name}")

    arena, ring, x, psum, ident = (mem[k] for k in ("arena", "ring", "x", "psum", "ident"))
    places = mem["stat"][:, 16:16 + TOPK]
    iota = ident[:, :]
    h_parts = mem["h_parts"][:, :].rearrange("p (c r t) -> p c r t", c=KC, r=2)
    u_parts = mem["u_parts"][:, :].rearrange("p (r c e) -> p r c e", r=2, c=KC)
    v_parts = mem["v_parts"][:, :].rearrange("p (r d) -> p r d", r=2)
    early_parts = [u_parts, mem["v_parts"][:, :].rearrange("p (r c e) -> p r c e", r=2, c=KC)]
    w_parts = mem["w_parts"][:, :].rearrange("p (b r t) -> p b r t", b=2, r=2)
    act_buf, low_buf = mem["act_buf"], mem["low_buf"]
    wq = arena[:, 0:16384].rearrange("p (g k m) -> p g k m", g=4, k=KC)
    keysT = arena[:, 16384:18432].rearrange("p (r n) -> p r n", r=ROWS)
    qT = arena[:, 18432:22528].rearrange("p (r t) -> p r t", t=SEQ)
    scores = [arena[:, 22528 + 2048 * tb:24576 + 2048 * tb].rearrange("p (r n) -> p r n", r=ROWS)
              for tb in range(TB)]
    rest = arena[:, 26624:28672].rearrange("p (r n) -> p r n", r=ROWS)
    hT = arena[:, 28672:30720]
    xn = arena[:, 30720:32768]
    cand = arena[:, 16384:18432].rearrange("p (h c) -> p h c", h=HEADS)
    cand_rest = arena[:, 18432:20480].rearrange("p (h c) -> p h c", h=HEADS)
    eq = arena[:, 20480:22528]

    def small(i, n=128):
        return arena[:, 28672 + 128 * i:28672 + 128 * i + n]
    best = small(0, 256).rearrange("p (r k) -> p r k", r=ROWS)
    best_at = small(2, 256).bitcast(U32).rearrange("p (r k) -> p r k", r=ROWS)
    key_of = small(4, 256).rearrange("p (r k) -> p r k", r=ROWS)
    top = [small(6 + tb).rearrange("p (h k) -> p h k", h=HEADS) for tb in range(TB)]
    top_at = small(8).bitcast(U32).rearrange("p (h k) -> p h k", h=HEADS)
    part_at = small(9).bitcast(U32)
    part = small(10)
    total = [small(11 + tb, HEADS) for tb in range(TB)]
    choice = [[arena[:, 30720 + 384 * tb + 128 * n:30720 + 384 * tb + 128 * (n + 1)] for n in range(3)]
              for tb in range(TB)]
    pick_keys = act_buf[:, :].rearrange("p (z t) -> p z t", z=2)
    pick_gate = low_buf[:, :]
    one_hot = [ring[:, 1024 * b:1024 * (b + 1)].rearrange("p (z t e) -> p z t e", z=2, t=GATE_TOKENS)
               for b in range(UNROLL)]
    group_gate = [mem["stat"][:, 32 + GATE_TOKENS * b:32 + GATE_TOKENS * (b + 1)] for b in range(UNROLL)]
    gates = arena[:, :].rearrange("p (e t) -> p e t", t=SEQ)
    table_u = [ring[:, 1024 * n:1024 * (n + 1)] for n in range(UNROLL)]
    table_v = [ring[:, 4096 + 1024 * n:4096 + 1024 * (n + 1)] for n in range(UNROLL)]
    u_src = a[layer + "_peer_u"]
    v_src = a[layer + "_peer_v"].rearrange("(p e) d -> e p d", p=P)
    gain = act_buf[:, 0:KC]

    def fetch_u(sp, i, slot):
        sp.dma_start(table_u[slot], u_src[i]).then_inc(s(f"u_in_{slot}"), 16)

    def fetch_v(sp, i, slot):
        sp.dma_start(table_v[slot], v_src[i]).then_inc(s(f"v_in_{slot}"), 16)

    def u_high(act, i, turn, n, parts, lag, first=False):
        act.wait_ge(s(f"u_in_{n}"), turn * 16 + 16)
        for hf in range(2):
            if not first:
                act.wait_ge(s("u_used"), (i - lag) * 2 + 1 + hf)
            nc.scalar.activation(parts[:, 0, 4 * hf:4 * (hf + 1)],
                                 table_u[n][:, 512 * hf:512 * (hf + 1)].rearrange("p (c e) -> p c e", c=4),
                                 ACT.Copy).then_inc(s("u_high"), 1)

    def u_low(eng, tensor_tensor, i, hf, n, parts):
        eng.wait_ge(s("u_high"), i * 2 + hf + 1)
        cut = slice(4 * hf, 4 * (hf + 1))
        tensor_tensor(parts[:, 1, cut],
                      table_u[n][:, 512 * hf:512 * (hf + 1)].rearrange("p (c e) -> p c e", c=4),
                      parts[:, 0, cut].bitcast(F32), ALU.subtract).then_inc(s("u_split"), 1)

    with nc.Block() as block:
        @block.sync
        def _(sp):
            sp.dma_start(gain, a[layer + "_norm_ffn_g"]).then_inc(s("gain_in"), 16)
            src = a[layer + "_peer_wq"].rearrange("(k p) (g m) -> g p k m", p=P, g=4)
            for g in range(4):
                sp.dma_start(wq[:, g], src[g]).then_inc(s(f"wq_{g}"), 16)
            sp.dma_start(arena[:, 16384:18432], a[layer + "_keys"]).then_inc(s("keys_in"), 16)
            for n in range(UNROLL):
                fetch_u(sp, n, n)
            for n in range(UNROLL):
                fetch_v(sp, n, n)
            with sp.Fori(1, EARLY // UNROLL) as turn:
                for n in range(UNROLL):
                    sp.wait_ge(s("u_split"), (turn * UNROLL + n) * 2 - 2 * UNROLL + 2)
                    fetch_u(sp, turn * UNROLL + n, n)

        @block.gpsimd
        def _(pool):
            nc.gpsimd.iota(places, [[1, TOPK]], base=0, channel_multiplier=0,
                           allow_small_or_imprecise_dtypes=True).then_inc(s("places_made"), 1)
            with pool.Fori(0, EARLY // UNROLL) as turn:
                for n in range(UNROLL):
                    for hf in range(2):
                        u_low(pool, nc.gpsimd.tensor_tensor, turn * UNROLL + n, hf, n, early_parts[n % 2])

        @block.scalar
        def _(act):
            norm_act(nc, act, mem, s, "n", xn)
            for b in range(4):
                act.wait_ge(s("n_hT"), 4)
                act.activation(h_parts[:, 2 * b:2 * b + 2, 0], hT[:, 512 * b:512 * (b + 1)]
                               .rearrange("p (c t) -> p c t", c=2), ACT.Copy).then_inc(s("h_high"), 1)
            for b in range(8):
                act.wait_ge(s("query"), b + 1)
                nc.scalar.activation(qT[:, 2 * b:2 * b + 2], psum[b % 4][:, :].rearrange("p (r t) -> p r t", r=2),
                                     ACT.Copy).then_inc(s("qT"), 1)
            for tb in range(TB):
                for b in range(4):
                    act.wait_ge(s("scored"), 4 * tb + b + 1)
                    nc.scalar.activation(scores[tb][:, 4 * b:4 * b + 4],
                                         psum[4 * (1 - tb) + b][:, :].rearrange("p (r n) -> p r n", r=4),
                                         ACT.Copy).then_inc(s("scores"), 1)
            def early(i, turn, n, first):
                u_high(act, i, turn, n, early_parts[n % 2], 2, first and n < 2)
                if not (first and n == 0):
                    early_gelu(i - 1, (n - 1) % UNROLL)

            def early_gelu(i, n):
                act.wait_ge(s("u_used"), i * 2 + 2)
                nc.scalar.activation(arena[:, bass.ds(i * SEQ, SEQ)], psum[4 + n % 2][:, 0:SEQ],
                                     ACT.Gelu_apprx_tanh).then_inc(s("early_acts"), 1)
            for n in range(UNROLL):
                early(n, 0, n, True)
            with act.Fori(1, EARLY // UNROLL) as turn:
                for n in range(UNROLL):
                    early(turn * UNROLL + n, turn, n, False)
            early_gelu(EARLY - 1, UNROLL - 1)
            for tb in range(TB):
                act.wait_ge(s("top_shifted"), tb + 1)
                nc.scalar.activation(top[tb], top[tb], ACT.Exp).then_inc(s("top_exp"), 1)

        @block.vector
        def _(dve):
            tt, ts = nc.vector.tensor_tensor, nc.vector.tensor_scalar
            link = ordered(dve, s("dve_order"))
            norm_scale(nc, dve, mem, s, "n", xn)
            dve.wait_ge(s("gain_in"), 16)
            norm_gain(nc, dve, mem, s, "n", hT, gain)
            dve.wait_ge(s("n_hT"), 4)
            dve.wait_ge(s("h_high"), 4)
            dve.wait_ge(s("places_made"), 1)
            for b in range(4):
                h_in = hT[:, 512 * b:512 * (b + 1)].rearrange("p (c t) -> p c t", c=2)
                tt(h_parts[:, 2 * b:2 * b + 2, 1], h_in, h_parts[:, 2 * b:2 * b + 2, 0].bitcast(F32),
                   ALU.subtract).then_inc(s("h_low"), 1)
            dve.wait_ge(s("h_low"), 4)
            for tb in range(TB):
                def best16(n, src, left, val, at):
                    for r in range(n):
                        last = nc.vector.max(val[:, r, 0:8], src[:, r])
                    link(last)
                    for r in range(n):
                        nc.vector.max_index(at[:, r, 0:8], val[:, r, 0:8], src[:, r])
                        last = nc.vector.match_replace(left[:, r], val[:, r, 0:8], src[:, r], LOWEST)
                    link(last)
                    for r in range(n):
                        last = nc.vector.max(val[:, r, 8:16], left[:, r])
                    link(last)
                    for r in range(n):
                        last = nc.vector.max_index(at[:, r, 8:16], val[:, r, 8:16], left[:, r])
                    link(last)
                dve.wait_ge(s("scores"), 4 * tb + 4)
                best16(ROWS, scores[tb], rest, best, best_at)
                link(nc.vector.tensor_copy(key_of, best_at))
                if tb == 0:
                    dve.wait_ge(s("scored"), 8)
                halves = best.rearrange("p (h z) k -> p h z k", z=2)
                link(tt(cand.rearrange("p h (i j) -> p h i j", i=TOPK),
                        halves[:, :, 0].unsqueeze(3).broadcast_to([P, HEADS, TOPK, TOPK]),
                        halves[:, :, 1].unsqueeze(2).broadcast_to([P, HEADS, TOPK, TOPK]), ALU.add))
                best16(HEADS, cand, cand_rest, top[tb], top_at)
                keys = key_of.rearrange("p (h z) k -> p h z k", z=2)
                for z in range(2):
                    if z == 0:
                        link(ts(part_at, small(8).bitcast(U32), 4, None, ALU.logical_shift_right))
                    else:
                        link(ts(part_at, small(8).bitcast(U32), 15, None, ALU.bitwise_and))
                    link(nc.vector.tensor_copy(part, part_at))
                    eq4 = eq.rearrange("p (h k j) -> p h k j", h=HEADS, k=TOPK)
                    link(tt(eq4, part.rearrange("p (h k) -> p h k", h=HEADS).unsqueeze(3)
                            .broadcast_to([P, HEADS, TOPK, TOPK]),
                            places.unsqueeze(1).unsqueeze(1).broadcast_to([P, HEADS, TOPK, TOPK]),
                            ALU.is_equal))
                    link(tt(eq4, eq4, keys[:, :, z].unsqueeze(2).broadcast_to([P, HEADS, TOPK, TOPK]), ALU.mult))
                    link(nc.vector.tensor_reduce(choice[tb][z], eq.rearrange("p (n j) -> p n j", j=TOPK),
                                                 AXX, ALU.add))
                link(nc.vector.tensor_copy(total[tb], top[tb][:, :, 0]))
                tt(top[tb], top[tb], total[tb].unsqueeze(2).broadcast_to([P, HEADS, TOPK]), ALU.subtract)\
                    .then_inc(s("top_shifted"), 1)
            for tb in range(TB):
                dve.wait_ge(s("top_exp"), tb + 1)
                link(nc.vector.tensor_reduce(total[tb], top[tb], AXX, ALU.add))
                link(nc.vector.reciprocal(total[tb], total[tb]))
                tt(choice[tb][2].rearrange("p (h k) -> p h k", h=HEADS), top[tb],
                   total[tb].unsqueeze(2).broadcast_to([P, HEADS, TOPK]), ALU.mult).then_inc(s("chosen"), 1)
            dve.wait_ge(s("chosen"), TB)
            dve.wait_ge(s("choice_turned"), 1)
            nc.vector.tensor_copy(act_buf[:, :], psum[0][:, :]).then_inc(s("picks"), 1)
            nc.vector.tensor_copy(pick_gate, psum[1][:, 0:SEQ]).then_inc(s("picks"), 1)

        @block.tensor
        def _(pe):
            norm_pe(nc, pe, mem, s, "n", xn)
            pe.wait_ge(s("n_hT"), 4)
            for r in range(ROWS):
                if r % 4 == 0:
                    pe.wait_ge(s(f"wq_{r // 4}"), 16)
                if r % 2 == 0 and r >= 8:
                    pe.wait_ge(s("qT"), r // 2 - 3)
                for k in range(KC):
                    last = nc.tensor.matmul(psum[(r // 2) % 4][:, (r % 2) * SEQ:(r % 2 + 1) * SEQ],
                                            wq[:, r // 4, k, (r % 4) * P:(r % 4 + 1) * P],
                                            hT[:, k * SEQ:(k + 1) * SEQ], start=(k == 0), stop=(k == KC - 1))
                if r % 2:
                    last.then_inc(s("query"), 1)
            pe.wait_ge(s("keys_in"), 16)
            pe.wait_ge(s("qT"), 8)
            for tb in range(TB):
                for r in range(ROWS):
                    last = nc.tensor.matmul(psum[4 * (1 - tb) + r // 4][:, (r % 4) * P:(r % 4 + 1) * P],
                                            qT[:, r, tb * P:(tb + 1) * P], keysT[:, r, :], start=True, stop=True)
                    if r % 4 == 3:
                        last.then_inc(s("scored"), 1)
            pe.wait_ge(s("scores"), 8)
            pe.wait_ge(s("h_low"), 4)

            def early(i, n, first):
                if not first:
                    pe.wait_ge(s("early_acts"), i - 1)
                bank = psum[4 + n % 2][:, 0:SEQ]
                for hf in range(2):
                    pe.wait_ge(s("u_split"), i * 2 + hf + 1)
                    for c in range(4 * hf, 4 * hf + 4):
                        parts = early_parts[n % 2]
                        nc.tensor.matmul(bank, parts[:, 0, c], h_parts[:, c, 0], start=(c == 0), stop=False)
                        nc.tensor.matmul(bank, parts[:, 0, c], h_parts[:, c, 1], start=False, stop=False)
                        last = nc.tensor.matmul(bank, parts[:, 1, c], h_parts[:, c, 0],
                                                start=False, stop=(c == KC - 1))
                    last.then_inc(s("u_used"), 1)
            for n in range(UNROLL):
                early(n, n, n < 2)
            with pe.Fori(1, EARLY // UNROLL) as turn:
                for n in range(UNROLL):
                    early(turn * UNROLL + n, n, False)
            for tb in range(TB):
                pe.wait_ge(s("chosen"), tb + 1)
                for n in range(3):
                    o = (n % 2) * SEQ + tb * P
                    last = nc.tensor.transpose(psum[n // 2][:, o:o + P], choice[tb][n], ident[:, :])
            last.then_inc(s("choice_turned"), 1)

    GROUPS = SEQ // GATE_TOKENS
    with nc.Block() as block:
        def groups(eng, step):
            for n in range(UNROLL):
                step(n, n, True)
            with eng.Fori(1, GROUPS // UNROLL) as turn:
                for n in range(UNROLL):
                    step(turn * UNROLL + n, n, False)

        @block.gpsimd
        def _(pool):
            nc.gpsimd.iota(iota, [[1, KEYS]], base=0, channel_multiplier=0,
                           allow_small_or_imprecise_dtypes=True).then_inc(s("iota_made"), 1)

            def scale_rows(g, b, first):
                pool.wait_ge(s("gate_staged"), g + 1)
                pool.wait_ge(s("hot_rows"), g + 1)
                nc.gpsimd.tensor_tensor(one_hot[b][:, 0], one_hot[b][:, 0],
                                        group_gate[b].unsqueeze(2).broadcast_to([P, GATE_TOKENS, KEYS]), ALU.mult)\
                    .then_inc(s("hot_scaled"), 1)
            groups(pool, scale_rows)

        @block.vector
        def _(dve):
            wide = [P, 2, GATE_TOKENS, KEYS]

            def merge(g, b):
                dve.wait_ge(s("gate_copied"), g + 1)
                here = gates[:, 0:EARLY, bass.ds(g * GATE_TOKENS, GATE_TOKENS)]
                nc.vector.tensor_tensor(here, psum[b][:, :].rearrange("p (t e) -> p e t", t=GATE_TOKENS)[:, 0:EARLY],
                                        here, ALU.mult).then_inc(s("gate_merged"), 1)

            def build(g, b, first):
                if not first:
                    dve.wait_ge(s("gate_banks"), g - 3)
                at = bass.ds(g * GATE_TOKENS, GATE_TOKENS)
                nc.vector.tensor_copy(group_gate[b], pick_gate[:, at]).then_inc(s("gate_staged"), 1)
                nc.vector.tensor_tensor(one_hot[b], pick_keys[:, :, at].unsqueeze(3).broadcast_to(wide),
                                        iota.unsqueeze(1).unsqueeze(1).broadcast_to(wide), ALU.is_equal)\
                    .then_inc(s("hot_rows"), 1)
                if not first or b == UNROLL - 1:
                    merge(g - 3, (b + 1) % UNROLL)
            dve.wait_ge(s("iota_made"), 1)
            groups(dve, build)
            for n in range(1, UNROLL):
                merge(GROUPS - UNROLL + n, n)

        @block.tensor
        def _(pe):
            def products(g, b, first):
                if not first:
                    pe.wait_ge(s("gate_merged"), g - 3)
                pe.wait_ge(s("hot_scaled"), g + 1)
                for t in range(GATE_TOKENS):
                    last = nc.tensor.matmul(psum[b][:, t * P:(t + 1) * P], one_hot[b][:, 0, t],
                                            one_hot[b][:, 1, t], start=True, stop=True)
                last.then_inc(s("gate_banks"), 1)
            groups(pe, products)

        @block.scalar
        def _(act):
            def copy_out(g, b, first):
                act.wait_ge(s("gate_banks"), g + 1)
                nc.scalar.activation(gates[:, EARLY:, bass.ds(g * GATE_TOKENS, GATE_TOKENS)],
                                     psum[b][:, :].rearrange("p (t e) -> p e t", t=GATE_TOKENS)[:, EARLY:],
                                     ACT.Copy).then_inc(s("gate_copied"), 1)
            groups(act, copy_out)

    with nc.Block() as block:
        @block.gpsimd
        def _(pool):
            nc.gpsimd.memset(ident[:, :], 0.0).then_inc(s("ident_zero"), 1)
            pool.wait_ge(s("ident_zero"), 1)
            nc.gpsimd.affine_select(out=ident[:, :], in_=ident[:, :], compare_op=ALU.not_equal, fill=1.0,
                                    base=0, pattern=[[-1, P]], channel_multiplier=1)\
                .then_inc(s("ident_made"), 1)

        def steps(eng, first, count, step):
            turns = range(first // UNROLL, (first + count) // UNROLL)
            for n in range(UNROLL):
                step(first + n, turns[0], n, True)
            with eng.Fori(turns[1], turns[-1]) as turn:
                for n in range(UNROLL):
                    step(turn * UNROLL + n, turn, n, False)
            for n in range(UNROLL):
                step(turns[-1] * UNROLL + n, turns[-1], n, True)

        @block.sync
        def _(sp):
            def fetch_v_when_free(i, n):
                sp.wait_ge(s("v_split"), i * 2 - 2 * UNROLL + 2)
                fetch_v(sp, i, n)
            for n in range(UNROLL):
                fetch_u(sp, EARLY + n, n)
            with sp.Fori(1, EARLY // UNROLL) as turn:
                for n in range(UNROLL):
                    fetch_v_when_free(turn * UNROLL + n, n)
            with sp.Fori(EARLY // UNROLL, SLICES // UNROLL - 1) as turn:
                for n in range(UNROLL):
                    i = turn * UNROLL + n
                    fetch_v_when_free(i, n)
                    sp.wait_ge(s("u_split"), i * 2 + 2)
                    fetch_u(sp, i + UNROLL, n)
            for n in range(UNROLL):
                fetch_v_when_free(SLICES - UNROLL + n, n)

        @block.scalar
        def _(act):
            def v_high(i, turn, n, first):
                act.wait_ge(s(f"v_in_{n}"), turn * 16 + 16)
                for hf in range(2):
                    if not first:
                        act.wait_ge(s("v_used"), i * 2 - 1 + hf)
                    nc.scalar.activation(v_parts[:, 0, 512 * hf:512 * (hf + 1)],
                                         table_v[n][:, 512 * hf:512 * (hf + 1)], ACT.Copy)\
                        .then_inc(s("v_high"), 1)

            def pre_low(i, n, first):
                if not first:
                    act.wait_ge(s("pre_sum"), i - EARLY)
                act.wait_ge(s("u_used"), i * 2 + 2)
                nc.scalar.activation(low_buf[:, :], psum[4 + n % 2][:, SEQ:],
                                     ACT.Copy).then_inc(s("pre_low"), 1)

            def gelu(i, n):
                act.wait_ge(s("pre_sum"), i - EARLY + 1)
                nc.scalar.activation(act_buf[:, (n % 2) * SEQ:(n % 2 + 1) * SEQ],
                                     act_buf[:, (n % 2) * SEQ:(n % 2 + 1) * SEQ],
                                     ACT.Gelu_apprx_tanh).then_inc(s("gelu"), 1)

            def known_step(i, turn, n, peeled):
                v_high(i, turn, n, peeled and i == 0)

            def step(i, turn, n, peeled):
                if not (peeled and i == SLICES - 1):
                    u_high(act, i + 1, turn if n < UNROLL - 1 else turn + 1, (n + 1) % UNROLL, u_parts, 1)
                pre_low(i, n, peeled and i == EARLY)
                gelu(i, n)
                v_high(i, turn, n, False)
            steps(act, 0, EARLY, known_step)
            u_high(act, EARLY, EARLY // UNROLL, 0, u_parts, 1)
            steps(act, EARLY, SLICES - EARLY, step)

        @block.vector
        def _(dve):
            tt = nc.vector.tensor_tensor

            def v_low(i, n):
                for hf in range(2):
                    dve.wait_ge(s("v_high"), i * 2 + hf + 1)
                    cut = slice(512 * hf, 512 * (hf + 1))
                    tt(v_parts[:, 1, cut], table_v[n][:, cut], v_parts[:, 0, cut].bitcast(F32),
                       ALU.subtract).then_inc(s("v_split"), 1)

            def split_weight(i, n, weight):
                nc.vector.tensor_copy(w_parts[:, n % 2, 0], weight).then_inc(s("weight_high"), 1)
                dve.wait_ge(s("weight_high"), i + 1)
                tt(w_parts[:, n % 2, 1], weight, w_parts[:, n % 2, 0].bitcast(F32), ALU.subtract)\
                    .then_inc(s("weight"), 1)

            def pre_sum(i, n):
                dve.wait_ge(s("pre_low"), i - EARLY + 1)
                tt(act_buf[:, (n % 2) * SEQ:(n % 2 + 1) * SEQ], psum[4 + n % 2][:, 0:SEQ], low_buf[:, :], ALU.add)\
                    .then_inc(s("pre_sum"), 1)

            def known_step(i, turn, n, peeled):
                split_weight(i, n, arena[:, bass.ds(i * SEQ, SEQ)])
                v_low(i, n)

            def step(i, turn, n, peeled):
                if peeled and i == SLICES - 1:
                    pre_sum(i, n)
                else:
                    u_low(dve, tt, i + 1, 0, (n + 1) % UNROLL, u_parts)
                    pre_sum(i, n)
                    u_low(dve, tt, i + 1, 1, (n + 1) % UNROLL, u_parts)
                buf = act_buf[:, (n % 2) * SEQ:(n % 2 + 1) * SEQ]
                dve.wait_ge(s("gelu"), i - EARLY + 1)
                tt(buf, buf, arena[:, bass.ds(i * SEQ, SEQ)], ALU.mult).then_inc(s("weighed"), 1)
                dve.wait_ge(s("weighed"), i - EARLY + 1)
                split_weight(i, n, buf)
                v_low(i, n)
            steps(dve, 0, EARLY, known_step)
            u_low(dve, tt, EARLY, 0, 0, u_parts)
            u_low(dve, tt, EARLY, 1, 0, u_parts)
            steps(dve, EARLY, SLICES - EARLY, step)
            for n in range(4):
                dve.wait_ge(s("v_used"), 2 * SLICES)
                xs = x[:, n * 512:(n + 1) * 512]
                tt(xs, xs, psum[n][:, :], ALU.add).then_inc(s("x_after"), 1)
            dve.wait_ge(s("x_after"), 4)

        @block.tensor
        def _(pe):
            def pre(i, n, first):
                if not first:
                    pe.wait_ge(s("pre_sum"), i - EARLY - 1)
                bank = psum[4 + n % 2]
                for hf in range(2):
                    pe.wait_ge(s("u_split"), i * 2 + hf + 1)
                    for c in range(4 * hf, 4 * hf + 4):
                        nc.tensor.matmul(bank[:, :], u_parts[:, 0, c], h_parts[:, c].rearrange("p r t -> p (r t)"),
                                         start=(c == 0), stop=False)
                        last = nc.tensor.matmul(bank[:, 0:SEQ], u_parts[:, 1, c], h_parts[:, c, 0],
                                                start=False, stop=(c == KC - 1))
                    last.then_inc(s("u_used"), 1)

            def combine(i, n, first=False, final=False):
                pe.wait_ge(s("weight"), i + 1)
                for hf in range(2):
                    pe.wait_ge(s("v_split"), i * 2 + hf + 1)
                    for tb in range(TB):
                        w = [w_parts[:, n % 2, r, tb * P:(tb + 1) * P] for r in range(2)]
                        v = [v_parts[:, r, 512 * hf:512 * (hf + 1)] for r in range(2)]
                        o = psum[2 * tb + hf][:, :]
                        nc.tensor.matmul(o, w[0], v[0], start=first, stop=False)
                        nc.tensor.matmul(o, w[0], v[1], start=False, stop=False)
                        last = nc.tensor.matmul(o, w[1], v[0], start=False, stop=final)
                    last.then_inc(s("v_used"), 1)

            def known_step(i, turn, n, peeled):
                combine(i, n, peeled and i == 0)

            def step(i, turn, n, peeled):
                pre(i, n, peeled and i < EARLY + 2)
                if not (peeled and i == EARLY):
                    combine(i - 1, (n - 1) % UNROLL)
            steps(pe, 0, EARLY, known_step)
            steps(pe, EARLY, SLICES - EARLY, step)
            combine(SLICES - 1, UNROLL - 1, final=True)


def final_norm(nc, a, mem, s, out):
    arena, x, stat = mem["arena"], mem["x"], mem["stat"]
    xn = arena[:, 0:2048]
    gain = arena[:, 2048:3072]
    with nc.Block() as block:
        @block.scalar
        def _(act):
            norm_act(nc, act, mem, s, "nf", xn)

        @block.vector
        def _(dve):
            norm_scale(nc, dve, mem, s, "nf", xn)
            dve.wait_ge(s("gainf_in"), 16)
            for tb in range(TB):
                xs = xn[:, tb * D:(tb + 1) * D]
                dve.wait_ge(s("nf_xn"), tb + 1)
                nc.vector.tensor_tensor(xs, xs, gain, ALU.mult).then_inc(s("y"), 1)

        @block.sync
        def _(sp):
            sp.dma_start(gain, a["final_norm_g"].partition_broadcast(P)).then_inc(s("gainf_in"), 16)
            dst = out.rearrange("(b p) d -> b p d", p=P)
            for tb in range(TB):
                sp.wait_ge(s("y"), tb + 1)
                sp.dma_start(dst[tb], xn[:, tb * D:(tb + 1) * D]).then_inc(s("y_out"), 16)
            sp.wait_ge(s("y_out"), 16 * TB)



def _layout(np, i):
    f = {k: np.asarray(v) for k, v in i.items()}
    d = {"x": f["x"].reshape(SEQ, D)}
    for k in ("l0_w_in", "l0_w_out", "l1_w_in", "l1_w_out", "l0_peer_wq", "l1_peer_wq", "l0_peer_v",
              "l1_peer_v", "a_glu_w", "final_norm_g", "c_vnorm_g"):
        d[k] = f[k]
    for k in ("l0_norm_mix_g", "l0_norm_ffn_g", "l1_norm_mix_g", "l1_norm_ffn_g"):
        d[k] = f[k].reshape(KC, P).T

    def states(m):
        return m.reshape(S5_TILES, P).T
    d["s5_params"] = np.concatenate([states(f["a_lam_re"]), states(f["a_lam_im"]),
                                     states(np.repeat(f["a_log_dt"], 64).reshape(32, 64))], 1)
    b = np.zeros((2, 8, 16, WC, 2, 64), np.float32)
    c = np.zeros((2, 2, 64, S5_TILES, 2, 16), np.float32)
    for r, (bb, cc) in enumerate(((f["a_b_re"], f["a_c_re"]), (f["a_b_im"], f["a_c_im"]))):
        for g in range(32):
            b[r, g % 8, :, g // 8, g % 2, :] = bb[g].T
            c[r, g % 2, :, g // 2, g % 2, :] = cc[g].T
    d["s5_b"] = b.reshape(2, P, 512).transpose(1, 0, 2).reshape(P, 1024)
    d["s5_c"] = c.reshape(2, P, 512).transpose(1, 0, 2).reshape(P, 1024)
    d["conv_w"] = f["b_conv_w"].reshape(3, WC, P).transpose(2, 0, 1).reshape(P, 12)
    d["d_and_glu_b"] = np.concatenate([f["a_d"].reshape(WC, P).T, f["a_glu_b"].reshape(WC, P).T], 1)
    d["c_ws"] = f["c_ws"].transpose(2, 0, 1)
    d["c_bs"] = f["c_bs"].T
    for n in ("l0", "l1"):
        keys = np.stack([f[n + "_peer_k1"], f[n + "_peer_k2"]], 1).reshape(ROWS, KEYS, P)
        d[n + "_keys"] = keys.transpose(2, 0, 1).reshape(P, ROWS * KEYS)
        u = f[n + "_peer_u"].reshape(KEYS, SLICES, KC, P)
        d[n + "_peer_u"] = u.transpose(1, 3, 2, 0).reshape(SLICES, P, KC * KEYS)
    return {k: np.ascontiguousarray(v) for k, v in d.items()}


def kernel(**inputs):
    import numpy as _np
    import concourse.bacc as _bacc
    from concourse import mybir as _mybir
    from concourse.bass_utils import run_bass_kernel_spmd as _run

    nc = _bacc.Bacc("TRN2", target_bir_lowering=False, num_devices=1)
    arrays, aps = {}, {}
    for name, v in _layout(_np, inputs).items():
        arrays[f"in_{name}"] = v
        aps[name] = nc.dram_tensor(f"in_{name}", v.shape, _mybir.dt.from_np(v.dtype), kind="ExternalInput").ap()
    out = nc.dram_tensor("out_0", (SEQ, D), F32, kind="ExternalOutput").ap()
    trunk(nc, aps, out)
    r = _run(nc, [arrays], core_ids=[0])
    return r.results[0]["out_0"].reshape(1, SEQ, D)
```

```python
import concourse.bass as bass
from concourse import mybir
from contextlib import ExitStack

F32 = mybir.dt.float32
BF16 = mybir.dt.bfloat16
F32R = mybir.dt.float32r
U32 = mybir.dt.uint32
ALU = mybir.AluOpType
ACT = mybir.ActivationFunctionType
AXX = mybir.AxisListType.X

P = 128
SEQ = 256
TB = SEQ // P
D = 1024
KC = D // P
GROUP = 512
EVEN_IN = 2048
ODD_IN = 2560
WIDTH = 512
WC = WIDTH // P
S5_TILES = 2048 // P
S5_DVE_TILES = 11
HEADS = 8
ROWS = 2 * HEADS
KEYS = 128
TOPK = 16
CAND = TOPK * TOPK
PICKS = HEADS * TOPK
SLICES = 128
UNROLL = 4
GATE_TOKENS = 4
EARLY = 36
FIRST_PROJECTIONS = 9
POOL_TABLE_STEPS = 8 * 4 + 7 * 2
EPS = 1e-6
LOWEST = -3.0e38
NEVER = 1.0e30
TWO_PI = 6.283185307179586
TP1 = 6.28125
TP2 = 0.0019340515136718750
TP3 = TWO_PI - TP1 - TP2
ROUND = 12582912.0
PI_IN = 3.1415925


def trunk(nc, a, out):
    ctx = ExitStack()
    with ctx:
        def sb(name, shape, dt=F32):
            return ctx.enter_context(nc.sbuf_tensor(name, shape, dt))

        arena = sb("arena", [P, 32768])
        ring = sb("ring", [P, 8192])
        x = sb("x_res", [P, TB * D])
        h_parts = sb("h_parts", [P, KC * 2 * SEQ], F32R)
        u_parts = sb("u_parts", [P, 2 * D], F32R)
        v_parts = sb("v_parts", [P, 2 * D], F32R)
        w_parts = sb("w_parts", [P, 2 * 2 * SEQ], F32R)
        act_buf = sb("act_buf", [P, 2 * SEQ])
        low_buf = sb("low_buf", [P, SEQ])
        ident = sb("ident", [P, P])
        stat = sb("stat", [P, 64])
        psum = [ctx.enter_context(nc.psum_tensor(f"bank{i}", [P, 512], F32)) for i in range(8)]

        mem = dict(arena=arena, ring=ring, x=x, h_parts=h_parts, u_parts=u_parts, v_parts=v_parts,
                   w_parts=w_parts, act_buf=act_buf, low_buf=low_buf, ident=ident, stat=stat, psum=psum)
        made = {}

        def sem(name):
            if name not in made:
                made[name] = nc.alloc_semaphore(name)
            return made[name]

        def phase_over():
            nc.clear_and_free_semaphores(list(made.values()))
            nc.all_engine_barrier()
            made.clear()

        even_mixer(nc, a, mem, sem)
        phase_over()
        peer(nc, a, mem, sem, "l0")
        phase_over()
        odd_mixer(nc, a, mem, sem)
        phase_over()
        peer(nc, a, mem, sem, "l1")
        phase_over()
        final_norm(nc, a, mem, sem, out)


def ordered(eng, sem):
    count = [0]

    def link(ins):
        count[0] += 1
        ins.then_inc(sem, 1)
        eng.wait_ge(sem, count[0])
    return link



def norm_act(nc, act, mem, s, n, xn):
    for tb in range(TB):
        nc.scalar.activation(xn[:, tb * D:(tb + 1) * D], mem["x"][:, tb * D:(tb + 1) * D], ACT.Square,
                             accum_out=mem["stat"][:, tb:tb + 1]).then_inc(s(n + "_squares"), 1)
    act.wait_ge(s(n + "_meansq"), 1)
    nc.scalar.activation(mem["stat"][:, 4:6], mem["stat"][:, 2:4], ACT.Sqrt).then_inc(s(n + "_rms"), 1)


def norm_scale(nc, dve, mem, s, n, xn):
    stat = mem["stat"]
    dve.wait_ge(s(n + "_squares"), TB)
    nc.vector.tensor_scalar(stat[:, 2:4], stat[:, 0:2], 1.0 / D, EPS, ALU.mult, ALU.add)\
        .then_inc(s(n + "_meansq"), 1)
    dve.wait_ge(s(n + "_rms"), 1)
    nc.vector.reciprocal(stat[:, 6:8], stat[:, 4:6]).then_inc(s(n + "_rstd"), 1)
    dve.wait_ge(s(n + "_rstd"), 1)
    for tb in range(TB):
        nc.vector.tensor_scalar(xn[:, tb * D:(tb + 1) * D], mem["x"][:, tb * D:(tb + 1) * D],
                                stat[:, 6 + tb:7 + tb], None, ALU.mult).then_inc(s(n + "_xn"), 1)


def norm_pe(nc, pe, mem, s, n, xn):
    for tb in range(TB):
        pe.wait_ge(s(n + "_xn"), tb + 1)
        for c in range(KC):
            o = (c % 2) * SEQ + tb * P
            last = nc.tensor.transpose(mem["psum"][c // 2][:, o:o + P],
                                       xn[:, tb * D + c * P:tb * D + (c + 1) * P], mem["ident"][:, :])
    last.then_inc(s(n + "_turned"), 1)


def norm_gain(nc, dve, mem, s, n, hT, gain):
    dve.wait_ge(s(n + "_turned"), 1)
    for b in range(4):
        nc.vector.tensor_tensor(
            hT[:, 2 * b * SEQ:2 * (b + 1) * SEQ].rearrange("p (c t) -> p c t", c=2),
            mem["psum"][b][:, :].rearrange("p (c t) -> p c t", c=2),
            gain[:, 2 * b:2 * b + 2].unsqueeze(2).broadcast_to([P, 2, SEQ]), ALU.mult)\
            .then_inc(s(n + "_hT"), 1)



def weight_parts(mem):
    return [mem[k][:, :].rearrange("p (r n) -> p r n", r=2) for k in ("u_parts", "v_parts")]


def unit_high(nc, act, s, parts, j, halves):
    for hf in range(2):
        if j >= 2:
            act.wait_ge(s("unit_used"), 2 * j - 3 + hf)
        out = parts[j % 2][:, 0, 512 * hf:512 * (hf + 1)]
        if len(halves[hf].shape) == 3:
            out = out.rearrange("p (c e) -> p c e", c=4)
        nc.scalar.activation(out, halves[hf], ACT.Copy).then_inc(s("unit_high"), 1)


def unit_low(nc, dve, s, parts, j, halves):
    for hf in range(2):
        dve.wait_ge(s("unit_high"), 2 * j + hf + 1)
        high, low = (parts[j % 2][:, r, 512 * hf:512 * (hf + 1)] for r in range(2))
        if len(halves[hf].shape) == 3:
            high, low = (o.rearrange("p (c e) -> p c e", c=4) for o in (high, low))
        nc.vector.tensor_tensor(low, halves[hf], high.bitcast(F32), ALU.subtract).then_inc(s("unit_split"), 1)


def feature_major_unit(nc, pe, s, parts, h_parts, j, bank):
    w = parts[j % 2].rearrange("p r (c e) -> p r c e", c=KC)
    for hf in range(2):
        if j == 0:
            pe.wait_ge(s("h_low"), 2 * hf + 2)
        pe.wait_ge(s("unit_split"), 2 * j + hf + 1)
        for c in range(4 * hf, 4 * hf + 4):
            nc.tensor.matmul(bank, w[:, 0, c], h_parts[:, c, 0], start=(c == 0), stop=False)
            nc.tensor.matmul(bank, w[:, 0, c], h_parts[:, c, 1], start=False, stop=False)
            last = nc.tensor.matmul(bank, w[:, 1, c], h_parts[:, c, 0], start=False, stop=(c == KC - 1))
        last.then_inc(s("unit_used"), 1)


def token_major_unit(nc, pe, s, parts, h_parts, j, quarter, banks):
    for hf in range(2):
        c = 2 * quarter + hf
        if j < 4:
            pe.wait_ge(s("h_low"), quarter + 1)
        pe.wait_ge(s("unit_split"), 2 * j + hf + 1)
        w = [parts[j % 2][:, r, 512 * hf:512 * (hf + 1)] for r in range(2)]
        for tb in range(TB):
            t = slice(tb * P, (tb + 1) * P)
            nc.tensor.matmul(banks[tb][:, :], h_parts[:, c, 0, t], w[0], start=(c == 0), stop=False)
            nc.tensor.matmul(banks[tb][:, :], h_parts[:, c, 0, t], w[1], start=False, stop=False)
            last = nc.tensor.matmul(banks[tb][:, :], h_parts[:, c, 1, t], w[0], start=False, stop=(c == KC - 1))
        last.then_inc(s("unit_used"), 1)


def h_high(nc, act, s, n, h_parts, hT):
    for b in range(4):
        act.wait_ge(s(n + "_hT"), b + 1)
        nc.scalar.activation(h_parts[:, 2 * b:2 * b + 2, 0], hT[:, 512 * b:512 * (b + 1)]
                             .rearrange("p (c t) -> p c t", c=2), ACT.Copy).then_inc(s("h_high"), 1)


def h_low(nc, dve, s, h_parts, hT):
    for b in range(4):
        dve.wait_ge(s("h_high"), b + 1)
        nc.vector.tensor_tensor(h_parts[:, 2 * b:2 * b + 2, 1],
                                hT[:, 512 * b:512 * (b + 1)].rearrange("p (c t) -> p c t", c=2),
                                h_parts[:, 2 * b:2 * b + 2, 0].bitcast(F32), ALU.subtract)\
            .then_inc(s("h_low"), 1)



def even_mixer(nc, a, mem, s):
    arena, ring, x, psum, ident = mem["arena"], mem["ring"], mem["x"], mem["psum"], mem["ident"]
    w_in = arena[:, 0:16384].rearrange("p (g k m) -> p g k m", g=4, k=KC)
    pT = arena[:, 16384:20480].rearrange("p (m t) -> p m t", t=SEQ)
    e_cos = arena[:, 20480:24576].rearrange("p (i t) -> p i t", t=SEQ)
    e_sin = arena[:, 24576:28672].rearrange("p (i t) -> p i t", t=SEQ)
    hT = arena[:, 28672:30720]
    xn = arena[:, 30720:32768]
    w_out = arena[:, 0:8192].rearrange("p (k m) -> p k m", k=KC)
    catT = hT.rearrange("p (m t) -> p m t", t=SEQ)
    b_re = ring[:, 0:512].rearrange("p (c n) -> p c n", c=WC)
    b_im = ring[:, 512:1024].rearrange("p (c n) -> p c n", c=WC)
    c_re = ring[:, 1024:1536].rearrange("p (i n) -> p i n", i=S5_TILES)
    c_im = ring[:, 1536:2048].rearrange("p (i n) -> p i n", i=S5_TILES)
    glu_w = ring[:, 2048:4096].rearrange("p (k m) -> p k m", k=WC)
    t1 = ring[:, 4096:6144]
    t2 = ring[:, 6144:8192]
    c_minus_re = t2[:, 0:512].rearrange("p (i n) -> p i n", i=S5_TILES)
    by_cos = [t1[:, 1024 * b:1024 * b + 512] for b in range(2)]
    by_sin = [t1[:, 1024 * b + 512:1024 * b + 1024] for b in range(2)]
    scanned = [xn[:, 1024 * b:1024 * b + 512] for b in range(2)]
    back_cos = [xn[:, 1024 * b + 512:1024 * b + 1024] for b in range(2)]
    back_sin = [t2[:, 512 + 512 * b:1024 + 512 * b] for b in range(2)]
    conv_z, conv_acc = t2[:, 1536:1536 + SEQ], t2[:, 1792:1792 + SEQ]

    def rotation_tables(tt, link, lo, hi, v1, v2):
        w = hi - lo
        pc, ps, pc2, ps2, tmp = (c[:, lo:hi] for c in (pw_cos, pw_sin, pw_cos2, pw_sin2, pw_tmp))
        n = 1
        while n < SEQ:
            wide = [P, w, n]
            bc, bs = pc.unsqueeze(2).broadcast_to(wide), ps.unsqueeze(2).broadcast_to(wide)
            u1, u2 = (v[:, 0:w * n].rearrange("p (i t) -> p i t", i=w) for v in (v1, v2))
            ec, es = e_cos[:, lo:hi], e_sin[:, lo:hi]
            tt(u1, ec[:, :, 0:n], bc, ALU.mult)
            link(tt(u2, es[:, :, 0:n], bs, ALU.mult))
            link(tt(ec[:, :, n:2 * n], u1, u2, ALU.subtract))
            tt(u1, ec[:, :, 0:n], bs, ALU.mult)
            link(tt(u2, es[:, :, 0:n], bc, ALU.mult))
            link(tt(es[:, :, n:2 * n], u1, u2, ALU.add))
            n *= 2
            if n < SEQ:
                tt(pc2, pc, pc, ALU.mult)
                tt(tmp, ps, ps, ALU.mult)
                link(tt(ps2, pc, ps, ALU.mult))
                tt(pc, pc2, tmp, ALU.subtract)
                link(tt(ps, ps2, ps2, ALU.add))

    def parts2(rows):
        return rows.rearrange("p (r t) -> p r t", r=2)
    small = mem["act_buf"]

    def col(i, n=S5_TILES):
        return small[:, 16 * i:16 * i + n]
    (lam_re, lam_im, dt, lrdt, mag, th, rev, turn, rem, sin, half, cos, a_im, den, nr, f_re, f_im,
     tmp1, tmp2, pw_cos, pw_sin, pw_cos2, pw_sin2, pw_tmp) = (col(i) for i in range(24))
    gain = small[:, 408:408 + KC]
    conv_w = small[:, 384:396].rearrange("p (k c) -> p k c", k=3)
    d_skip = small[:, 400:404]
    glu_b = small[:, 404:408]

    with nc.Block() as block:
        @block.sync
        def _(sp):
            sp.dma_start(x[:, :].rearrange("p (b d) -> p b d", b=TB),
                         a["x"].rearrange("(b p) d -> p b d", p=P)).then_inc(s("x_in"), 16)
            sp.dma_start(small[:, 0:48], a["s5_params"]).then_inc(s("s5_params_in"), 16)
            sp.dma_start(gain, a["l0_norm_mix_g"]).then_inc(s("gain0_in"), 16)
            src = a["l0_w_in"].rearrange("(k p) (g m) -> g p k m", p=P, g=4)
            for g in range(4):
                sp.dma_start(w_in[:, g], src[g]).then_inc(s(f"w_in0_{g}"), 16)
            sp.dma_start(ring[:, 0:1024], a["s5_b"]).then_inc(s("s5_b_in"), 16)
            sp.dma_start(ring[:, 1024:2048], a["s5_c"]).then_inc(s("s5_c_in"), 16)
            sp.dma_start(small[:, 384:396], a["conv_w"]).then_inc(s("conv_w_in"), 16)
            sp.dma_start(small[:, 400:408], a["d_and_glu_b"]).then_inc(s("d_in"), 16)
            sp.dma_start(glu_w, a["a_glu_w"].rearrange("(k p) m -> p k m", p=P)).then_inc(s("glu_w_in"), 16)
            sp.wait_ge(s("proj0"), 8)
            sp.dma_start(w_out, a["l0_w_out"].rearrange("(k p) m -> p k m", p=P)).then_inc(s("w_out0_in"), 16)

        @block.gpsimd
        def _(pool):
            nc.gpsimd.memset(ident[:, :], 0.0).then_inc(s("ident_zero"), 1)
            pool.wait_ge(s("ident_zero"), 1)
            nc.gpsimd.affine_select(out=ident[:, :], in_=ident[:, :], compare_op=ALU.not_equal, fill=1.0,
                                    base=0, pattern=[[-1, P]], channel_multiplier=1)\
                .then_inc(s("ident_made"), 1)
            lo, hi = S5_DVE_TILES, S5_TILES
            pool.wait_ge(s("s5_powers"), 1)
            rotation_tables(nc.gpsimd.tensor_tensor, ordered(pool, s("pool_tables_order")), lo, hi,
                            t1[:, 1408:2048], t2[:, 1408:2048])
            pool.wait_ge(s("e_tables"), 1)
            for i in range(S5_TILES):
                pool.wait_ge(s("s5_scanned"), 2 * i + 2)
                if i >= 2:
                    pool.wait_ge(s("s5_y"), i - 1)
                for out, table in ((back_cos[i % 2], e_cos), (back_sin[i % 2], e_sin)):
                    nc.gpsimd.tensor_tensor(parts2(out), parts2(scanned[i % 2]),
                                            table[:, i].unsqueeze(1).broadcast_to([P, 2, SEQ]), ALU.mult)\
                        .then_inc(s("s5_turned"), 1)

        @block.scalar
        def _(act):
            act.wait_ge(s("x_in"), 16)
            norm_act(nc, act, mem, s, "n0", xn)
            act.wait_ge(s("s5_params_in"), 16)
            nc.scalar.activation(dt, dt, ACT.Exp).then_inc(s("s5_dt"), 1)
            act.wait_ge(s("s5_angles"), 1)
            nc.scalar.activation(mag, lrdt, ACT.Exp).then_inc(s("s5_mag"), 1)
            nc.scalar.activation(sin, rem, ACT.Sin).then_inc(s("s5_sin"), 1)
            nc.scalar.activation(half, rem, ACT.Sin, scale=0.5).then_inc(s("s5_sin"), 1)
            for b in range(8):
                act.wait_ge(s("proj0"), b + 1)
                nc.scalar.activation(pT[:, 2 * b:2 * b + 2], psum[b % 2][:, :].rearrange("p (m t) -> p m t", m=2),
                                     ACT.Copy).then_inc(s("pT"), 1)
            for c in range(WC):
                act.wait_ge(s("s5_skip"), c + 1)
                nc.scalar.activation(pT[:, c], pT[:, c], ACT.Gelu_apprx_tanh).then_inc(s("s5_gelu"), 1)
            for c in range(WC):
                act.wait_ge(s("glu"), c + 1)
                nc.scalar.activation(t1[:, c * SEQ:(c + 1) * SEQ], psum[c][:, 0:SEQ], ACT.Sigmoid,
                                     bias=glu_b[:, c:c + 1]).then_inc(s("glu_sig"), 1)

        @block.vector
        def _(dve):
            link = ordered(dve, s("even_dve_order"))
            tt, ts = nc.vector.tensor_tensor, nc.vector.tensor_scalar
            dve.wait_ge(s("x_in"), 16)
            norm_scale(nc, dve, mem, s, "n0", xn)
            dve.wait_ge(s("s5_dt"), 1)
            link(tt(lrdt, lam_re, dt, ALU.mult))
            link(tt(th, lam_im, dt, ALU.mult))
            link(ts(rev, th, 1.0 / TWO_PI, ROUND, ALU.mult, ALU.add))
            link(ts(turn, rev, -ROUND, None, ALU.add))
            link(nc.vector.scalar_tensor_tensor(rem, turn, -TP1, th, ALU.mult, ALU.add))
            link(nc.vector.scalar_tensor_tensor(rem, turn, -TP2, rem, ALU.mult, ALU.add))
            link(nc.vector.scalar_tensor_tensor(rem, turn, -TP3, rem, ALU.mult, ALU.add))
            ts(rem, rem, PI_IN, -PI_IN, ALU.min, ALU.max).then_inc(s("s5_angles"), 1)
            norm_needs_gain = s("gain0_in")
            dve.wait_ge(norm_needs_gain, 16)
            norm_gain(nc, dve, mem, s, "n0", hT, gain)
            dve.wait_ge(s("s5_mag"), 1)
            dve.wait_ge(s("s5_sin"), 2)
            link(tt(cos, half, half, ALU.mult))
            link(ts(cos, cos, -2.0, 1.0, ALU.mult, ALU.add))
            link(tt(nr, mag, cos, ALU.mult))
            link(ts(nr, nr, -1.0, None, ALU.add))
            link(tt(a_im, mag, sin, ALU.mult))
            link(tt(tmp1, lam_re, lam_re, ALU.mult))
            link(tt(tmp2, lam_im, lam_im, ALU.mult))
            link(tt(den, tmp1, tmp2, ALU.add))
            link(nc.vector.reciprocal(den, den))
            link(tt(tmp1, nr, lam_re, ALU.mult))
            link(tt(tmp2, a_im, lam_im, ALU.mult))
            link(tt(tmp1, tmp1, tmp2, ALU.add))
            link(tt(f_re, tmp1, den, ALU.mult))
            link(tt(tmp1, a_im, lam_re, ALU.mult))
            link(tt(tmp2, nr, lam_im, ALU.mult))
            link(tt(tmp1, tmp1, tmp2, ALU.subtract))
            link(tt(f_im, tmp1, den, ALU.mult))
            nc.vector.memset(e_cos[:, :, 0:1], 1.0)
            link(nc.vector.memset(e_sin[:, :, 0:1], 0.0))
            link(nc.vector.tensor_copy(pw_cos, cos))
            link(nc.vector.tensor_copy(pw_sin, sin))
            nc.vector.tensor_copy(tmp1, tmp2).then_inc(s("s5_powers"), 1)
            rotation_tables(tt, link, 0, S5_DVE_TILES, t1[:, 0:1408], t2[:, 0:1408])
            dve.wait_ge(s("s5_c_in"), 16)
            fr = f_re.unsqueeze(2).broadcast_to([P, S5_TILES, 32])
            fi = f_im.unsqueeze(2).broadcast_to([P, S5_TILES, 32])
            q1, q2 = (t1[:, 512 * n:512 * (n + 1)].rearrange("p (i n) -> p i n", i=S5_TILES) for n in range(2))
            q3, q4 = (t2[:, 512 * n:512 * (n + 1)].rearrange("p (i n) -> p i n", i=S5_TILES) for n in range(2))
            tt(q1, c_re, fr, ALU.mult)
            tt(q2, c_im, fi, ALU.mult)
            tt(q3, c_re, fi, ALU.mult)
            link(tt(q4, c_im, fr, ALU.mult))
            link(tt(c_re, q1, q2, ALU.subtract))
            link(tt(q3, q3, q4, ALU.add))
            link(ts(c_im, q3, -1.0, None, ALU.mult))
            ts(c_minus_re, c_re, -1.0, None, ALU.mult).then_inc(s("s5_c_scaled"), 1)
            nc.vector.tensor_copy(tmp1, tmp2).then_inc(s("e_tables"), 1)
            dve.wait_ge(s("s5_c_scaled"), 1)
            dve.wait_ge(s("pool_tables_order"), POOL_TABLE_STEPS)
            for i in range(S5_TILES):
                m1, m2, g = by_cos[i % 2], by_sin[i % 2], scanned[i % 2]
                dve.wait_ge(s("s5_bu"), i + 1)
                bu = parts2(psum[2 + i % 2][:, :])
                tt(parts2(m1), bu, e_cos[:, i].unsqueeze(1).broadcast_to([P, 2, SEQ]), ALU.mult)\
                    .then_inc(s("s5_bu_used"), 1)
                tt(parts2(m2), bu, e_sin[:, i].unsqueeze(1).broadcast_to([P, 2, SEQ]), ALU.mult)\
                    .then_inc(s("s5_bu_used"), 1)
                dve.wait_ge(s("s5_bu_used"), 2 * i + 2)
                tt(m1[:, 0:SEQ], m1[:, 0:SEQ], m2[:, SEQ:], ALU.add)
                link(tt(m1[:, SEQ:], m1[:, SEQ:], m2[:, 0:SEQ], ALU.subtract))
                if i >= 2:
                    dve.wait_ge(s("s5_turned"), 2 * (i - 1))
                decay = mag[:, i:i + 1].broadcast_to([P, SEQ])
                for r in range(2):
                    nc.vector.tensor_tensor_scan(g[:, r * SEQ:(r + 1) * SEQ], decay,
                                                 m1[:, r * SEQ:(r + 1) * SEQ], 0.0, ALU.mult, ALU.add)\
                        .then_inc(s("s5_scanned"), 1)
                if i >= 12:
                    c = i - 12
                    if c == 0:
                        dve.wait_ge(s("pT"), 8)
                        dve.wait_ge(s("conv_w_in"), 16)
                    z, acc = conv_z, conv_acc
                    link(tt(z, pT[:, 8 + c], pT[:, 12 + c], ALU.mult))
                    link(ts(acc, z, conv_w[:, 2, c:c + 1], None, ALU.mult))
                    link(nc.vector.scalar_tensor_tensor(acc[:, 1:], z[:, 0:SEQ - 1], conv_w[:, 1, c:c + 1],
                                                        acc[:, 1:], ALU.mult, ALU.add))
                    link(nc.vector.scalar_tensor_tensor(acc[:, 2:], z[:, 0:SEQ - 2], conv_w[:, 0, c:c + 1],
                                                        acc[:, 2:], ALU.mult, ALU.add))
                    link(tt(catT[:, WC + c], acc, pT[:, 4 + c], ALU.mult))
            dve.wait_ge(s("d_in"), 16)
            for c in range(WC):
                dve.wait_ge(s("s5_y"), 4 * c + 4)
                nc.vector.scalar_tensor_tensor(pT[:, c], pT[:, c], d_skip[:, c:c + 1], psum[4 + c][:, 0:SEQ],
                                               ALU.mult, ALU.add).then_inc(s("s5_skip"), 1)
            for c in range(WC):
                dve.wait_ge(s("glu_sig"), c + 1)
                dve.wait_ge(s("s5_gelu"), WC)
                tt(catT[:, c], pT[:, c], t1[:, c * SEQ:(c + 1) * SEQ], ALU.mult)\
                    .then_inc(s("catT0"), 1)
            for n in range(4):
                dve.wait_ge(s("mixed0"), n + 1)
                xs = x[:, n * 512:(n + 1) * 512]
                tt(xs, xs, psum[4 + n][:, :], ALU.add).then_inc(s("x_after_mix0"), 1)
            dve.wait_ge(s("x_after_mix0"), 4)

        @block.tensor
        def _(pe):
            pe.wait_ge(s("ident_made"), 1)
            norm_pe(nc, pe, mem, s, "n0", xn)
            pe.wait_ge(s("n0_hT"), 4)

            def project(m):
                if m % 4 == 0:
                    pe.wait_ge(s(f"w_in0_{m // 4}"), 16)
                if m % 2 == 0 and m >= 4:
                    pe.wait_ge(s("pT"), m // 2 - 1)
                for k in range(KC):
                    last = nc.tensor.matmul(psum[m // 2 % 2][:, (m % 2) * SEQ:(m % 2 + 1) * SEQ],
                                            w_in[:, m // 4, k, (m % 4) * P:(m % 4 + 1) * P],
                                            hT[:, k * SEQ:(k + 1) * SEQ], start=(k == 0), stop=(k == KC - 1))
                if m % 2:
                    last.then_inc(s("proj0"), 1)

            def product_in(i):
                c, j = i // 4, i % 4
                if i >= 2:
                    pe.wait_ge(s("s5_bu_used"), 2 * (i - 1))
                for r, b in enumerate((b_re, b_im)):
                    last = nc.tensor.matmul(psum[2 + i % 2][:, r * SEQ:(r + 1) * SEQ], b[32 * j:32 * j + 32, c, :],
                                            pT[32 * j:32 * j + 32, c, :], start=True, stop=True)
                last.then_inc(s("s5_bu"), 1)

            def product_out(i):
                c, j = i // 4, i % 4
                pe.wait_ge(s("s5_turned"), 2 * i + 2)
                g_cos, g_sin = back_cos[i % 2], back_sin[i % 2]
                terms = ((c_re, g_cos[:, 0:SEQ]), (c_minus_re, g_sin[:, SEQ:]),
                         (c_im, g_cos[:, SEQ:]), (c_im, g_sin[:, 0:SEQ]))
                for n, (weight, rows) in enumerate(terms):
                    last = nc.tensor.matmul(psum[4 + c][32 * j:32 * j + 32, 0:SEQ], weight[:, i, :], rows,
                                            start=(n == 0), stop=(n == 3))
                last.then_inc(s("s5_y"), 1)

            for m in range(FIRST_PROJECTIONS):
                project(m)
            pe.wait_ge(s("s5_b_in"), 16)
            pe.wait_ge(s("pT"), 2)
            for i in range(S5_TILES + 2):
                if i < S5_TILES:
                    product_in(i)
                if FIRST_PROJECTIONS + i < 16:
                    project(FIRST_PROJECTIONS + i)
                if i == 1:
                    pe.wait_ge(s("s5_c_scaled"), 1)
                if i >= 2:
                    product_out(i - 2)
            pe.wait_ge(s("glu_w_in"), 16)
            pe.wait_ge(s("s5_gelu"), WC)
            for m in range(WC):
                for k in range(WC):
                    last = nc.tensor.matmul(psum[m][:, 0:SEQ], glu_w[:, k, m * P:(m + 1) * P], pT[:, k, :],
                                            start=(k == 0), stop=(k == WC - 1))
                last.then_inc(s("glu"), 1)
            pe.wait_ge(s("w_out0_in"), 16)
            pe.wait_ge(s("catT0"), WC)
            for n in range(4):
                tb, half = n // 2, n % 2
                for k in range(KC):
                    last = nc.tensor.matmul(psum[4 + n][:, :], catT[:, k, tb * P:(tb + 1) * P],
                                            w_out[:, k, half * 512:(half + 1) * 512],
                                            start=(k == 0), stop=(k == KC - 1))
                last.then_inc(s("mixed0"), 1)



def heads_of(arena, at, size):
    return arena[:, at:at + size]


def scratch_of(arena, at, span):
    return [arena[:, at + h * span:at + (h + 1) * span] for h in range(HEADS)]


def two_blocks(scores):
    return scores.rearrange("p (b t) -> p b t", b=3)[:, 0:3:2]


def odd_mixer(nc, a, mem, s):
    arena, ring, x, psum, ident = mem["arena"], mem["ring"], mem["x"], mem["psum"], mem["ident"]
    w_in = arena[:, 0:20480].rearrange("p (g k m) -> p g k m", g=5, k=KC)
    u = arena[:, 20480:21504]
    v = arena[:, 21504:22528]
    vals = arena[:, 22528:23552]
    qT = arena[:, 23552:24576].rearrange("p (c t) -> p c t", t=SEQ)
    kT = arena[:, 24576:25600].rearrange("p (c t) -> p c t", t=SEQ)
    ws = arena[:, 25600:26624].rearrange("p (h t) -> p h t", h=HEADS)
    catT = arena[:, 26624:28672].rearrange("p (m t) -> p m t", t=SEQ)
    hT = arena[:, 28672:30720]
    xn = arena[:, 30720:32768]
    w_out = arena[:, 0:8192].rearrange("p (k m) -> p k m", k=KC)
    vgain = ring[:, 0:512]
    before = ring[:, 512:640]
    tri = ring[:, 640:768]
    ones = ring[:, 768:896]
    never = ring[:, 896:1024]
    units = weight_parts(mem)
    h_parts = mem["h_parts"][:, :].rearrange("p (c r t) -> p c r t", c=KC, r=2)

    def w_unit(j):
        g, m = j // 4, j % 4
        if g in (2, 3):
            return [w_in[:, g, 4 * hf:4 * (hf + 1), m * P:(m + 1) * P] for hf in range(2)]
        return [w_in[:, g, 2 * m + hf, :] for hf in range(2)]
    U_DONE, V_DONE, Q_DONE, K_DONE, VALS_DONE = (8 * (g + 1) for g in range(5))
    SPAN = SEQ + P
    z = scratch_of(arena, 8192, SPAN)
    soft = scratch_of(arena, 8192 + HEADS * SPAN, SPAN)
    sq = ring[:, 2048:3072]
    small = mem["act_buf"]
    gain = small[:, 0:KC]
    bias = small[:, 16:16 + HEADS]
    stat = mem["stat"]


    with nc.Block() as block:
        @block.sync
        def _(sp):
            sp.dma_start(gain, a["l1_norm_mix_g"]).then_inc(s("gain2_in"), 16)
            src = a["l1_w_in"].rearrange("(k p) (g m) -> g p k m", p=P, g=5)
            for g in range(5):
                sp.dma_start(w_in[:, g], src[g]).then_inc(s(f"w_in1_{g}"), 16)
            sp.dma_start(vgain, a["c_vnorm_g"].partition_broadcast(P)).then_inc(s("vgain_in"), 16)
            sp.dma_start(ws, a["c_ws"]).then_inc(s("ws_in"), 16)
            sp.dma_start(bias, a["c_bs"]).then_inc(s("bias_in"), 16)
            sp.wait_ge(s("unit_used"), V_DONE)
            sp.dma_start(w_out, a["l1_w_out"].rearrange("(k p) m -> p k m", p=P)).then_inc(s("w_out1_in"), 16)

        @block.gpsimd
        def _(pool):
            nc.gpsimd.memset(ring[:, 512:896], 1.0).then_inc(s("masks_filled"), 1)
            nc.gpsimd.memset(never, 0.0).then_inc(s("masks_filled"), 1)
            pool.wait_ge(s("masks_filled"), 2)
            for m, fill, base, query, key in ((before, 0.0, -1, 1, -1), (never, NEVER, -1, 1, -1), (tri, 0.0, 0, -1, 1)):
                nc.gpsimd.affine_select(out=m, in_=m, compare_op=ALU.is_ge, fill=fill, base=base,
                                        pattern=[[query, P]], channel_multiplier=key)\
                    .then_inc(s("masks_made"), 1)
            pool.wait_ge(s("ws_in"), 16)
            nc.gpsimd.affine_select(out=ws, in_=ws, compare_op=ALU.is_ge, fill=0.0,
                                    base=0, pattern=[[0, HEADS], [1, P]], channel_multiplier=-1)\
                .then_inc(s("ws_masked"), 1)

        @block.scalar
        def _(act):
            norm_act(nc, act, mem, s, "n2", xn)

            def highs(lo, hi):
                for j in range(lo, hi):
                    if j % 4 == 0:
                        act.wait_ge(s(f"w_in1_{j // 4}"), 16)
                    unit_high(nc, act, s, units, j, w_unit(j))

            def copy_pair(done, sem, out, bank, b, scale):
                act.wait_ge(s("unit_used"), done - 4 + 4 * b)
                nc.scalar.activation(out[:, 2 * b:2 * b + 2], psum[bank + b][:, :].rearrange("p (c t) -> p c t", c=2),
                                     ACT.Copy, scale=scale).then_inc(s(sem), 1)
            highs(0, 1)
            h_high(nc, act, s, "n2", h_parts, hT)
            highs(1, 6)
            act.wait_ge(s("unit_used"), U_DONE)
            for tb in range(TB):
                nc.scalar.activation(u[:, tb * 512:(tb + 1) * 512], psum[4 + tb][:, :],
                                     ACT.Gelu_apprx_tanh).then_inc(s("u_gelu"), 1)
            highs(6, 10)
            act.wait_ge(s("unit_used"), V_DONE)
            for tb in range(TB):
                nc.scalar.activation(v[:, tb * 512:(tb + 1) * 512], psum[6 + tb][:, :],
                                     ACT.Gelu_apprx_tanh).then_inc(s("v_gelu"), 1)
            highs(10, 11)
            act.wait_ge(s("v_gelu"), TB)
            for tb in range(TB):
                nc.scalar.activation(sq[:, tb * 512:(tb + 1) * 512], v[:, tb * 512:(tb + 1) * 512], ACT.Square,
                                     accum_out=stat[:, 16 + tb:17 + tb]).then_inc(s("v_squares"), 1)
            highs(11, 12)
            copy_pair(Q_DONE, "qT", qT, 0, 0, 0.125)
            highs(12, 13)
            act.wait_ge(s("v_meansq"), 1)
            nc.scalar.activation(stat[:, 20:22], stat[:, 18:20], ACT.Sqrt).then_inc(s("v_rms"), 1)
            highs(13, 14)
            copy_pair(Q_DONE, "qT", qT, 0, 1, 0.125)
            highs(14, 16)
            copy_pair(K_DONE, "kT", kT, 2, 0, 1.0)
            highs(16, 18)
            copy_pair(K_DONE, "kT", kT, 2, 1, 1.0)
            highs(18, 20)
            act.wait_ge(s("unit_used"), VALS_DONE)
            for tb in range(TB):
                nc.scalar.activation(vals[:, tb * 512:(tb + 1) * 512], psum[4 + tb][:, :],
                                     ACT.Copy).then_inc(s("vals"), 1)
            for h in range(HEADS):
                act.wait_ge(s("sb_z"), h + 1)
                nc.scalar.activation(z[h], psum[h % 2][:, 0:SPAN], ACT.Copy).then_inc(s("sb_z_copied"), 1)
            for h in range(0, HEADS, 4):
                act.wait_ge(s("sb_abs"), h + 4)
                e = heads_of(arena, 8192 + (HEADS + h) * SPAN, 4 * SPAN)
                nc.scalar.activation(e, e, ACT.Exp, scale=-1.0).then_inc(s("sb_exp_abs"), 1)
            for h in range(0, HEADS, 4):
                act.wait_ge(s("sb_exp_abs"), h // 4 + 1)
                e = heads_of(arena, 8192 + (HEADS + h) * SPAN, 4 * SPAN)
                nc.scalar.activation(e, e, ACT.Ln, bias=1.0).then_inc(s("sb_ln"), 1)
            for h in range(HEADS):
                act.wait_ge(s("sb_arg"), h + 1)
                nc.scalar.activation(z[h], z[h], ACT.Exp).then_inc(s("sb_w"), 1)
            for c in range(WC):
                act.wait_ge(s("sb_o"), 2 * c + 2)
                nc.scalar.activation(catT[:, WC + c], psum[4 + c][:, 0:SEQ], ACT.Copy).then_inc(s("sb_out"), 1)

        @block.vector
        def _(dve):
            link = ordered(dve, s("odd_dve_order"))
            tt, ts, stt = nc.vector.tensor_tensor, nc.vector.tensor_scalar, nc.vector.scalar_tensor_tensor
            norm_scale(nc, dve, mem, s, "n2", xn)
            dve.wait_ge(s("gain2_in"), 16)
            norm_gain(nc, dve, mem, s, "n2", hT, gain)

            def lows(lo, hi):
                for j in range(lo, hi):
                    unit_low(nc, dve, s, units, j, w_unit(j))
            lows(0, 1)
            dve.wait_ge(s("n2_hT"), 4)
            h_low(nc, dve, s, h_parts, hT)
            lows(1, 12)
            dve.wait_ge(s("v_squares"), TB)
            ts(stat[:, 18:20], stat[:, 16:18], 1.0 / WIDTH, EPS, ALU.mult, ALU.add).then_inc(s("v_meansq"), 1)
            lows(12, 14)
            dve.wait_ge(s("v_rms"), 1)
            link(nc.vector.reciprocal(stat[:, 22:24], stat[:, 20:22]))
            dve.wait_ge(s("vgain_in"), 16)
            for tb in range(TB):
                vs = v[:, tb * 512:(tb + 1) * 512]
                stt(vs, vs, stat[:, 22 + tb:23 + tb], vgain, ALU.mult, ALU.mult).then_inc(s("v_normed"), 1)
            lows(14, 20)
            for h in range(HEADS):
                dve.wait_ge(s("sb_z_copied"), h + 1)
                if h == 0:
                    dve.wait_ge(s("unit_used"), VALS_DONE)
                stt(soft[h], z[h], -1.0, z[h], ALU.mult, ALU.max).then_inc(s("sb_abs"), 1)
            dve.wait_ge(s("bias_in"), 16)
            dve.wait_ge(s("u_gelu"), TB)
            for tb in range(TB):
                dve.wait_ge(s("spatial"), tb + 1)
                us = u[:, tb * 512:(tb + 1) * 512]
                y = sq[:, tb * 512:(tb + 1) * 512]
                link(tt(y.rearrange("p (h d) -> p h d", h=HEADS),
                        psum[6 + tb][:, :].rearrange("p (h d) -> p h d", h=HEADS),
                        bias.unsqueeze(2).broadcast_to([P, HEADS, 64]), ALU.add))
                tt(us, us, y, ALU.mult).then_inc(s("gmlp"), 1)
            dve.wait_ge(s("gmlp_turned"), 1)
            for b in range(2):
                nc.vector.tensor_copy(catT[:, 2 * b:2 * b + 2],
                                      psum[2 + b][:, :].rearrange("p (c t) -> p c t", c=2))\
                    .then_inc(s("catT1"), 1)
            dve.wait_ge(s("masks_made"), 3)
            for h in range(HEADS):
                dve.wait_ge(s("sb_ln"), h // 4 + 1)
                stt(soft[h], z[h], 0.0, soft[h], ALU.max, ALU.add).then_inc(s("sb_softplus"), 1)
                dve.wait_ge(s("sb_softplus"), 2 * h + 1)
                diagonal = two_blocks(soft[h])
                tt(diagonal, diagonal, before.unsqueeze(1).broadcast_to([P, 2, P]), ALU.mult)\
                    .then_inc(s("sb_softplus"), 1)
                if h >= 1:
                    dve.wait_ge(s("sb_sum"), h)
                    tt(z[h - 1], z[h - 1], psum[2 + (h - 1) % 2][:, 0:SPAN], ALU.subtract).then_inc(s("sb_arg"), 1)
            dve.wait_ge(s("sb_sum"), HEADS)
            tt(z[HEADS - 1], z[HEADS - 1], psum[3][:, 0:SPAN], ALU.subtract).then_inc(s("sb_arg"), 1)
            for n in range(4):
                dve.wait_ge(s("mixed1"), n + 1)
                xs = x[:, n * 512:(n + 1) * 512]
                tt(xs, xs, psum[n][:, :], ALU.add).then_inc(s("x_after_mix1"), 1)
            dve.wait_ge(s("x_after_mix1"), 4)

        @block.tensor
        def _(pe):
            norm_pe(nc, pe, mem, s, "n2", xn)
            def token_major(g, bank):
                for m in range(4):
                    token_major_unit(nc, pe, s, units, h_parts, 4 * g + m, m, [psum[bank + tb] for tb in range(TB)])

            def feature_major(g, bank):
                for m in range(WC):
                    feature_major_unit(nc, pe, s, units, h_parts, 4 * g + m,
                                       psum[bank + m // 2][:, (m % 2) * SEQ:(m % 2 + 1) * SEQ])

            token_major(0, 4)
            token_major(1, 6)
            feature_major(2, 0)
            feature_major(3, 2)
            pe.wait_ge(s("u_gelu"), TB)
            token_major(4, 4)
            pe.wait_ge(s("qT"), 2)
            pe.wait_ge(s("kT"), 2)
            for h in range(HEADS):
                if h >= 2:
                    pe.wait_ge(s("sb_z_copied"), h - 1)
                r = 64 * (h % 2)
                nc.tensor.matmul(psum[h % 2][:, 0:SEQ], kT[r:r + 64, h // 2, 0:P], qT[r:r + 64, h // 2, :],
                                 start=True, stop=True)
                nc.tensor.matmul(psum[h % 2][:, SEQ:SPAN], kT[r:r + 64, h // 2, P:], qT[r:r + 64, h // 2, P:],
                                 start=True, stop=True).then_inc(s("sb_z"), 1)
            pe.wait_ge(s("ws_masked"), 1)
            for tb in range(TB):
                pe.wait_ge(s("v_normed"), tb + 1)
                for h in range(HEADS):
                    last = nc.tensor.matmul(psum[6 + tb][:, h * 64:(h + 1) * 64], ws[:, h, :],
                                            v[:, tb * 512 + h * 64:tb * 512 + (h + 1) * 64],
                                            start=True, stop=True)
                last.then_inc(s("spatial"), 1)
            for tb in range(TB):
                pe.wait_ge(s("gmlp"), tb + 1)
                for c in range(WC):
                    o = (c % 2) * SEQ + tb * P
                    last = nc.tensor.transpose(psum[2 + c // 2][:, o:o + P],
                                               u[:, tb * 512 + c * P:tb * 512 + (c + 1) * P], ident[:, :])
            last.then_inc(s("gmlp_turned"), 1)
            pe.wait_ge(s("vals"), TB)
            pe.wait_ge(s("masks_made"), 3)

            def sums(h):
                if h < 2:
                    pe.wait_ge(s("catT1"), 2)
                else:
                    pe.wait_ge(s("sb_arg"), h - 1)
                pe.wait_ge(s("sb_softplus"), 2 * h + 2)
                bank = psum[2 + h % 2]
                nc.tensor.matmul(bank[:, 0:SPAN], tri, soft[h], start=True, stop=False)
                nc.tensor.matmul(bank[:, P:SEQ], ones, soft[h][:, SEQ:], start=False, stop=False)
                nc.tensor.matmul(bank[:, 0:P], ident[:, :], never, start=False, stop=False)
                nc.tensor.matmul(bank[:, SEQ:SPAN], ident[:, :], never, start=False, stop=True)\
                    .then_inc(s("sb_sum"), 1)

            def outputs(h):
                c, r = h // 2, 64 * (h % 2)
                pe.wait_ge(s("sb_w"), h + 1)
                v0, v1 = (vals[:, b * 512 + h * 64:b * 512 + (h + 1) * 64] for b in range(2))
                nc.tensor.matmul(psum[4 + c][r:r + 64, 0:SEQ], v0, z[h][:, 0:SEQ], start=True, stop=False)
                nc.tensor.matmul(psum[4 + c][r:r + 64, P:SEQ], v1, z[h][:, SEQ:], start=False, stop=True)\
                    .then_inc(s("sb_o"), 1)

            for h in range(HEADS + 3):
                if h < HEADS:
                    sums(h)
                if h >= 3:
                    outputs(h - 3)
            pe.wait_ge(s("w_out1_in"), 16)
            pe.wait_ge(s("sb_out"), WC)
            pe.wait_ge(s("sb_arg"), HEADS)
            for n in range(4):
                tb, half = n // 2, n % 2
                for k in range(KC):
                    last = nc.tensor.matmul(psum[n][:, :], catT[:, k, tb * P:(tb + 1) * P],
                                            w_out[:, k, half * 512:(half + 1) * 512],
                                            start=(k == 0), stop=(k == KC - 1))
                last.then_inc(s("mixed1"), 1)



def peer(nc, a, mem, shared_sem, layer):
    def s(name):
        return shared_sem(f"{layer}_{name}")

    arena, ring, x, psum, ident = (mem[k] for k in ("arena", "ring", "x", "psum", "ident"))
    places = mem["stat"][:, 16:16 + TOPK]
    h_parts = mem["h_parts"][:, :].rearrange("p (c r t) -> p c r t", c=KC, r=2)
    u_parts = mem["u_parts"][:, :].rearrange("p (r c e) -> p r c e", r=2, c=KC)
    v_parts = mem["v_parts"][:, :].rearrange("p (r d) -> p r d", r=2)
    early_parts = [u_parts, mem["v_parts"][:, :].rearrange("p (r c e) -> p r c e", r=2, c=KC)]
    known_parts = [mem["u_parts"][:, :].rearrange("p (r d) -> p r d", r=2), v_parts]
    w_parts = mem["w_parts"][:, :].rearrange("p (b r t) -> p b r t", b=2, r=2)
    act_buf, low_buf = mem["act_buf"], mem["low_buf"]
    wq = arena[:, 0:16384].rearrange("p (g k m) -> p g k m", g=4, k=KC)
    units = weight_parts(mem)

    def query_unit(r):
        return [wq[:, r // 4, 4 * hf:4 * (hf + 1), (r % 4) * P:(r % 4 + 1) * P] for hf in range(2)]
    keysT = arena[:, 16384:18432].rearrange("p (r n) -> p r n", r=ROWS)
    qT = arena[:, 18432:22528].rearrange("p (r t) -> p r t", t=SEQ)
    scores = [arena[:, 22528 + 2048 * tb:24576 + 2048 * tb].rearrange("p (r n) -> p r n", r=ROWS)
              for tb in range(TB)]
    rest = arena[:, 26624:28672].rearrange("p (r n) -> p r n", r=ROWS)
    hT = arena[:, 28672:30720]
    xn = arena[:, 30720:32768]
    cand = arena[:, 16384:18432].rearrange("p (h c) -> p h c", h=HEADS)
    cand_rest = arena[:, 18432:20480].rearrange("p (h c) -> p h c", h=HEADS)
    eq = arena[:, 20480:22528]

    def small(i, n=128):
        return arena[:, 28672 + 128 * i:28672 + 128 * i + n]
    best = small(0, 256).rearrange("p (r k) -> p r k", r=ROWS)
    best_at = small(2, 256).bitcast(U32).rearrange("p (r k) -> p r k", r=ROWS)
    key_of = small(4, 256).rearrange("p (r k) -> p r k", r=ROWS)
    top = [small(6 + tb).rearrange("p (h k) -> p h k", h=HEADS) for tb in range(TB)]
    top_at = small(8).bitcast(U32).rearrange("p (h k) -> p h k", h=HEADS)
    part_at = small(9).bitcast(U32)
    part = small(10)
    total = [small(11 + tb, HEADS) for tb in range(TB)]
    choice = [[arena[:, 30720 + 384 * tb + 128 * n:30720 + 384 * tb + 128 * (n + 1)] for n in range(3)]
              for tb in range(TB)]
    pick_keys = act_buf[:, 0:SEQ].bitcast(BF16).rearrange("p (z t) -> p z t", z=2)
    pick_gate = low_buf[:, :]
    hot = [ring[:, 512 * b:512 * (b + 1)].bitcast(BF16).rearrange("p (z e t) -> p z e t", z=2, t=GATE_TOKENS)
           for b in range(2)]
    scaled = [ring[:, 2048 + 512 * b:2560 + 512 * b].rearrange("p (t e) -> p t e", t=GATE_TOKENS)
              for b in range(UNROLL)]
    one_hot = [ring[:, 1024 + 512 * b:1536 + 512 * b].rearrange("p (t e) -> p t e", t=GATE_TOKENS) for b in range(2)]
    iota = act_buf[:, SEQ:].bitcast(BF16).rearrange("p (e t) -> p e t", t=GATE_TOKENS)
    group_gate = [mem["stat"][:, 32 + GATE_TOKENS * b:32 + GATE_TOKENS * (b + 1)] for b in range(2)]
    gates = arena[:, :].rearrange("p (e t) -> p e t", t=SEQ)
    table_u = [ring[:, 1024 * n:1024 * (n + 1)] for n in range(UNROLL)]
    table_v = [ring[:, 4096 + 1024 * n:4096 + 1024 * (n + 1)] for n in range(UNROLL)]
    u_src = a[layer + "_peer_u"]
    v_src = a[layer + "_peer_v"].rearrange("(p e) d -> e p d", p=P)
    gain = act_buf[:, 0:KC]

    def fetch_u(sp, i, slot):
        sp.dma_start(table_u[slot], u_src[i]).then_inc(s(f"u_in_{slot}"), 16)

    def fetch_v(sp, i, slot):
        sp.dma_start(table_v[slot], v_src[i]).then_inc(s(f"v_in_{slot}"), 16)

    def u_high(act, i, turn, n, parts, lag, first=False):
        act.wait_ge(s(f"u_in_{n}"), turn * 16 + 16)
        for hf in range(2):
            if not first:
                act.wait_ge(s("u_used"), (i - lag) * 2 + 1 + hf)
            nc.scalar.activation(parts[:, 0, 4 * hf:4 * (hf + 1)],
                                 table_u[n][:, 512 * hf:512 * (hf + 1)].rearrange("p (c e) -> p c e", c=4),
                                 ACT.Copy).then_inc(s("u_high"), 1)

    def u_low(eng, tensor_tensor, i, hf, n, parts):
        eng.wait_ge(s("u_high"), i * 2 + hf + 1)
        cut = slice(4 * hf, 4 * (hf + 1))
        tensor_tensor(parts[:, 1, cut],
                      table_u[n][:, 512 * hf:512 * (hf + 1)].rearrange("p (c e) -> p c e", c=4),
                      parts[:, 0, cut].bitcast(F32), ALU.subtract).then_inc(s("u_split"), 1)

    with nc.Block() as block:
        @block.sync
        def _(sp):
            sp.dma_start(gain, a[layer + "_norm_ffn_g"]).then_inc(s("gain_in"), 16)
            src = a[layer + "_peer_wq"].rearrange("(k p) (g m) -> g p k m", p=P, g=4)
            for g in range(4):
                sp.dma_start(wq[:, g], src[g]).then_inc(s(f"wq_{g}"), 16)
            sp.dma_start(arena[:, 16384:18432], a[layer + "_keys"]).then_inc(s("keys_in"), 16)
            for n in range(UNROLL):
                fetch_u(sp, n, n)
            for n in range(UNROLL):
                fetch_v(sp, n, n)
            with sp.Fori(1, EARLY // UNROLL) as turn:
                for n in range(UNROLL):
                    sp.wait_ge(s("u_split"), (turn * UNROLL + n) * 2 - 2 * UNROLL + 2)
                    fetch_u(sp, turn * UNROLL + n, n)

        @block.gpsimd
        def _(pool):
            nc.gpsimd.iota(places, [[1, TOPK]], base=0, channel_multiplier=0,
                           allow_small_or_imprecise_dtypes=True).then_inc(s("places_made"), 1)
            with pool.Fori(0, EARLY // UNROLL) as turn:
                for n in range(UNROLL):
                    for hf in range(2):
                        u_low(pool, nc.gpsimd.tensor_tensor, turn * UNROLL + n, hf, n, early_parts[n % 2])

        @block.scalar
        def _(act):
            norm_act(nc, act, mem, s, "n", xn)
            act.wait_ge(s("wq_0"), 16)
            unit_high(nc, act, s, units, 0, query_unit(0))
            h_high(nc, act, s, "n", h_parts, hT)

            def copy_query(b):
                act.wait_ge(s("unit_used"), 4 * b + 4)
                nc.scalar.activation(qT[:, 2 * b:2 * b + 2], psum[b % 4][:, :].rearrange("p (r t) -> p r t", r=2),
                                     ACT.Copy).then_inc(s("qT"), 1)
            for r in range(1, ROWS):
                if r % 4 == 0:
                    act.wait_ge(s(f"wq_{r // 4}"), 16)
                unit_high(nc, act, s, units, r, query_unit(r))
                if r % 2 and r >= 3:
                    copy_query(r // 2 - 1)
            copy_query(ROWS // 2 - 1)
            for tb in range(TB):
                for b in range(4):
                    act.wait_ge(s("scored"), 4 * tb + b + 1)
                    nc.scalar.activation(scores[tb][:, 4 * b:4 * b + 4],
                                         psum[4 * (1 - tb) + b][:, :].rearrange("p (r n) -> p r n", r=4),
                                         ACT.Copy).then_inc(s("scores"), 1)
            def early(i, turn, n, first):
                u_high(act, i, turn, n, early_parts[n % 2], 2, first and n < 2)
                if not (first and n == 0):
                    early_gelu(i - 1, (n - 1) % UNROLL)

            def early_gelu(i, n):
                act.wait_ge(s("u_used"), i * 2 + 2)
                nc.scalar.activation(arena[:, bass.ds(i * SEQ, SEQ)], psum[4 + n % 2][:, 0:SEQ],
                                     ACT.Gelu_apprx_tanh).then_inc(s("early_acts"), 1)
            for n in range(UNROLL):
                early(n, 0, n, True)
            with act.Fori(1, EARLY // UNROLL) as turn:
                for n in range(UNROLL):
                    early(turn * UNROLL + n, turn, n, False)
            early_gelu(EARLY - 1, UNROLL - 1)
            for tb in range(TB):
                act.wait_ge(s("top_shifted"), tb + 1)
                nc.scalar.activation(top[tb], top[tb], ACT.Exp).then_inc(s("top_exp"), 1)

        @block.vector
        def _(dve):
            tt, ts = nc.vector.tensor_tensor, nc.vector.tensor_scalar
            link = ordered(dve, s("dve_order"))
            norm_scale(nc, dve, mem, s, "n", xn)
            dve.wait_ge(s("gain_in"), 16)
            norm_gain(nc, dve, mem, s, "n", hT, gain)
            dve.wait_ge(s("n_hT"), 4)
            unit_low(nc, dve, s, units, 0, query_unit(0))
            h_low(nc, dve, s, h_parts, hT)
            for r in range(1, ROWS):
                unit_low(nc, dve, s, units, r, query_unit(r))
            dve.wait_ge(s("places_made"), 1)
            dve.wait_ge(s("h_low"), 4)
            for tb in range(TB):
                def best16(n, src, left, val, at):
                    for r in range(n):
                        last = nc.vector.max(val[:, r, 0:8], src[:, r])
                    link(last)
                    for r in range(n):
                        nc.vector.max_index(at[:, r, 0:8], val[:, r, 0:8], src[:, r])
                        last = nc.vector.match_replace(left[:, r], val[:, r, 0:8], src[:, r], LOWEST)
                    link(last)
                    for r in range(n):
                        last = nc.vector.max(val[:, r, 8:16], left[:, r])
                    link(last)
                    for r in range(n):
                        last = nc.vector.max_index(at[:, r, 8:16], val[:, r, 8:16], left[:, r])
                    link(last)
                dve.wait_ge(s("scores"), 4 * tb + 4)
                best16(ROWS, scores[tb], rest, best, best_at)
                link(nc.vector.tensor_copy(key_of, best_at))
                if tb == 0:
                    dve.wait_ge(s("scored"), 8)
                halves = best.rearrange("p (h z) k -> p h z k", z=2)
                link(tt(cand.rearrange("p h (i j) -> p h i j", i=TOPK),
                        halves[:, :, 0].unsqueeze(3).broadcast_to([P, HEADS, TOPK, TOPK]),
                        halves[:, :, 1].unsqueeze(2).broadcast_to([P, HEADS, TOPK, TOPK]), ALU.add))
                best16(HEADS, cand, cand_rest, top[tb], top_at)
                keys = key_of.rearrange("p (h z) k -> p h z k", z=2)
                for z in range(2):
                    if z == 0:
                        link(ts(part_at, small(8).bitcast(U32), 4, None, ALU.logical_shift_right))
                    else:
                        link(ts(part_at, small(8).bitcast(U32), 15, None, ALU.bitwise_and))
                    link(nc.vector.tensor_copy(part, part_at))
                    eq4 = eq.rearrange("p (h k j) -> p h k j", h=HEADS, k=TOPK)
                    link(tt(eq4, part.rearrange("p (h k) -> p h k", h=HEADS).unsqueeze(3)
                            .broadcast_to([P, HEADS, TOPK, TOPK]),
                            places.unsqueeze(1).unsqueeze(1).broadcast_to([P, HEADS, TOPK, TOPK]),
                            ALU.is_equal))
                    link(tt(eq4, eq4, keys[:, :, z].unsqueeze(2).broadcast_to([P, HEADS, TOPK, TOPK]), ALU.mult))
                    link(nc.vector.tensor_reduce(choice[tb][z], eq.rearrange("p (n j) -> p n j", j=TOPK),
                                                 AXX, ALU.add))
                link(nc.vector.tensor_copy(total[tb], top[tb][:, :, 0]))
                tt(top[tb], top[tb], total[tb].unsqueeze(2).broadcast_to([P, HEADS, TOPK]), ALU.subtract)\
                    .then_inc(s("top_shifted"), 1)
            for tb in range(TB):
                dve.wait_ge(s("top_exp"), tb + 1)
                link(nc.vector.tensor_reduce(total[tb], top[tb], AXX, ALU.add))
                link(nc.vector.reciprocal(total[tb], total[tb]))
                tt(choice[tb][2].rearrange("p (h k) -> p h k", h=HEADS), top[tb],
                   total[tb].unsqueeze(2).broadcast_to([P, HEADS, TOPK]), ALU.mult).then_inc(s("chosen"), 1)
            dve.wait_ge(s("chosen"), TB)
            dve.wait_ge(s("choice_turned"), 1)
            nc.vector.tensor_copy(pick_keys, psum[0][:, :].rearrange("p (z t) -> p z t", z=2)).then_inc(s("picks"), 1)
            nc.vector.tensor_copy(pick_gate, psum[1][:, 0:SEQ]).then_inc(s("picks"), 1)

        @block.tensor
        def _(pe):
            norm_pe(nc, pe, mem, s, "n", xn)
            for r in range(ROWS):
                if r % 2 == 0 and r >= 8:
                    pe.wait_ge(s("qT"), r // 2 - 3)
                feature_major_unit(nc, pe, s, units, h_parts, r, psum[(r // 2) % 4][:, (r % 2) * SEQ:(r % 2 + 1) * SEQ])
            pe.wait_ge(s("keys_in"), 16)
            pe.wait_ge(s("qT"), 8)
            for tb in range(TB):
                for r in range(ROWS):
                    last = nc.tensor.matmul(psum[4 * (1 - tb) + r // 4][:, (r % 4) * P:(r % 4 + 1) * P],
                                            qT[:, r, tb * P:(tb + 1) * P], keysT[:, r, :], start=True, stop=True)
                    if r % 4 == 3:
                        last.then_inc(s("scored"), 1)
            pe.wait_ge(s("scores"), 8)
            pe.wait_ge(s("h_low"), 4)

            def early(i, n, first):
                if not first:
                    pe.wait_ge(s("early_acts"), i - 1)
                bank = psum[4 + n % 2][:, 0:SEQ]
                for hf in range(2):
                    pe.wait_ge(s("u_split"), i * 2 + hf + 1)
                    for c in range(4 * hf, 4 * hf + 4):
                        parts = early_parts[n % 2]
                        nc.tensor.matmul(bank, parts[:, 0, c], h_parts[:, c, 0], start=(c == 0), stop=False)
                        nc.tensor.matmul(bank, parts[:, 0, c], h_parts[:, c, 1], start=False, stop=False)
                        last = nc.tensor.matmul(bank, parts[:, 1, c], h_parts[:, c, 0],
                                                start=False, stop=(c == KC - 1))
                    last.then_inc(s("u_used"), 1)
            for n in range(UNROLL):
                early(n, n, n < 2)
            with pe.Fori(1, EARLY // UNROLL) as turn:
                for n in range(UNROLL):
                    early(turn * UNROLL + n, n, False)
            for tb in range(TB):
                pe.wait_ge(s("chosen"), tb + 1)
                for n in range(3):
                    o = (n % 2) * SEQ + tb * P
                    last = nc.tensor.transpose(psum[n // 2][:, o:o + P], choice[tb][n], ident[:, :])
            last.then_inc(s("choice_turned"), 1)

    GROUPS = SEQ // GATE_TOKENS
    with nc.Block() as block:
        def groups(eng, step):
            for n in range(UNROLL):
                step(n, n, True)
            with eng.Fori(1, GROUPS // UNROLL) as turn:
                for n in range(UNROLL):
                    step(turn * UNROLL + n, n, False)

        @block.gpsimd
        def _(pool):
            nc.gpsimd.iota(iota, [[1, KEYS], [0, GATE_TOKENS]], base=0, channel_multiplier=0,
                           allow_small_or_imprecise_dtypes=True).then_inc(s("iota_made"), 1)

            def scale_rows(g, b, first):
                pool.wait_ge(s("gate_staged"), g + 1)
                pool.wait_ge(s("hot_rows"), g + 1)
                if not first:
                    pool.wait_ge(s("gate_banks"), g - 3)
                nc.gpsimd.tensor_tensor(scaled[b], hot[b % 2][:, 0].rearrange("p e t -> p t e"),
                                        group_gate[b % 2].unsqueeze(2).broadcast_to([P, GATE_TOKENS, KEYS]),
                                        ALU.mult).then_inc(s("hot_scaled"), 1)
            groups(pool, scale_rows)

        @block.vector
        def _(dve):
            wide = [P, 2, KEYS, GATE_TOKENS]

            def merge(g, b):
                dve.wait_ge(s("gate_copied"), g + 1)
                here = gates[:, 0:EARLY, bass.ds(g * GATE_TOKENS, GATE_TOKENS)]
                nc.vector.tensor_tensor(here, psum[b][:, :].rearrange("p (t e) -> p e t", t=GATE_TOKENS)[:, 0:EARLY],
                                        here, ALU.mult).then_inc(s("gate_merged"), 1)

            def build(g, b, first):
                if not first:
                    merge(g - 4, b)
                if not first or b >= 2:
                    dve.wait_ge(s("hot_scaled"), g - 1)
                    dve.wait_ge(s("hot_widened"), g - 1)
                at = bass.ds(g * GATE_TOKENS, GATE_TOKENS)
                nc.vector.tensor_copy(group_gate[b % 2], pick_gate[:, at]).then_inc(s("gate_staged"), 1)
                nc.vector.tensor_tensor(hot[b % 2], pick_keys[:, :, at].unsqueeze(2).broadcast_to(wide),
                                        iota.unsqueeze(1).broadcast_to(wide), ALU.is_equal)\
                    .then_inc(s("hot_rows"), 1)
            dve.wait_ge(s("iota_made"), 1)
            groups(dve, build)
            for n in range(UNROLL):
                merge(GROUPS - UNROLL + n, n)

        @block.tensor
        def _(pe):
            def products(g, b, first):
                if not first:
                    pe.wait_ge(s("gate_merged"), g - 3)
                pe.wait_ge(s("hot_widened"), g + 1)
                pe.wait_ge(s("hot_scaled"), g + 1)
                for t in range(GATE_TOKENS):
                    last = nc.tensor.matmul(psum[b][:, t * P:(t + 1) * P], scaled[b][:, t],
                                            one_hot[b % 2][:, t], start=True, stop=True)
                last.then_inc(s("gate_banks"), 1)
            groups(pe, products)

        @block.scalar
        def _(act):
            def widen(g, b, first):
                if not first or b >= 2:
                    copy_out(g - 2, (b - 2) % UNROLL)
                act.wait_ge(s("hot_rows"), g + 1)
                nc.scalar.activation(one_hot[b % 2], hot[b % 2][:, 1].rearrange("p e t -> p t e"), ACT.Copy)\
                    .then_inc(s("hot_widened"), 1)

            def copy_out(g, b):
                act.wait_ge(s("gate_banks"), g + 1)
                nc.scalar.activation(gates[:, EARLY:, bass.ds(g * GATE_TOKENS, GATE_TOKENS)],
                                     psum[b][:, :].rearrange("p (t e) -> p e t", t=GATE_TOKENS)[:, EARLY:],
                                     ACT.Copy).then_inc(s("gate_copied"), 1)
            groups(act, widen)
            for n in range(UNROLL - 2, UNROLL):
                copy_out(GROUPS - UNROLL + n, n)

    with nc.Block() as block:
        def steps(eng, first, count, step):
            turns = range(first // UNROLL, (first + count) // UNROLL)
            for n in range(UNROLL):
                step(first + n, turns[0], n, True)
            with eng.Fori(turns[1], turns[-1]) as turn:
                for n in range(UNROLL):
                    step(turn * UNROLL + n, turn, n, False)
            for n in range(UNROLL):
                step(turns[-1] * UNROLL + n, turns[-1], n, True)

        @block.sync
        def _(sp):
            def fetch_v_when_free(i, n):
                sp.wait_ge(s("v_split"), i * 2 - 2 * UNROLL + 2)
                fetch_v(sp, i, n)
            for n in range(UNROLL):
                fetch_u(sp, EARLY + n, n)
            with sp.Fori(1, EARLY // UNROLL) as turn:
                for n in range(UNROLL):
                    fetch_v_when_free(turn * UNROLL + n, n)
            with sp.Fori(EARLY // UNROLL, SLICES // UNROLL - 1) as turn:
                for n in range(UNROLL):
                    i = turn * UNROLL + n
                    fetch_v_when_free(i, n)
                    sp.wait_ge(s("u_split"), i * 2 + 2)
                    fetch_u(sp, i + UNROLL, n)
            for n in range(UNROLL):
                fetch_v_when_free(SLICES - UNROLL + n, n)

        @block.scalar
        def _(act):
            def v_high(i, turn, n, parts, lag, first=False):
                act.wait_ge(s(f"v_in_{n}"), turn * 16 + 16)
                for hf in range(2):
                    if not first:
                        act.wait_ge(s("v_used"), (i - lag) * 2 + 1 + hf)
                    nc.scalar.activation(parts[:, 0, 512 * hf:512 * (hf + 1)],
                                         table_v[n][:, 512 * hf:512 * (hf + 1)], ACT.Copy)\
                        .then_inc(s("v_high"), 1)

            def pre_low(i, n, first):
                if not first:
                    act.wait_ge(s("pre_sum"), i - EARLY)
                act.wait_ge(s("u_used"), i * 2 + 2)
                nc.scalar.activation(low_buf[:, :], psum[4 + n % 2][:, SEQ:],
                                     ACT.Copy).then_inc(s("pre_low"), 1)

            def gelu(i, n):
                act.wait_ge(s("pre_sum"), i - EARLY + 1)
                nc.scalar.activation(act_buf[:, (n % 2) * SEQ:(n % 2 + 1) * SEQ],
                                     act_buf[:, (n % 2) * SEQ:(n % 2 + 1) * SEQ],
                                     ACT.Gelu_apprx_tanh).then_inc(s("gelu"), 1)

            def known_step(i, turn, n, peeled):
                v_high(i, turn, n, known_parts[n % 2], 2, peeled and i < 2)

            def step(i, turn, n, peeled):
                if not (peeled and i == SLICES - 1):
                    u_high(act, i + 1, turn if n < UNROLL - 1 else turn + 1, (n + 1) % UNROLL, u_parts, 1)
                pre_low(i, n, peeled and i == EARLY)
                gelu(i, n)
                v_high(i, turn, n, v_parts, 1)
            steps(act, 0, EARLY, known_step)
            act.wait_ge(s("v_used"), 2 * EARLY - 2)
            u_high(act, EARLY, EARLY // UNROLL, 0, u_parts, 1)
            steps(act, EARLY, SLICES - EARLY, step)

        @block.vector
        def _(dve):
            tt = nc.vector.tensor_tensor

            def v_low(i, n, parts):
                for hf in range(2):
                    dve.wait_ge(s("v_high"), i * 2 + hf + 1)
                    cut = slice(512 * hf, 512 * (hf + 1))
                    tt(parts[:, 1, cut], table_v[n][:, cut], parts[:, 0, cut].bitcast(F32),
                       ALU.subtract).then_inc(s("v_split"), 1)

            def split_weight(i, n, weight):
                nc.vector.tensor_copy(w_parts[:, n % 2, 0], weight).then_inc(s("weight_high"), 1)
                dve.wait_ge(s("weight_high"), i + 1)
                tt(w_parts[:, n % 2, 1], weight, w_parts[:, n % 2, 0].bitcast(F32), ALU.subtract)\
                    .then_inc(s("weight"), 1)

            def pre_sum(i, n):
                dve.wait_ge(s("pre_low"), i - EARLY + 1)
                tt(act_buf[:, (n % 2) * SEQ:(n % 2 + 1) * SEQ], psum[4 + n % 2][:, 0:SEQ], low_buf[:, :], ALU.add)\
                    .then_inc(s("pre_sum"), 1)

            def known_step(i, turn, n, peeled):
                if not (peeled and i < 2):
                    dve.wait_ge(s("v_used"), i * 2 - 2)
                split_weight(i, n, arena[:, bass.ds(i * SEQ, SEQ)])
                v_low(i, n, known_parts[n % 2])

            def step(i, turn, n, peeled):
                if peeled and i == SLICES - 1:
                    pre_sum(i, n)
                else:
                    u_low(dve, tt, i + 1, 0, (n + 1) % UNROLL, u_parts)
                    pre_sum(i, n)
                    u_low(dve, tt, i + 1, 1, (n + 1) % UNROLL, u_parts)
                buf = act_buf[:, (n % 2) * SEQ:(n % 2 + 1) * SEQ]
                dve.wait_ge(s("gelu"), i - EARLY + 1)
                tt(buf, buf, arena[:, bass.ds(i * SEQ, SEQ)], ALU.mult).then_inc(s("weighed"), 1)
                dve.wait_ge(s("weighed"), i - EARLY + 1)
                split_weight(i, n, buf)
                v_low(i, n, v_parts)
            steps(dve, 0, EARLY, known_step)
            u_low(dve, tt, EARLY, 0, 0, u_parts)
            u_low(dve, tt, EARLY, 1, 0, u_parts)
            steps(dve, EARLY, SLICES - EARLY, step)
            for n in range(4):
                dve.wait_ge(s("v_used"), 2 * SLICES)
                xs = x[:, n * 512:(n + 1) * 512]
                tt(xs, xs, psum[n][:, :], ALU.add).then_inc(s("x_after"), 1)
            dve.wait_ge(s("x_after"), 4)

        @block.tensor
        def _(pe):
            def pre(i, n, first):
                if not first:
                    pe.wait_ge(s("pre_sum"), i - EARLY - 1)
                bank = psum[4 + n % 2]
                for hf in range(2):
                    pe.wait_ge(s("u_split"), i * 2 + hf + 1)
                    for c in range(4 * hf, 4 * hf + 4):
                        nc.tensor.matmul(bank[:, :], u_parts[:, 0, c], h_parts[:, c].rearrange("p r t -> p (r t)"),
                                         start=(c == 0), stop=False)
                        last = nc.tensor.matmul(bank[:, 0:SEQ], u_parts[:, 1, c], h_parts[:, c, 0],
                                                start=False, stop=(c == KC - 1))
                    last.then_inc(s("u_used"), 1)

            def combine(i, n, parts, first=False, final=False):
                pe.wait_ge(s("weight"), i + 1)
                for hf in range(2):
                    pe.wait_ge(s("v_split"), i * 2 + hf + 1)
                    for tb in range(TB):
                        w = [w_parts[:, n % 2, r, tb * P:(tb + 1) * P] for r in range(2)]
                        v = [parts[:, r, 512 * hf:512 * (hf + 1)] for r in range(2)]
                        o = psum[2 * tb + hf][:, :]
                        nc.tensor.matmul(o, w[0], v[0], start=first, stop=False)
                        nc.tensor.matmul(o, w[0], v[1], start=False, stop=False)
                        last = nc.tensor.matmul(o, w[1], v[0], start=False, stop=final)
                    last.then_inc(s("v_used"), 1)

            def known_step(i, turn, n, peeled):
                combine(i, n, known_parts[n % 2], peeled and i == 0)

            def step(i, turn, n, peeled):
                pre(i, n, peeled and i < EARLY + 2)
                if not (peeled and i == EARLY):
                    combine(i - 1, (n - 1) % UNROLL, v_parts)
            steps(pe, 0, EARLY, known_step)
            steps(pe, EARLY, SLICES - EARLY, step)
            combine(SLICES - 1, UNROLL - 1, v_parts, final=True)


def final_norm(nc, a, mem, s, out):
    arena, x, stat = mem["arena"], mem["x"], mem["stat"]
    xn = arena[:, 0:2048]
    gain = arena[:, 2048:3072]
    with nc.Block() as block:
        @block.scalar
        def _(act):
            norm_act(nc, act, mem, s, "nf", xn)

        @block.vector
        def _(dve):
            norm_scale(nc, dve, mem, s, "nf", xn)
            dve.wait_ge(s("gainf_in"), 16)
            for tb in range(TB):
                xs = xn[:, tb * D:(tb + 1) * D]
                dve.wait_ge(s("nf_xn"), tb + 1)
                nc.vector.tensor_tensor(xs, xs, gain, ALU.mult).then_inc(s("y"), 1)

        @block.sync
        def _(sp):
            sp.dma_start(gain, a["final_norm_g"].partition_broadcast(P)).then_inc(s("gainf_in"), 16)
            dst = out.rearrange("(b p) d -> b p d", p=P)
            for tb in range(TB):
                sp.wait_ge(s("y"), tb + 1)
                sp.dma_start(dst[tb], xn[:, tb * D:(tb + 1) * D]).then_inc(s("y_out"), 16)
            sp.wait_ge(s("y_out"), 16 * TB)



def _layout(np, i):
    f = {k: np.asarray(v) for k, v in i.items()}
    d = {"x": f["x"].reshape(SEQ, D)}
    for k in ("l0_w_in", "l0_w_out", "l1_w_in", "l1_w_out", "l0_peer_wq", "l1_peer_wq", "l0_peer_v",
              "l1_peer_v", "a_glu_w", "final_norm_g", "c_vnorm_g"):
        d[k] = f[k]
    for k in ("l0_norm_mix_g", "l0_norm_ffn_g", "l1_norm_mix_g", "l1_norm_ffn_g"):
        d[k] = f[k].reshape(KC, P).T

    def states(m):
        return m.reshape(S5_TILES, P).T
    d["s5_params"] = np.concatenate([states(f["a_lam_re"]), states(f["a_lam_im"]),
                                     states(np.repeat(f["a_log_dt"], 64).reshape(32, 64))], 1)
    b = np.zeros((2, 8, 16, WC, 2, 64), np.float32)
    c = np.zeros((2, 2, 64, S5_TILES, 2, 16), np.float32)
    for r, (bb, cc) in enumerate(((f["a_b_re"], f["a_c_re"]), (f["a_b_im"], f["a_c_im"]))):
        for g in range(32):
            b[r, g % 8, :, g // 8, g % 2, :] = bb[g].T
            c[r, g % 2, :, g // 2, g % 2, :] = cc[g].T
    d["s5_b"] = b.reshape(2, P, 512).transpose(1, 0, 2).reshape(P, 1024)
    d["s5_c"] = c.reshape(2, P, 512).transpose(1, 0, 2).reshape(P, 1024)
    d["conv_w"] = f["b_conv_w"].reshape(3, WC, P).transpose(2, 0, 1).reshape(P, 12)
    d["d_and_glu_b"] = np.concatenate([f["a_d"].reshape(WC, P).T, f["a_glu_b"].reshape(WC, P).T], 1)
    d["c_ws"] = f["c_ws"].transpose(2, 0, 1)
    d["c_bs"] = f["c_bs"].T
    for n in ("l0", "l1"):
        keys = np.stack([f[n + "_peer_k1"], f[n + "_peer_k2"]], 1).reshape(ROWS, KEYS, P)
        d[n + "_keys"] = keys.transpose(2, 0, 1).reshape(P, ROWS * KEYS)
        u = f[n + "_peer_u"].reshape(KEYS, SLICES, KC, P)
        d[n + "_peer_u"] = u.transpose(1, 3, 2, 0).reshape(SLICES, P, KC * KEYS)
    return {k: np.ascontiguousarray(v) for k, v in d.items()}


def kernel(**inputs):
    import numpy as _np
    import concourse.bacc as _bacc
    from concourse import mybir as _mybir
    from concourse.bass_utils import run_bass_kernel_spmd as _run

    nc = _bacc.Bacc("TRN2", target_bir_lowering=False, num_devices=1)
    arrays, aps = {}, {}
    for name, v in _layout(_np, inputs).items():
        arrays[f"in_{name}"] = v
        aps[name] = nc.dram_tensor(f"in_{name}", v.shape, _mybir.dt.from_np(v.dtype), kind="ExternalInput").ap()
    out = nc.dram_tensor("out_0", (SEQ, D), F32, kind="ExternalOutput").ap()
    trunk(nc, aps, out)
    r = _run(nc, [arrays], core_ids=[0])
    return r.results[0]["out_0"].reshape(1, SEQ, D)
```
